# Optimizing a Trainium2 kernel written in Bass

```python
import jax
import jax.numpy as jnp
from jax import lax
import numpy as np

D_MODEL = 1024
BATCH = 1
SEQ = 1024
DEPTH = 1
DEC_BATCH = 8
DEC_SEQ = 8
PAST_LEN = 8192
PAGE_SIZE = 128

N_META = 16
D_MIX = D_MODEL
SSD_WIDTH = D_MIX // 2
SSD_HEAD_DIM = 64
SSD_HEADS = SSD_WIDTH // SSD_HEAD_DIM
SSD_GROUPS = 2
SSD_STATE = 128
CONV_W = 4
SSD_CHUNK = 128
CONV_DIM = SSD_WIDTH + 2 * SSD_GROUPS * SSD_STATE
SSD_IN = SSD_WIDTH + CONV_DIM + SSD_HEADS
RWKV_WIDTH = D_MIX - SSD_WIDTH
RWKV_HEAD_DIM = 64
RWKV_HEADS = RWKV_WIDTH // RWKV_HEAD_DIM
DECAY_LORA = 64
AAA_LORA = 64
GATE_LORA = 128
RWKV_IN = 3 * RWKV_WIDTH + DECAY_LORA + AAA_LORA + GATE_LORA
D_IN = SSD_IN + RWKV_IN
PEER_HEADS = 8
N_KEYS = 128
N_EXPERTS = N_KEYS * N_KEYS
PEER_TOPK = 16
D_KEY = 256
PEER_BLOCK = 128
RMS_EPS = 1e-6
GN_EPS = 64e-5
F32 = jnp.float32

kernel_name = 'hymba_ssd_rwkv7_peer_step'

def rmsnorm(x, g):
    x32 = x.astype(F32)
    y = x32 * lax.rsqrt(jnp.mean(x32 * x32, axis=-1, keepdims=True) + RMS_EPS)
    return (y * g.astype(F32)).astype(x.dtype)

def causal_conv(u, buf, w, b):
    L = u.shape[1]
    full = jnp.concatenate([buf.astype(u.dtype), u], axis=1)
    y = b + full[:, 0:L] * w[0]
    for k in range(1, CONV_W):
        y = y + full[:, k:k + L] * w[k]
    return y, full[:, L:]

def chunk_len(L):
    return SSD_CHUNK if L % SSD_CHUNK == 0 else L

def ssd_chunked(xs, dt, A, Bm, Cm, h0, chunk):
    b, L, H, P = xs.shape
    N = Bm.shape[-1]
    nc = L // chunk
    xdt = (xs * dt[..., None]).reshape(b, nc, chunk, H, P)
    Bc = Bm.reshape(b, nc, chunk, H, N)
    Cc = Cm.reshape(b, nc, chunk, H, N)
    acum = jnp.cumsum((dt * A).reshape(b, nc, chunk, H), axis=2)
    causal = jnp.tril(jnp.ones((chunk, chunk), dtype=bool))[None, None, :, :, None]
    seg = acum[:, :, :, None, :] - acum[:, :, None, :, :]
    decay_ls = jnp.exp(jnp.where(causal, seg, -jnp.inf))
    scores = jnp.einsum('bclhn,bcshn->bclsh', Cc, Bc) * decay_ls
    y_diag = jnp.einsum('bclsh,bcshp->bclhp', scores, xdt)
    to_end = jnp.exp(acum[:, :, -1:, :] - acum)
    chunk_states = jnp.einsum('bclhn,bclh,bclhp->bchpn', Bc, to_end, xdt)
    chunk_decay = jnp.exp(acum[:, :, -1, :])

    def step(h, inp):
        s_c, d_c = inp
        return h * d_c[:, :, None, None] + s_c, h

    h_last, h_prev = lax.scan(step, h0, (jnp.moveaxis(chunk_states, 1, 0), jnp.moveaxis(chunk_decay, 1, 0)))
    h_prev = jnp.moveaxis(h_prev, 0, 1)
    y_off = jnp.einsum('bclhn,bchpn,bclh->bclhp', Cc, h_prev, jnp.exp(acum))
    return (y_diag + y_off).reshape(b, L, H, P), h_last

def ssd_group(p, conv_buf, h0, segments, conv_w, conv_b, dt_bias, a_log, d_skip, ssm_norm):
    bsz, L, _ = p.shape
    z = p[..., :SSD_WIDTH]
    xbc_raw = p[..., SSD_WIDTH:SSD_WIDTH + CONV_DIM]
    dt_raw = p[..., SSD_WIDTH + CONV_DIM:SSD_IN]
    xbc, new_buf = causal_conv(xbc_raw, conv_buf, conv_w, conv_b)
    xbc = jax.nn.silu(xbc.astype(F32))
    gn = SSD_GROUPS * SSD_STATE
    xs = xbc[..., :SSD_WIDTH].reshape(bsz, L, SSD_HEADS, SSD_HEAD_DIM)
    rep = SSD_HEADS // SSD_GROUPS
    Bm = jnp.repeat(xbc[..., SSD_WIDTH:SSD_WIDTH + gn].reshape(bsz, L, SSD_GROUPS, SSD_STATE), rep, axis=2)
    Cm = jnp.repeat(xbc[..., SSD_WIDTH + gn:].reshape(bsz, L, SSD_GROUPS, SSD_STATE), rep, axis=2)
    dt = jax.nn.softplus(dt_raw.astype(F32) + dt_bias.astype(F32))
    A = -jnp.exp(a_log.astype(F32))
    h = h0.astype(F32)
    ys = []
    start = 0
    for seg in segments:
        y_seg, h = ssd_chunked(xs[:, start:start + seg], dt[:, start:start + seg], A,
                               Bm[:, start:start + seg], Cm[:, start:start + seg], h, chunk_len(seg))
        ys.append(y_seg)
        start += seg
    y = jnp.concatenate(ys, axis=1)
    y = (y + d_skip.astype(F32)[:, None] * xs).reshape(bsz, L, SSD_WIDTH)
    y = rmsnorm(y * jax.nn.silu(z.astype(F32)), ssm_norm)
    return y, new_buf, h

def rwkv_group(p, shift_buf, s0, shift_mu, decay_w0, decay_w2, iclr_a0, iclr_a2, gate_g2, k_k, k_a, r_k, lnx_w, lnx_b):
    bsz, L, _ = p.shape
    prev = jnp.concatenate([shift_buf[:, None].astype(p.dtype), p[:, :-1]], axis=1)
    pm = p + (prev - p) * shift_mu
    new_shift = p[:, -1]
    rw = RWKV_WIDTH
    r, k, v, wl, al, gl = jnp.split(pm, [rw, 2 * rw, 3 * rw, 3 * rw + DECAY_LORA, 3 * rw + DECAY_LORA + AAA_LORA], axis=-1)
    w = -jax.nn.softplus(-(decay_w0.astype(F32) + (jnp.tanh(wl) @ decay_w2).astype(F32))) - 0.5
    a = jax.nn.sigmoid(iclr_a0.astype(F32) + (al @ iclr_a2).astype(F32))
    g = (jax.nn.sigmoid(gl) @ gate_g2).astype(F32)

    def heads(t):
        return t.astype(F32).reshape(bsz, L, RWKV_HEADS, RWKV_HEAD_DIM)

    r, k, v, w, a = heads(r), heads(k), heads(v), heads(w), heads(a)
    kk = k * k_k.astype(F32).reshape(RWKV_HEADS, RWKV_HEAD_DIM)
    kk = kk / jnp.maximum(jnp.sqrt(jnp.sum(kk * kk, axis=-1, keepdims=True)), 1e-12)
    k = k * (1.0 + (a - 1.0) * k_a.astype(F32).reshape(RWKV_HEADS, RWKV_HEAD_DIM))
    decay = jnp.exp(-jnp.exp(w))

    def step(S, inp):
        r_t, d_t, k_t, v_t, kk_t, a_t = inp
        sa = jnp.einsum('bhvk,bhk->bhv', S, kk_t)
        S = S * d_t[:, :, None, :] - sa[..., None] * (kk_t * a_t)[:, :, None, :] + v_t[..., None] * k_t[:, :, None, :]
        return S, jnp.einsum('bhvk,bhk->bhv', S, r_t)

    tm = lambda t: jnp.moveaxis(t, 1, 0)
    S, y = lax.scan(step, s0.astype(F32), (tm(r), tm(decay), tm(k), tm(v), tm(kk), tm(a)))
    y = jnp.moveaxis(y, 0, 1)
    mu = jnp.mean(y, axis=-1, keepdims=True)
    var = jnp.mean(jnp.square(y - mu), axis=-1, keepdims=True)
    yn = ((y - mu) * lax.rsqrt(var + GN_EPS)).reshape(bsz, L, rw) * lnx_w.astype(F32) + lnx_b.astype(F32)
    bonus = (jnp.sum(r * k * r_k.astype(F32), axis=-1, keepdims=True) * v).reshape(bsz, L, rw)
    return (yn + bonus) * g, new_shift, S

def mixer_sublayer(h, conv_buf, ssd_h, shift_buf, wkv_s, segments, mp):
    (norm_mix, w_in, conv_w, conv_b, dt_bias, a_log, d_skip, ssm_norm, shift_mu, decay_w0, decay_w2,
     iclr_a0, iclr_a2, gate_g2, k_k, k_a, r_k, lnx_w, lnx_b, w_out) = mp
    u = rmsnorm(h, norm_mix)
    p = u @ w_in
    y_a, conv_new, ssd_new = ssd_group(p[..., :SSD_IN], conv_buf, ssd_h, segments, conv_w, conv_b, dt_bias, a_log, d_skip, ssm_norm)
    y_b, shift_new, wkv_new = rwkv_group(p[..., SSD_IN:], shift_buf, wkv_s, shift_mu, decay_w0, decay_w2,
                                         iclr_a0, iclr_a2, gate_g2, k_k, k_a, r_k, lnx_w, lnx_b)
    y = jnp.concatenate([y_a.astype(h.dtype), y_b.astype(h.dtype)], axis=-1) @ w_out
    return h + y, conv_new, ssd_new, shift_new, wkv_new

def peer(u, w_query, sub_keys, expert_u, expert_v):
    lead = u.shape[:-1]
    t = u.reshape(-1, D_MODEL)
    n = t.shape[0]
    nb = -(-n // PEER_BLOCK)
    t = jnp.pad(t, ((0, nb * PEER_BLOCK - n), (0, 0))).reshape(nb, PEER_BLOCK, D_MODEL)
    half = D_KEY // 2

    def block(tb):
        q = (tb @ w_query).astype(F32).reshape(PEER_BLOCK, PEER_HEADS, 2, half)
        s1 = jnp.einsum('thd,hkd->thk', q[:, :, 0], sub_keys[0].astype(F32))
        s2 = jnp.einsum('thd,hkd->thk', q[:, :, 1], sub_keys[1].astype(F32))
        v1, i1 = lax.top_k(s1, PEER_TOPK)
        v2, i2 = lax.top_k(s2, PEER_TOPK)
        cand = (v1[..., :, None] + v2[..., None, :]).reshape(PEER_BLOCK, PEER_HEADS, PEER_TOPK * PEER_TOPK)
        top_s, pos = lax.top_k(cand, PEER_TOPK)
        e1 = jnp.take_along_axis(i1, pos // PEER_TOPK, axis=-1)
        e2 = jnp.take_along_axis(i2, pos % PEER_TOPK, axis=-1)
        experts = e1 * N_KEYS + e2
        gate = jax.nn.softmax(top_s, axis=-1)
        ue = expert_u[experts]
        act = jax.nn.gelu(jnp.einsum('thkd,td->thk', ue, tb).astype(F32), approximate=False) * gate
        return jnp.einsum('thk,thkd->td', act.astype(tb.dtype), expert_v[experts])

    out = lax.map(block, t).reshape(-1, D_MODEL)[:n]
    return out.reshape(*lead, D_MODEL)

def setup_inputs(seed: int = 0) -> dict:
    key = jax.random.key(seed)
    ks = jax.random.split(key, 40)

    def nrm(k, shape, scale):
        return jax.random.normal(k, shape, F32) * scale

    dt0 = jnp.exp(jax.random.uniform(ks[9], (DEPTH, SSD_HEADS), F32, np.log(1e-3), np.log(1e-1)))
    return {
        'x_prompt': nrm(ks[0], (BATCH, SEQ, D_MODEL), 1.0),
        'x_sample': nrm(ks[1], (DEC_BATCH, DEC_SEQ, D_MODEL), 1.0),
        'state_conv': nrm(ks[2], (DEPTH, DEC_BATCH, CONV_W - 1, CONV_DIM), 1.0),
        'state_ssd': nrm(ks[3], (DEPTH, DEC_BATCH, SSD_HEADS, SSD_HEAD_DIM, SSD_STATE), 0.1),
        'state_shift': nrm(ks[4], (DEPTH, DEC_BATCH, RWKV_IN), 1.0),
        'state_wkv': nrm(ks[5], (DEPTH, DEC_BATCH, RWKV_HEADS, RWKV_HEAD_DIM, RWKV_HEAD_DIM), 0.1),
        'meta_tokens': nrm(ks[6], (N_META, D_MODEL), 1.0),
        'norm_mix': 1.0 + nrm(ks[7], (DEPTH, D_MODEL), 0.02),
        'w_in': nrm(ks[8], (DEPTH, D_MODEL, D_IN), D_MODEL ** -0.5),
        'conv_w': nrm(ks[10], (DEPTH, CONV_W, CONV_DIM), 0.5),
        'conv_b': nrm(ks[11], (DEPTH, CONV_DIM), 0.02),
        'dt_bias': dt0 + jnp.log(-jnp.expm1(-dt0)),
        'a_log': jnp.log(jax.random.uniform(ks[12], (DEPTH, SSD_HEADS), F32, 1.0, 16.0)),
        'd_skip': 1.0 + nrm(ks[13], (DEPTH, SSD_HEADS), 0.1),
        'ssm_norm': 1.0 + nrm(ks[14], (DEPTH, SSD_WIDTH), 0.02),
        'shift_mu': jax.random.uniform(ks[15], (DEPTH, RWKV_IN), F32, 0.0, 1.0),
        'decay_w0': jax.random.uniform(ks[16], (DEPTH, RWKV_WIDTH), F32, -6.0, 1.0),
        'decay_w2': nrm(ks[17], (DEPTH, DECAY_LORA, RWKV_WIDTH), 0.5 * DECAY_LORA ** -0.5),
        'iclr_a0': nrm(ks[18], (DEPTH, RWKV_WIDTH), 0.1),
        'iclr_a2': nrm(ks[19], (DEPTH, AAA_LORA, RWKV_WIDTH), AAA_LORA ** -0.5),
        'gate_g2': nrm(ks[20], (DEPTH, GATE_LORA, RWKV_WIDTH), GATE_LORA ** -0.5),
        'k_k': 0.85 + nrm(ks[21], (DEPTH, RWKV_WIDTH), 0.05),
        'k_a': 1.0 + nrm(ks[22], (DEPTH, RWKV_WIDTH), 0.05),
        'r_k': nrm(ks[23], (DEPTH, RWKV_HEADS, RWKV_HEAD_DIM), 0.1),
        'lnx_w': 1.0 + nrm(ks[24], (DEPTH, RWKV_WIDTH), 0.02),
        'lnx_b': nrm(ks[25], (DEPTH, RWKV_WIDTH), 0.02),
        'w_out': nrm(ks[26], (DEPTH, D_MIX, D_MODEL), D_MIX ** -0.5),
        'norm_ffn': 1.0 + nrm(ks[27], (DEPTH, D_MODEL), 0.02),
        'w_query': nrm(ks[28], (DEPTH, D_MODEL, PEER_HEADS * D_KEY), D_MODEL ** -0.5),
        'sub_keys': nrm(ks[29], (DEPTH, 2, PEER_HEADS, N_KEYS, D_KEY // 2), (D_KEY // 2) ** -0.5),
        'expert_u': nrm(ks[30], (DEPTH, N_EXPERTS, D_MODEL), D_MODEL ** -0.5),
        'expert_v': nrm(ks[31], (DEPTH, N_EXPERTS, D_MODEL), 0.5),
        'norm_final': 1.0 + nrm(ks[32], (D_MODEL,), 0.02),
    }

def reference(x_prompt, x_sample, state_conv, state_ssd, state_shift, state_wkv, meta_tokens, norm_mix, w_in,
              conv_w, conv_b, dt_bias, a_log, d_skip, ssm_norm, shift_mu, decay_w0, decay_w2, iclr_a0, iclr_a2,
              gate_g2, k_k, k_a, r_k, lnx_w, lnx_b, w_out, norm_ffn, w_query, sub_keys, expert_u, expert_v,
              norm_final):
    bp, seq_p, _ = x_prompt.shape
    seq_s = x_sample.shape[1]
    h_p = jnp.concatenate([jnp.broadcast_to(meta_tokens[None].astype(x_prompt.dtype), (bp, N_META, D_MODEL)), x_prompt], axis=1)
    h_s = x_sample
    zc = jnp.zeros((bp, CONV_W - 1, CONV_DIM), x_prompt.dtype)
    zs = jnp.zeros((bp, SSD_HEADS, SSD_HEAD_DIM, SSD_STATE), F32)
    zsh = jnp.zeros((bp, RWKV_IN), x_prompt.dtype)
    zw = jnp.zeros((bp, RWKV_HEADS, RWKV_HEAD_DIM, RWKV_HEAD_DIM), F32)
    cp, sp, shp, wp, cs, ss, shs, ws = [], [], [], [], [], [], [], []
    for i in range(DEPTH):
        mp = (norm_mix[i], w_in[i], conv_w[i], conv_b[i], dt_bias[i], a_log[i], d_skip[i], ssm_norm[i], shift_mu[i],
              decay_w0[i], decay_w2[i], iclr_a0[i], iclr_a2[i], gate_g2[i], k_k[i], k_a[i], r_k[i], lnx_w[i], lnx_b[i], w_out[i])
        h_p, c1, s1, sh1, w1 = mixer_sublayer(h_p, zc, zs, zsh, zw, (N_META, seq_p), mp)
        h_s, c2, s2, sh2, w2 = mixer_sublayer(h_s, state_conv[i], state_ssd[i], state_shift[i], state_wkv[i], (seq_s,), mp)
        cp.append(c1); sp.append(s1); shp.append(sh1); wp.append(w1)
        cs.append(c2); ss.append(s2); shs.append(sh2); ws.append(w2)
        if i == DEPTH - 1:
            h_p = h_p[:, N_META:]
        h_p = h_p + peer(rmsnorm(h_p, norm_ffn[i]), w_query[i], sub_keys[i], expert_u[i], expert_v[i])
        h_s = h_s + peer(rmsnorm(h_s, norm_ffn[i]), w_query[i], sub_keys[i], expert_u[i], expert_v[i])
    y_prompt = rmsnorm(h_p, norm_final)
    y_sample = rmsnorm(h_s, norm_final)
    new_conv_prompt = jnp.stack(cp).astype(state_conv.dtype)
    new_ssd_prompt = jnp.stack(sp).astype(state_ssd.dtype)
    new_shift_prompt = jnp.stack(shp).astype(state_shift.dtype)
    new_wkv_prompt = jnp.stack(wp).astype(state_wkv.dtype)
    new_conv_sample = jnp.stack(cs).astype(state_conv.dtype)
    new_ssd_sample = jnp.stack(ss).astype(state_ssd.dtype)
    new_shift_sample = jnp.stack(shs).astype(state_shift.dtype)
    new_wkv_sample = jnp.stack(ws).astype(state_wkv.dtype)
    return (y_prompt, y_sample, new_conv_prompt, new_ssd_prompt, new_shift_prompt, new_wkv_prompt,
            new_conv_sample, new_ssd_sample, new_shift_sample, new_wkv_sample)


_drawn_inputs = setup_inputs


def setup_inputs(seed=0):
    import zlib

    import numpy as np

    out = dict(_drawn_inputs(seed))
    spreads = {}
    factors = {}
    for name, (base, spread) in spreads.items():
        noise = np.random.default_rng([zlib.crc32(name.encode()), seed]).standard_normal(out[name].shape)
        drawn = base * np.exp(spread * noise) if base else spread * noise
        out[name] = jnp.asarray(drawn.astype(out[name].dtype))
    for name, factor in factors.items():
        out[name] = (out[name] * factor).astype(out[name].dtype)
    return out
```

```python
from contextlib import ExitStack

import numpy as np

import concourse.bass as bass
from concourse import mybir

F32 = mybir.dt.float32
U32 = mybir.dt.uint32
ALU = mybir.AluOpType
ACT = mybir.ActivationFunctionType
AX_X = mybir.AxisListType.X

P = 128
D = 1024
KD = D // P
SEQS, STEPS = 8, 8
NS = SEQS * STEPS
META = 16
PROMPT = 1024
T = P + PROMPT
NT = T // P
KEPT = NS + PROMPT
HIST = 3
CONV_TILES, SHIFT_TILES, GATE_TILES = 8, 14, 4
IN_TILES = CONV_TILES + SHIFT_TILES + GATE_TILES + 1
CH = T // 3
E_SAMPLE = SEQS * (HIST + STEPS)
E_COLS = E_SAMPLE + HIST + T - NS
WCOLS = KD * P
RMS_EPS = 1e-6
GN_EPS = 64e-5
HEADS = 8
HD = 64
STATE = 128
BANK = 512


class Stage:

    def __init__(self, nc, name):
        self.nc, self.name, self.ctx, self.sems = nc, name, ExitStack(), []

    def __enter__(self):
        self.ctx.__enter__()
        return self

    def __exit__(self, *failure):
        self.ctx.__exit__(*failure)
        if failure[0] is None:
            self.nc.clear_and_free_semaphores(self.sems)
            self.nc.all_engine_barrier()

    def sb(self, name, shape, dt=F32):
        return self.ctx.enter_context(self.nc.sbuf_tensor(f"{self.name}_{name}", shape, dt))

    def psum(self, name, *shape):
        n = int(np.prod(shape))
        banks = self.ctx.enter_context(self.nc.psum_tensor(f"{self.name}_{name}", [P, -(-n // BANK) * BANK], F32))
        used = banks[:, 0:n]
        return used if len(shape) == 1 else used.rearrange("p (a b) -> p a b", a=shape[0])

    def sem(self, name):
        self.sems.append(self.nc.alloc_semaphore(f"{self.name}_{name}"))
        return self.sems[-1]


def sample_cols(buf):
    return buf[:, 0:NS].rearrange("p (b w) -> p b w", b=SEQS)


def at(dram, m):
    return dram[m] if isinstance(m, int) else dram[bass.ds(m, 1)].rearrange("a p c -> (a p) c")


def input_projection(nc, x_t, norm_g_d, w_pack, hist_d, cols_d, new_conv_s, new_conv_p, new_shift_s, new_shift_p):
    with Stage(nc, "inp") as st:
        sb, sem = st.sb, st.sem
        u = sb("u", [P, KD, T])
        squares = sb("squares", [P, 2, T])
        inv_rms = sb("inv_rms", [P, T])
        ones = sb("in_ones", [P, P])
        norm_g = sb("norm_mix_g", [P, KD])
        w = [sb(f"w_in_{s}", [P, WCOLS + 8]) for s in range(2)]
        raw = [sb(f"raw_{s}", [P, E_COLS]) for s in range(2)]
        mid = [sb(f"mid_{s}", [P, T]) for s in range(2)]
        done = [sb(f"done_{s}", [P, T]) for s in range(2)]
        proj = [st.psum(f"proj_{s}", 3, BANK) for s in range(2)]

        x_loaded = [sem(f"x_loaded_{k}") for k in range(KD)]
        g_loaded = sem("norm_g_loaded")
        w_loaded = [sem(f"w_in_loaded_{s}") for s in range(2)]
        hist_loaded = [sem(f"hist_loaded_{s}") for s in range(2)]
        consts_ready = sem("in_consts_ready")
        square_ready = sem("square_ready")
        sum_done = sem("sum_done")
        rms_step = sem("rms_step")
        u_ready = sem("u_ready")
        proj_ready = sem("proj_ready")
        raw_ready = sem("raw_ready")
        vec_step = sem("in_vec_step")
        act_out = sem("in_act_out")
        stored = [sem(f"in_stored_{s}") for s in range(2)]
        edge_stored = [sem(f"edge_stored_{s}") for s in range(2)]

        def tap_sample(s, j):
            return raw[s][:, 0:E_SAMPLE].rearrange("p (b w) -> p b w", b=SEQS)[:, :, j:j + STEPS]

        def tap_rest(s, j):
            return raw[s][:, E_SAMPLE + j:E_SAMPLE + j + T - NS]

        CONV_OPS, SHIFT_OPS = 8, 4

        def vec_before(m, kind):
            return m * CONV_OPS if kind == "conv" else m * SHIFT_OPS + CONV_TILES * (CONV_OPS - SHIFT_OPS)

        def over_tiles(eng, body):
            body(0, 0, 0, "conv")
            body(0, 1, 1, "conv")
            lo = 1
            for kind, tiles in (("conv", CONV_TILES - 2), ("shift", SHIFT_TILES), ("gate", GATE_TILES)):
                with eng.Fori(lo, lo + tiles // 2) as q:
                    for s in range(2):
                        body(q, s, q * 2 + s, kind)
                lo += tiles // 2
            body(lo, 0, 2 * lo, "dt")

        with nc.Block() as block:
            @block.sync
            def _(sp):
                sp.dma_start(norm_g[:], norm_g_d).then_inc(g_loaded, 16)
                for k in range(KD):
                    sp.dma_start(u[:, k, :], x_t[k]).then_inc(x_loaded[k], 16)

                def load(q, s, m, kind):
                    first = isinstance(m, int) and m < 2
                    if not first:
                        sp.wait_ge(stored[s], q * 16)
                    sp.dma_start(w[s][:], at(w_pack, m)).then_inc(w_loaded[s], 16)
                    if kind in ("conv", "shift"):
                        if not first:
                            sp.wait_ge(edge_stored[s], q * 32)
                        dst = raw[s][:, 0:E_SAMPLE].rearrange("p (b w) -> p b w", b=SEQS)[:, :, 0:HIST]
                        src = hist_d[m] if isinstance(m, int) else hist_d[bass.ds(m, 1)].rearrange("a p b w -> (a p) b w")
                        sp.dma_start(dst, src).then_inc(hist_loaded[s], 16)

                over_tiles(sp, load)

            @block.gpsimd
            def _(pool):
                for s in range(2):
                    pool.memset(raw[s][:, E_SAMPLE:E_SAMPLE + HIST], 0.0).then_inc(consts_ready, 1)
                pool.memset(ones[:], 1.0).then_inc(consts_ready, 1)

                def store(q, s, m, kind):
                    if kind in ("conv", "shift"):
                        pool.wait_ge(raw_ready, m + 1)
                        out_s, out_p = (new_conv_s, new_conv_p) if kind == "conv" else (new_shift_s, new_shift_p)
                        i = m if kind == "conv" else m - CONV_TILES
                        src = raw[s][:, 0:E_SAMPLE].rearrange("p (b w) -> p b w", b=SEQS)[:, :, STEPS:STEPS + HIST]
                        dst = out_s[i] if isinstance(i, int) else out_s[bass.ds(i, 1)].rearrange("a p b w -> (a p) b w")
                        pool.dma_start(dst, src).then_inc(edge_stored[s], 16)
                        pool.dma_start(at(out_p, i), raw[s][:, E_COLS - HIST:E_COLS]).then_inc(edge_stored[s], 16)
                    if kind == "shift":
                        pool.wait_ge(vec_step, vec_before(m + 1, kind))
                    else:
                        pool.wait_ge(act_out, m + 1 if kind == "conv" else m + 1 - SHIFT_TILES)
                    pool.dma_start(at(cols_d, m), done[s][:]).then_inc(stored[s], 16)

                over_tiles(pool, store)
                for s in range(2):
                    pool.wait_ge(edge_stored[s], 16 * (CONV_TILES + SHIFT_TILES))
                    pool.wait_ge(stored[s], 16 * ((IN_TILES + 1 - s) // 2))

            @block.scalar
            def _(act):
                for k in range(KD):
                    act.wait_ge(x_loaded[k], 16)
                    if k >= 2:
                        act.wait_ge(sum_done, k - 1)
                    act.activation(squares[:, k % 2, :], u[:, k, :], ACT.Square).then_inc(square_ready, 1)
                act.wait_ge(rms_step, 3)
                act.activation(inv_rms[:], inv_rms[:], ACT.Sqrt).then_inc(rms_step, 1)

                def evacuate(q, s, m, kind):
                    first = isinstance(m, int) and m < 2
                    if not first:
                        act.wait_ge(stored[s], q * 16)
                    if kind in ("conv", "shift"):
                        act.wait_ge(hist_loaded[s], q * 16 + 16)
                        if first:
                            act.wait_ge(consts_ready, 2)
                        for c in range(3):
                            act.wait_ge(proj_ready, m * 3 + c + 1)
                            lo = NS if c == 0 else 0
                            if c == 0:
                                act.activation(tap_sample(s, HIST), sample_cols(proj[s][:, 0, :]), ACT.Copy)
                            at0 = E_SAMPLE + HIST - NS + c * CH
                            out = act.activation(raw[s][:, at0 + lo:at0 + CH], proj[s][:, c, lo:CH], ACT.Copy)
                        out.then_inc(raw_ready, 1)
                    if kind == "conv":
                        act.wait_ge(vec_step, vec_before(m + 1, kind))
                        act.activation(done[s][:], mid[s][:], ACT.Silu).then_inc(act_out, 1)
                    if kind in ("gate", "dt"):
                        for c in range(3):
                            act.wait_ge(proj_ready, m * 3 + c + 1)
                            out = act.activation(done[s][:, c * CH:c * CH + CH], proj[s][:, c, 0:CH],
                                                 ACT.Silu if kind == "gate" else ACT.Copy)
                        out.then_inc(act_out, 1)

                over_tiles(act, evacuate)

            @block.vector
            def _(dve):
                dve.wait_ge(sum_done, KD)
                for c in range(3):
                    dve.tensor_scalar(inv_rms[:, c * CH:c * CH + CH], proj[0][:, c, 0:CH], 1.0 / D, RMS_EPS,
                                      ALU.mult, ALU.add).then_inc(rms_step, 1)
                dve.wait_ge(rms_step, 4)
                dve.reciprocal(inv_rms[:], inv_rms[:]).then_inc(rms_step, 1)
                dve.wait_ge(rms_step, 5)
                dve.wait_ge(g_loaded, 16)
                for k in range(KD):
                    dve.scalar_tensor_tensor(out=u[:, k, :], in0=u[:, k, :], scalar=norm_g[:, k:k + 1],
                                             in1=inv_rms[:], op0=ALU.mult, op1=ALU.mult).then_inc(u_ready, 1)

                def column_work(q, s, m, kind):
                    if kind not in ("conv", "shift"):
                        return
                    coef = w[s][:, WCOLS:WCOLS + 8]
                    before = vec_before(m, kind)
                    dve.wait_ge(raw_ready, m + 1)
                    if kind == "conv":
                        for j in range(HIST + 1):
                            for r, (src, dst) in enumerate(((tap_sample(s, j), sample_cols(mid[s])),
                                                            (tap_rest(s, j), mid[s][:, NS:T]))):
                                if j == 0:
                                    if r == 0 and not (isinstance(m, int) and m < 2):
                                        dve.wait_ge(act_out, m - 1)
                                    dve.tensor_scalar(dst, src, coef[:, 0:1], coef[:, 4:5], ALU.mult,
                                                      ALU.add).then_inc(vec_step, 1)
                                else:
                                    dve.wait_ge(vec_step, before + (2 * j - 1 + r))
                                    dve.scalar_tensor_tensor(out=dst, in0=src, scalar=coef[:, j:j + 1], in1=dst,
                                                             op0=ALU.mult, op1=ALU.add).then_inc(vec_step, 1)
                    else:
                        sides = ((tap_sample(s, HIST), tap_sample(s, HIST - 1), sample_cols(mid[s]), sample_cols(done[s])),
                                 (tap_rest(s, HIST), tap_rest(s, HIST - 1), mid[s][:, NS:T], done[s][:, NS:T]))
                        dve.wait_ge(act_out, CONV_TILES)
                        dve.wait_ge(stored[s], q * 16)
                        for now, prev, diff, _ in sides:
                            dve.tensor_tensor(diff, prev, now, ALU.subtract).then_inc(vec_step, 1)
                        for r, (now, _, diff, out) in enumerate(sides):
                            dve.wait_ge(vec_step, before + (1 + r))
                            dve.scalar_tensor_tensor(out=out, in0=diff, scalar=coef[:, 0:1], in1=now,
                                                     op0=ALU.mult, op1=ALU.add).then_inc(vec_step, 1)

                over_tiles(dve, column_work)

            @block.tensor
            def _(pe):
                pe.wait_ge(consts_ready, 3)
                for k in range(KD):
                    pe.wait_ge(square_ready, k + 1)
                    for c in range(3):
                        mm = pe.matmul(proj[0][:, c, 0:CH], ones[:], squares[:, k % 2, c * CH:c * CH + CH],
                                       start=(k == 0), stop=(k == KD - 1))
                    mm.then_inc(sum_done, 1)
                pe.wait_ge(rms_step, 3)

                def project(q, s, m, kind):
                    pe.wait_ge(w_loaded[s], q * 16 + 16)
                    if not (isinstance(m, int) and m < 2):
                        if kind in ("conv", "shift"):
                            pe.wait_ge(raw_ready, m - 1)
                        else:
                            pe.wait_ge(raw_ready, CONV_TILES + SHIFT_TILES)
                            if kind == "gate":
                                pe.wait_ge(act_out, m - (SHIFT_TILES + 1))
                            else:
                                pe.wait_ge(act_out, m - SHIFT_TILES - 1)
                    for c in range(3):
                        for k in range(KD):
                            if isinstance(m, int) and m == 0 and c == 0:
                                pe.wait_ge(u_ready, k + 1)
                            mm = pe.matmul(proj[s][:, c, 0:CH], w[s][:, k * P:k * P + P],
                                           u[:, k, c * CH:c * CH + CH], start=(k == 0), stop=(k == KD - 1))
                        mm.then_inc(proj_ready, 1)

                over_tiles(pe, project)


LEVELS = 7


def constants():
    r = np.arange(P)
    blocks = [np.where(r < NS, r // STEPS, SEQS), np.zeros(P, int)]
    same = [b[:, None] == b[None, :] for b in blocks]
    s, t = r[:, None], r[None, :]
    causal = np.stack([(s <= t) & m for m in same]).astype(np.float32)
    before = np.stack([(s < t) & m for m in same]).astype(np.float32)
    last = np.stack([m & ~np.roll(m, -1, 0) & (s >= t) if b.any() else m & (s == P - 1)
                     for m, b in zip(same, blocks)])
    last[0] = same[0] & np.isin(s, list(range(STEPS - 1, NS, STEPS)) + [P - 1])
    level = np.stack([np.stack([(s < t) & m & (s >> (l + 1) == t >> (l + 1)) & (s >> l != t >> l)
                                for l in range(LEVELS)]) for m in same]).astype(np.float32)
    keep = np.ones((P, T), np.float32)
    keep[:, [STEPS * b for b in range(SEQS)] + [P * c for c in range(NT)] + [NS]] = 0.0
    head_row = (r[:HEADS, None, None] == r[None, :HEADS, None]) * np.ones((1, 1, P))
    return {
        "eye": np.eye(P, dtype=np.float32),
        "causal": causal, "before": before, "last_row": last.astype(np.float32), "level": level, "keep": keep,
        "block_row": (blocks[0][:, None] == np.arange(SEQS + 1)[None, :]).astype(np.float32),
        "head_row": head_row.astype(np.float32),
        "head_pair": (s // HD == t // HD).astype(np.float32),
        "level0_t": level[1, 0].T.copy(),
        "iota": np.broadcast_to(r.astype(np.float32), (P, P)).copy(),
    }


def tile_cols(c):
    return slice(c * P, c * P + P) if isinstance(c, int) else bass.ds(c * P, P)


def over_chunks(eng, body):
    body(0, 0, 0)
    with eng.Fori(0, (NT - 1) // 2) as q:
        body(q, 1, q * 2 + 1)
        body(q + 1, 0, q * 2 + 2)


SSD_W = HEADS * HD
GROUPS = 2
PER_GROUP = HEADS // GROUPS


def ssd_heads(nc, cols_d, dt_par_d, ssd_par_d, state_d, eye_d, causal_d, last_row_d, keep_d, block_row_d, head_row_d,
              y_d, new_state_s, new_state_p):
    with Stage(nc, "ssd") as st:
        sb, psum, sem = st.sb, st.psum, st.sem
        eye, ones = sb("eye", [P, P]), sb("ones", [P, P])
        causal = sb("causal", [P, 2, P])
        last_row = sb("last_row", [P, 2, P])
        keep = sb("keep", [HEADS, T])
        block_row = sb("block_row", [P, SEQS + 1])
        head_row = sb("head_row", [HEADS, HEADS, P])
        dt_par = sb("dt_par", [HEADS, 2])
        ssd_par = sb("ssd_par", [P, 2, 4])
        dt = sb("dt", [HEADS, T])
        dt_abs = sb("dt_abs", [HEADS, T])
        log_decay = sb("log_decay", [HEADS, T])
        cum = sb("cum", [HEADS, T])
        xbc = [sb(f"xbc_{s}", [P, CONV_TILES, P]) for s in range(2)]
        gate = [sb(f"gate_{s}", [P, GATE_TILES, P]) for s in range(2)]
        dt_cum = sb("dt_cum", [HEADS, 2, P])
        by_row = sb("by_row", [P, 2, HEADS])
        to_end = sb("to_end", [P, HEADS])
        b_rows = sb("b_rows", [P, GROUPS, STATE])
        decay = sb("decay", [P, HEADS, P])
        from_start = sb("from_start", [P, HEADS, P])
        x_dt = sb("x_dt", [P, HEADS, HD])
        x_end = sb("x_end", [P, HEADS, HD])
        x_block = sb("x_block", [P, SEQS + 1, SSD_W])
        scores = sb("scores", [P, GROUPS, P])
        weights = sb("weights", [P, HEADS, P])
        c_start = sb("c_start", [P, HEADS, P])
        h_seq = sb("h_seq", [P, SEQS, SSD_W])
        h_next = sb("h_next", [P, 2, SSD_W])
        h = sb("h", [P, SSD_W])
        h_kept = sb("h_kept", [P, SSD_W])
        y = sb("y", [P, GATE_TILES, P])
        y_sq = sb("y_sq", [P, GATE_TILES, P])
        y_rms = sb("y_rms", [P, P])
        y_out = sb("y_out", [P, GATE_TILES, P])
        x_ps = psum("x_ps", HEADS, HD)
        b_ps = psum("b_ps", GROUPS, STATE)
        small_ps = psum("small_ps", 3, HEADS)
        rows_ps = psum("rows_ps", HEADS, P)
        scores_ps = psum("scores_ps", GROUPS, P)
        y_ps = psum("y_ps", GATE_TILES, P)
        h_ps = psum("h_ps", SSD_W)

        consts_loaded, par_loaded, dt_loaded = sem("ssd_consts_loaded"), sem("ssd_par_loaded"), sem("dt_loaded")
        seq_loaded = sem("h_seq_loaded")
        loaded = [sem(f"xbc_loaded_{s}") for s in range(2)]
        ones_ready = sem("ssd_ones_ready")
        dt_step, dt_act = sem("dt_step"), sem("dt_act")
        fix_ready, small_done, by_row_ready, end_done = sem("fix_ready"), sem("small_done"), sem("by_row_ready"), sem("end_done")
        x_done, b_done, b_ready, rows_done = sem("x_rows_done"), sem("b_rows_done"), sem("b_rows_ready"), sem("rows_done")
        scores_done, start_ready, end_diff, end_ready = sem("scores_done"), sem("from_start_ready"), sem("end_diff"), sem("to_end_ready")
        seg_ready, decay_ready, xdt_ready, xend_ready = sem("seg_ready"), sem("decay_ready"), sem("x_dt_ready"), sem("x_end_ready")
        masked, c_ready, w_ready = sem("scores_masked"), sem("c_start_ready"), sem("weights_ready")
        y_done, h_done, h_step, h_ready = sem("y_done"), sem("h_done"), sem("h_step"), sem("h_ready")
        skip_done, gated, squared, var_done = sem("skip_done"), sem("gated"), sem("squared"), sem("var_done")
        mean_ready, root_ready, inv_ready, y_ready = sem("mean_ready"), sem("root_ready"), sem("inv_ready"), sem("ssd_y_ready")
        y_stored, h_stored = sem("ssd_y_stored"), [sem(f"h_stored_{s}") for s in range(2)]
        block_ready, seq_done, seq_step, seq_ready = sem("x_block_ready"), sem("seq_done"), sem("seq_step"), sem("seq_ready")
        var_ps = b_ps[:, 0, :]
        CONSTS = 6

        def of_head(buf, hh):
            return buf[:, hh * HD:hh * HD + HD]

        def y_rows(hh):
            lo = hh % 2 * HD
            return y_ps[lo:lo + HD, hh // 2, :]

        with nc.Block() as block:
            @block.sync
            def _(sp):
                sp.dma_start(dt[:], cols_d[IN_TILES - 1, 0:HEADS, :]).then_inc(dt_loaded, 16)
                sp.dma_start(dt_par[:], dt_par_d).then_inc(par_loaded, 16)
                sp.dma_start(keep[:], keep_d[0:HEADS, :]).then_inc(par_loaded, 16)
                sp.dma_start(eye[:], eye_d).then_inc(consts_loaded, 16)
                sp.dma_start(causal[:], causal_d.rearrange("a s t -> s a t")).then_inc(consts_loaded, 16)
                sp.dma_start(last_row[:], last_row_d.rearrange("a s t -> s a t")).then_inc(consts_loaded, 16)
                sp.dma_start(block_row[:], block_row_d).then_inc(consts_loaded, 16)
                sp.dma_start(head_row[:], head_row_d).then_inc(consts_loaded, 16)
                sp.dma_start(ssd_par[:], ssd_par_d).then_inc(consts_loaded, 16)

                def load(k, s, c):
                    if not (isinstance(c, int) and c == 0):
                        sp.wait_ge(y_ready, c - 1)
                    sp.dma_start(xbc[s][:], cols_d[0:CONV_TILES, :, tile_cols(c)].rearrange("m p t -> p m t")).then_inc(loaded[s], 16)
                    sp.dma_start(gate[s][:], cols_d[IN_TILES - 1 - GATE_TILES:IN_TILES - 1, :, tile_cols(c)].rearrange("m p t -> p m t")).then_inc(loaded[s], 16)
                    if isinstance(c, int):
                        sp.dma_start(h_seq[:], state_d).then_inc(seq_loaded, 16)

                over_chunks(sp, load)

            @block.gpsimd
            def _(pool):
                pool.memset(ones[:], 1.0).then_inc(ones_ready, 1)

                def store(k, s, c):
                    if isinstance(c, int):
                        for b in range(SEQS):
                            pool.wait_ge(seq_ready, b + 1)
                            pool.dma_start(new_state_s[b], h_next[:, b % 2, :]).then_inc(h_stored[b % 2], 16)
                    pool.wait_ge(y_ready, c + 1)
                    if isinstance(c, int):
                        pool.dma_start(y_d[0:GATE_TILES, :, 0:NS].rearrange("m p t -> p m t"), y_out[:, :, 0:NS]).then_inc(y_stored, 16)
                    else:
                        pool.dma_start(y_d[0:GATE_TILES, :, bass.ds(c * P - NS, P)].rearrange("m p t -> p m t"), y_out[:]).then_inc(y_stored, 16)

                over_chunks(pool, store)
                pool.wait_ge(h_ready, NT)
                pool.dma_start(new_state_p, h[:]).then_inc(h_stored[0], 16)
                pool.wait_ge(y_stored, 16 * NT)
                pool.wait_ge(h_stored[0], 16 * (SEQS // 2 + 1))
                pool.wait_ge(h_stored[1], 16 * (SEQS // 2))

            @block.scalar
            def _(act):
                act.wait_ge(par_loaded, 32)
                act.activation(dt_par[:, 1:2], dt_par[:, 1:2], ACT.Exp).then_inc(dt_act, 1)
                act.wait_ge(dt_step, 1)
                act.activation(dt_abs[:], dt[:], ACT.Abs).then_inc(dt_act, 1)
                act.wait_ge(dt_act, 2)
                act.activation(dt_abs[:], dt_abs[:], ACT.Exp, scale=-1.0).then_inc(dt_act, 1)
                act.wait_ge(dt_step, 2)
                act.activation(dt_abs[:], dt_abs[:], ACT.Ln).then_inc(dt_act, 1)

                def body(k, s, c):
                    first = isinstance(c, int)
                    if first:
                        act.wait_ge(dt_step, 6)
                    else:
                        act.wait_ge(rows_done, c)
                    act.activation(dt_cum[:, 0, :], dt[:, tile_cols(c)], ACT.Copy)
                    act.activation(dt_cum[:, 1, :], cum[:, tile_cols(c)], ACT.Copy).then_inc(fix_ready, 1)
                    act.wait_ge(small_done, c + 1)
                    if not first:
                        act.wait_ge(seg_ready, c)
                        act.wait_ge(xdt_ready, c)
                        act.wait_ge(end_done, c)
                    act.activation(by_row[:], small_ps[:, 0:2, :], ACT.Copy).then_inc(by_row_ready, 1)
                    act.wait_ge(rows_done, c + 1)
                    if not first:
                        act.wait_ge(h_ready, c)
                    act.activation(from_start[:], rows_ps[:], ACT.Exp).then_inc(start_ready, 1)
                    act.wait_ge(end_diff, c + 1)
                    act.activation(to_end[:], to_end[:], ACT.Exp).then_inc(end_ready, 1)
                    act.wait_ge(b_done, c + 1)
                    if not first:
                        act.wait_ge(h_done, c)
                    act.activation(b_rows[:], b_ps[:], ACT.Copy).then_inc(b_ready, 1)
                    act.wait_ge(seg_ready, c + 1)
                    act.activation(decay[:], decay[:], ACT.Exp).then_inc(decay_ready, 1)
                    act.wait_ge(gated, c + 1)
                    act.activation(y_sq[:], y[:], ACT.Square).then_inc(squared, 1)
                    act.wait_ge(mean_ready, c + 1)
                    act.activation(y_rms[:], y_rms[:], ACT.Sqrt).then_inc(root_ready, 1)

                over_chunks(act, body)

            @block.vector
            def _(dve):
                dve.wait_ge(dt_loaded, 16)
                dve.wait_ge(par_loaded, 32)
                dve.tensor_scalar(dt[:], dt[:], dt_par[:, 0:1], None, ALU.add).then_inc(dt_step, 1)
                dve.wait_ge(dt_act, 3)
                dve.tensor_scalar(dt_abs[:], dt_abs[:], 1.0, None, ALU.add).then_inc(dt_step, 1)
                dve.wait_ge(dt_act, 4)
                dve.scalar_tensor_tensor(out=dt[:], in0=dt[:], scalar=0.0, in1=dt_abs[:], op0=ALU.max, op1=ALU.add).then_inc(dt_step, 1)
                dve.wait_ge(dt_step, 3)
                dve.memset(dt[:, NS:P - META], 0.0).then_inc(dt_step, 1)
                dve.wait_ge(dt_step, 4)
                dve.tensor_scalar(log_decay[:], dt[:], dt_par[:, 1:2], -1.0, ALU.mult, ALU.mult).then_inc(dt_step, 1)
                dve.wait_ge(dt_step, 5)
                dve.tensor_tensor_scan(cum[:], keep[:], log_decay[:], 0.0, ALU.mult, ALU.add).then_inc(dt_step, 1)
                dve.wait_ge(consts_loaded, 16 * CONSTS)

                def body(k, s, c):
                    first = isinstance(c, int)
                    which = 0 if first else 1
                    dve.wait_ge(loaded[s], k * 32 + 32)
                    dve.wait_ge(by_row_ready, c + 1)
                    dve.wait_ge(end_done, c + 1)
                    dve.tensor_tensor(to_end[:], small_ps[:, 2, :], by_row[:, 1, :], ALU.subtract).then_inc(end_diff, 1)
                    dve.wait_ge(start_ready, c + 1)
                    for hh in range(HEADS):
                        last = dve.tensor_scalar(decay[:, hh, :], rows_ps[:, hh, :], by_row[:, 1, hh:hh + 1], 0.0,
                                                 ALU.subtract, ALU.min)
                    last.then_inc(seg_ready, 1)
                    dve.wait_ge(x_done, c + 1)
                    if not first:
                        dve.wait_ge(y_done, c)
                    dve.tensor_tensor(x_dt[:], x_ps[:], by_row[:, 0, :].unsqueeze(2).broadcast_to([P, HEADS, HD]), ALU.mult).then_inc(xdt_ready, 1)
                    dve.wait_ge(scores_done, c + 1)
                    dve.tensor_tensor(scores[:], scores_ps[:], causal[:, which:which + 1, :].broadcast_to([P, GROUPS, P]), ALU.mult).then_inc(masked, 1)
                    for g in range(GROUPS):
                        lo = g * PER_GROUP
                        last = dve.tensor_tensor(c_start[:, lo:lo + PER_GROUP, :], from_start[:, lo:lo + PER_GROUP, :],
                                                 xbc[s][:, 6 + g:7 + g, :].broadcast_to([P, PER_GROUP, P]), ALU.mult)
                    last.then_inc(c_ready, 1)
                    dve.wait_ge(decay_ready, c + 1)
                    dve.wait_ge(masked, c + 1)
                    for g in range(GROUPS):
                        lo = g * PER_GROUP
                        last = dve.tensor_tensor(weights[:, lo:lo + PER_GROUP, :], decay[:, lo:lo + PER_GROUP, :],
                                                 scores[:, g:g + 1, :].broadcast_to([P, PER_GROUP, P]), ALU.mult)
                    last.then_inc(w_ready, 1)
                    dve.wait_ge(end_ready, c + 1)
                    dve.wait_ge(xdt_ready, c + 1)
                    if not first:
                        dve.wait_ge(h_done, c)
                    dve.tensor_tensor(x_end[:], x_dt[:], to_end[:].unsqueeze(2).broadcast_to([P, HEADS, HD]), ALU.mult).then_inc(xend_ready, 1)
                    if first:
                        dve.wait_ge(xend_ready, 1)
                        xe = x_end[:].rearrange("p h d -> p (h d)")
                        for b in range(SEQS + 1):
                            last = dve.tensor_scalar(x_block[:, b, :], xe, block_row[:, b:b + 1], None, ALU.mult)
                        last.then_inc(block_ready, 1)
                    dve.wait_ge(y_done, c + 1)
                    for j in range(GATE_TILES):
                        last = dve.scalar_tensor_tensor(out=y[:, j, :], in0=xbc[s][:, j, :], scalar=ssd_par[:, 0, j:j + 1],
                                                        in1=y_ps[:, j, :], op0=ALU.mult, op1=ALU.add)
                    last.then_inc(skip_done, 1)
                    dve.wait_ge(skip_done, c + 1)
                    dve.tensor_tensor(y[:], y[:], gate[s][:], ALU.mult).then_inc(gated, 1)
                    if first:
                        dve.wait_ge(start_ready, 1)
                        for b in range(SEQS):
                            kept = from_start[:, :, b * STEPS + STEPS - 1:b * STEPS + STEPS].broadcast_to([P, HEADS, HD])
                            dve.tensor_tensor(h_kept[:].rearrange("p (h d) -> p h d", h=HEADS),
                                              h_seq[:, b, :].rearrange("p (h d) -> p h d", h=HEADS), kept, ALU.mult).then_inc(seq_step, 1)
                            dve.wait_ge(seq_step, b + 1)
                            dve.wait_ge(seq_done, b + 1)
                            if b >= 2:
                                dve.wait_ge(h_stored[b % 2], 16 * (b // 2))
                            dve.tensor_tensor(h_next[:, b % 2, :], h_kept[:], h_ps[:], ALU.add).then_inc(seq_ready, 1)
                            dve.wait_ge(seq_ready, b + 1)
                        dve.wait_ge(h_done, 1)
                        dve.tensor_copy(h[:], h_ps[:]).then_inc(h_ready, 1)
                    else:
                        dve.wait_ge(h_done, c + 1)
                        kept = from_start[:, :, P - 1:P].broadcast_to([P, HEADS, HD])
                        dve.tensor_tensor(h_kept[:].rearrange("p (h d) -> p h d", h=HEADS),
                                          h[:].rearrange("p (h d) -> p h d", h=HEADS), kept, ALU.mult).then_inc(h_step, 1)
                        dve.wait_ge(h_step, c)
                        dve.tensor_tensor(h[:], h_kept[:], h_ps[:], ALU.add).then_inc(h_ready, 1)
                        dve.wait_ge(h_ready, c + 1)
                    dve.wait_ge(var_done, c + 1)
                    dve.tensor_scalar(y_rms[:], var_ps, 1.0 / SSD_W, RMS_EPS, ALU.mult, ALU.add).then_inc(mean_ready, 1)
                    dve.wait_ge(root_ready, c + 1)
                    dve.reciprocal(y_rms[:], y_rms[:]).then_inc(inv_ready, 1)
                    dve.wait_ge(inv_ready, c + 1)
                    if not first:
                        dve.wait_ge(y_stored, c * 16)
                    for j in range(GATE_TILES):
                        last = dve.scalar_tensor_tensor(out=y_out[:, j, :], in0=y[:, j, :], scalar=ssd_par[:, 1, j:j + 1],
                                                        in1=y_rms[:], op0=ALU.mult, op1=ALU.mult)
                    last.then_inc(y_ready, 1)

                over_chunks(dve, body)

            @block.tensor
            def _(pe):
                pe.wait_ge(consts_loaded, 16 * CONSTS)
                pe.wait_ge(ones_ready, 1)

                def body(k, s, c):
                    first = isinstance(c, int)
                    which = 0 if first else 1
                    pe.wait_ge(fix_ready, c + 1)
                    if not first:
                        pe.wait_ge(end_diff, c)
                    for a in range(2):
                        mm = pe.matmul(small_ps[:, a, :], dt_cum[:, a, :], eye[0:HEADS, 0:HEADS], start=True, stop=True)
                    mm.then_inc(small_done, 1)
                    if not first:
                        pe.wait_ge(seg_ready, c)
                        pe.wait_ge(start_ready, c)
                    for hh in range(HEADS):
                        mm = pe.matmul(rows_ps[:, hh, :], head_row[:, hh, :], dt_cum[:, 1, :], start=True, stop=True)
                    mm.then_inc(rows_done, 1)
                    pe.wait_ge(by_row_ready, c + 1)
                    pe.matmul(small_ps[:, 2, :], last_row[:, which, :], by_row[:, 1, :], start=True, stop=True).then_inc(end_done, 1)
                    pe.wait_ge(loaded[s], k * 32 + 32)
                    if not first:
                        pe.wait_ge(xdt_ready, c)
                    for j in range(4):
                        mm = pe.transpose(x_ps[:, 2 * j:2 * j + 2, :].rearrange("p h d -> p (h d)"), xbc[s][:, j, :], eye[:])
                    mm.then_inc(x_done, 1)
                    if not first:
                        pe.wait_ge(mean_ready, c)
                    for g in range(GROUPS):
                        mm = pe.transpose(b_ps[:, g, :], xbc[s][:, 4 + g, :], eye[:])
                    mm.then_inc(b_done, 1)
                    if not first:
                        pe.wait_ge(masked, c)
                    for g in range(GROUPS):
                        mm = pe.matmul(scores_ps[:, g, :], xbc[s][:, 4 + g, :], xbc[s][:, 6 + g, :], start=True, stop=True)
                    mm.then_inc(scores_done, 1)
                    pe.wait_ge(xdt_ready, c + 1)
                    pe.wait_ge(w_ready, c + 1)
                    pe.wait_ge(c_ready, c + 1)
                    if first:
                        pe.wait_ge(seq_loaded, 16)
                    else:
                        pe.wait_ge(skip_done, c)
                        pe.wait_ge(h_ready, c)
                    for hh in range(HEADS):
                        mm = pe.matmul(y_rows(hh), x_dt[:, hh, :], weights[:, hh, :], start=True, stop=False,
                                       skip_group_check=True)
                        if first:
                            for b in range(SEQS):
                                t = slice(b * STEPS, b * STEPS + STEPS)
                                mm = pe.matmul(y_rows(hh)[:, t], of_head(h_seq[:, b, :], hh), c_start[:, hh, t], start=False,
                                               stop=(b == SEQS - 1), skip_group_check=True)
                        else:
                            mm = pe.matmul(y_rows(hh), of_head(h, hh), c_start[:, hh, :], start=False, stop=True, skip_group_check=True)
                    mm.then_inc(y_done, 1)
                    pe.wait_ge(b_ready, c + 1)
                    half = SSD_W // GROUPS
                    if first:
                        pe.wait_ge(block_ready, 1)
                        for b in range(SEQS + 1):
                            if b >= 1:
                                pe.wait_ge(seq_ready, b)
                            for g in range(GROUPS):
                                mm = pe.matmul(h_ps[:, g * half:g * half + half], b_rows[:, g, :], x_block[:, b, g * half:g * half + half],
                                               start=True, stop=True)
                            mm.then_inc(seq_done if b < SEQS else h_done, 1)
                        pe.wait_ge(squared, 1)
                    else:
                        pe.wait_ge(xend_ready, c + 1)
                        for g in range(GROUPS):
                            mm = pe.matmul(h_ps[:, g * half:g * half + half], b_rows[:, g, :],
                                           x_end[:, g * PER_GROUP:g * PER_GROUP + PER_GROUP, :].rearrange("p h d -> p (h d)"),
                                           start=True, stop=True)
                    if not first:
                        mm.then_inc(h_done, 1)
                        pe.wait_ge(squared, c + 1)
                    for j in range(GATE_TILES):
                        mm = pe.matmul(var_ps, ones[:], y_sq[:, j, :], start=(j == 0), stop=(j == GATE_TILES - 1))
                    mm.then_inc(var_done, 1)

                over_chunks(pe, body)


PAIRS = HEADS // 2
R0, K0, V0 = CONV_TILES, CONV_TILES + 4, CONV_TILES + 8
LORA0 = CONV_TILES + 12
GROUP_COUNT = 1 + (NT - 1) // 2
MERGES = LEVELS - 1
COEFS = 8
C_W0, C_A0, C_KK, C_KA, C_RK, C_LNW, C_LNB = range(7)
LOG_RATE = -float(np.exp(-0.5))


def rwkv_heads(nc, cols_d, pair_par_d, state_d, eye_d, causal_d, before_d, level_d, level0_t_d, keep_d, block_row_d, head_pair_d,
               y_d, new_state_s, new_state_p):
    with Stage(nc, "rwkv") as st:
        sb, psum, sem = st.sb, st.psum, st.sem
        eye, head_pair = sb("eye", [P, P]), sb("head_pair", [P, P])
        masks = sb("masks", [P, 2, 2, P])
        level = sb("level", [P, 2, LEVELS, P])
        level0_t = sb("level0_t", [P, P])
        keep = sb("keep", [P, T])
        block_row = sb("block_row", [P, SEQS + 1])
        lora_in, gate_in = sb("lora_in", [P, T]), sb("gate_in", [P, T])
        par = sb("pair_par", [P, 3 * P + COEFS])
        one_less_ka = sb("one_less_ka", [P, 1])
        r, k, v = sb("r", [P, T]), sb("k", [P, T]), sb("v", [P, T])
        kk, k_mod, b = sb("kk", [P, T]), sb("k_mod", [P, T]), sb("b", [P, T])
        before_decay, in_decay, inv_decay = sb("before_decay", [P, T]), sb("in_decay", [P, T]), sb("inv_decay", [P, T])
        cum, tmp, bonus, gate, y_all = sb("cum", [P, T]), sb("tmp", [P, T]), sb("bonus", [P, T]), sb("gate", [P, T]), sb("y_all", [P, T])
        mid = sb("mid", [P, NT + 1])
        to_next = sb("to_next", [P, NT])
        seq_end = sb("seq_end", [P, SEQS])
        s_seq = sb("s_seq", [P, SEQS, P])
        s_new = sb("s_new", [P, SEQS, P])
        s = sb("s", [P, P])
        queries = sb("queries", [P, 2, 2, P])
        keys = sb("keys", [P, 2, 2, P])
        v_fix = sb("v_fix", [P, 2, P])
        by_row = sb("by_row", [P, 2, 3, P])
        from_k, from_b = sb("from_k", [P, 4, 2, P]), sb("from_b", [P, 4, 2, P])
        joins = sb("joins", [P, MERGES, 4, P])
        inv, inv_t, neg_x = sb("inv", [P, 4, P]), sb("inv_t", [P, 4, P]), sb("neg_x", [P, 4, P])
        start_rows = sb("start_rows", [P, P])
        rhs, neg_u = sb("rhs", [P, P]), sb("neg_u", [P, P])
        v_block, u_block = sb("v_block", [P, SEQS + 1, P]), sb("u_block", [P, SEQS + 1, P])
        bank = [psum(f"bank_{i}", BANK) for i in range(8)]

        def quads(i):
            return bank[i].rearrange("p (m t) -> p m t", m=4)

        def halves(i):
            return bank[i][:, 0:4 * HD].rearrange("p (m t) -> p m t", m=4)

        consts_loaded, lora_loaded, loaded, zeroed, lora_ready = sem("rw_consts_loaded"), sem("lora_loaded"), sem("rw_loaded"), sem("rw_zeroed"), sem("lora_ready")
        pro_act, pro_vec, lora_done, sums_done = sem("pro_act"), sem("pro_vec"), sem("lora_done"), sem("sums_done")
        qk_ready, v_ready, turned, by_row_ready = sem("qk_ready"), sem("v_ready"), sem("turned"), sem("rw_by_row_ready")
        l_done, fk_done, fb_done = sem("l_done"), sem("from_k_done"), sem("from_b_done")
        inv_step, inv_ready, fk_ready, fb_ready = sem("inv_step"), sem("inv_start_ready"), sem("from_k_ready"), sem("from_b_ready")
        joins_ready, x_done, x_ready, z_done, merged = sem("joins_ready"), sem("x_done"), sem("x_ready"), sem("z_done"), sem("merged")
        start_done, start_ready = sem("start_rows_done"), sem("start_rows_ready")
        rhs_done, rhs_ready, u_done, u_ready = sem("rhs_done"), sem("rhs_ready"), sem("u_done"), sem("u_ready")
        y_done, y_ready, s_done, s_ready = sem("y_done"), sem("y_ready"), sem("s_done"), sem("s_ready")
        blocks_ready, seq_done, seq_ready = sem("blocks_ready"), sem("rw_seq_done"), sem("rw_seq_ready")
        ep_pe, ep_vec, ep_act = sem("ep_pe"), sem("ep_vec"), sem("ep_act")
        out_stored, seq_stored = sem("rw_out_stored"), sem("rw_seq_stored")
        CONSTS = 8
        PRO_ACT, PRO_VEC, LOADS = 10, 16, 6
        EP_VEC = 7

        def over_groups(eng, body, before, after):
            with eng.Fori(0, PAIRS) as j:
                before(j)
                body(j * GROUP_COUNT, j * NT, 0, 1)
                with eng.Fori(0, GROUP_COUNT - 1) as q:
                    body(j * GROUP_COUNT + q + 1, j * NT + q * 2 + 1, q * 2 + 1, 2)
                after(j)

        def group_cols(buf, c, n):
            cols = buf[:, 0:P] if isinstance(c, int) else buf[:, bass.ds(c * P, n * P)]
            return cols.rearrange("p (a t) -> p a t", a=n)

        def thirds(buf, c):
            return buf[:, c * CH:c * CH + CH]

        def half_cols(buf, l, which):
            return buf.rearrange("p m (a h w) -> p m a h w", h=2, w=1 << l)[:, :, :, which, :]

        with nc.Block() as block:
            @block.sync
            def _(sp):
                sp.dma_start(lora_in[:], cols_d[LORA0]).then_inc(lora_loaded, 16)
                sp.dma_start(gate_in[:], cols_d[LORA0 + 1]).then_inc(lora_loaded, 16)
                sp.dma_start(keep[:], keep_d).then_inc(consts_loaded, 16)
                sp.dma_start(eye[:], eye_d).then_inc(consts_loaded, 16)
                sp.dma_start(head_pair[:], head_pair_d).then_inc(consts_loaded, 16)
                sp.dma_start(masks[:, :, 0, :], before_d.rearrange("a s t -> s a t")).then_inc(consts_loaded, 16)
                sp.dma_start(masks[:, :, 1, :], causal_d.rearrange("a s t -> s a t")).then_inc(consts_loaded, 16)
                sp.dma_start(level[:], level_d.rearrange("a l s t -> s a l t")).then_inc(consts_loaded, 16)
                sp.dma_start(level0_t[:], level0_t_d).then_inc(consts_loaded, 16)
                sp.dma_start(block_row[:], block_row_d).then_inc(consts_loaded, 16)
                sp.wait_ge(zeroed, 1)

                def before(j):
                    sp.wait_ge(ep_vec, j * EP_VEC)
                    for dst, first in ((r, R0), (k, K0), (v, V0)):
                        sp.dma_start(dst[:], cols_d[bass.ds(j + first, 1)].rearrange("a p t -> (a p) t")).then_inc(loaded, 16)
                    sp.dma_start(par[:], pair_par_d[bass.ds(j, 1)].rearrange("a p t -> (a p) t")).then_inc(loaded, 16)
                    for h in range(2):
                        half = slice(h * HD, h * HD + HD)
                        sp.dma_start(s_seq[half, :, half], state_d[bass.ds(j, 1), half, :, :].rearrange("a k b v -> (a k) b v")).then_inc(loaded, 16)

                over_groups(sp, lambda *_: None, before, lambda j: None)

            @block.gpsimd
            def _(pool):
                pool.memset(s_seq[:], 0.0)
                pool.memset(start_rows[:], 0.0)
                pool.memset(mid[:], 0.0).then_inc(zeroed, 1)
                pool.wait_ge(consts_loaded, 16 * CONSTS)

                def body(gi, ci, c, n):
                    which = 0 if n == 1 else 1
                    pool.wait_ge(fb_ready, gi + 1)
                    pool.wait_ge(z_done, gi * MERGES)
                    for l in range(1, LEVELS):
                        pool.tensor_tensor(joins[:, l - 1, 0:2 * n, :], from_b[:, 0:2 * n, 0, :],
                                           level[:, which, l:l + 1, :].broadcast_to([P, 2 * n, P]), ALU.mult).then_inc(joins_ready, 1)
                    if n == 1:
                        j = pair[0]
                        pool.wait_ge(seq_ready, j + 1)
                        for h in range(2):
                            half = slice(h * HD, h * HD + HD)
                            pool.dma_start(new_state_s[bass.ds(j, 1), half, :, :].rearrange("a k b v -> (a k) b v"), s_new[half, :, half]).then_inc(seq_stored, 16)

                pair = [None]

                def before(j):
                    pair[0] = j

                def after(j):
                    pool.wait_ge(ep_vec, j * EP_VEC + EP_VEC)
                    out = y_d[bass.ds(j + GATE_TILES, 1)].rearrange("a p t -> (a p) t")
                    pool.dma_start(out[:, 0:NS], y_all[:, 0:NS]).then_inc(out_stored, 16)
                    pool.dma_start(out[:, NS:KEPT], y_all[:, P:T]).then_inc(out_stored, 16)
                    for h in range(2):
                        half = slice(h * HD, h * HD + HD)
                        pool.dma_start(new_state_p[bass.ds(j, 1), half, :].rearrange("a k v -> (a k) v"), s[half, half]).then_inc(out_stored, 16)
                    pool.wait_ge(out_stored, j * 64 + 64)
                    pool.wait_ge(seq_stored, j * 32 + 32)

                over_groups(pool, body, before, after)

            @block.scalar
            def _(act):
                act.wait_ge(lora_loaded, 32)
                act.activation(lora_in[0:HD, :], lora_in[0:HD, :], ACT.Tanh)
                act.activation(gate_in[:], gate_in[:], ACT.Sigmoid).then_inc(lora_ready, 1)

                def before(j):
                    a0, v0, l0, s0 = j * PRO_ACT, j * PRO_VEC, j * 3, j * 2
                    act.wait_ge(loaded, j * 16 * LOADS + 16 * LOADS)
                    act.wait_ge(lora_done, l0 + 1)
                    for c in range(3):
                        out = act.activation(thirds(before_decay, c), bank[c][:, 0:CH], ACT.Sigmoid, bias=par[:, 3 * P + C_W0:3 * P + C_W0 + 1])
                    out.then_inc(pro_act, 1)
                    act.wait_ge(lora_done, l0 + 2)
                    for c in range(3):
                        out = act.activation(thirds(b, c), bank[3 + c][:, 0:CH], ACT.Sigmoid, bias=par[:, 3 * P + C_A0:3 * P + C_A0 + 1])
                    out.then_inc(pro_act, 1)
                    act.wait_ge(lora_done, l0 + 3)
                    for c in range(3):
                        out = act.activation(thirds(gate, c), bank[c][:, 0:CH], ACT.Copy)
                    out.then_inc(pro_act, 1)
                    act.wait_ge(pro_vec, v0 + 1)
                    act.activation(tmp[:], kk[:], ACT.Square).then_inc(pro_act, 1)
                    act.wait_ge(sums_done, s0 + 1)
                    for c in range(3):
                        out = act.activation(thirds(tmp, c), bank[3 + c][:, 0:CH], ACT.Sqrt)
                    out.then_inc(pro_act, 1)
                    act.wait_ge(pro_vec, v0 + 7)
                    act.activation(inv_decay[:], in_decay[:], ACT.Exp, scale=-1.0).then_inc(pro_act, 1)
                    act.wait_ge(pro_vec, v0 + 8)
                    act.wait_ge(pro_act, a0 + 6)
                    act.activation(in_decay[:], in_decay[:], ACT.Exp).then_inc(pro_act, 1)
                    act.activation(before_decay[:], before_decay[:], ACT.Exp).then_inc(pro_act, 1)
                    act.wait_ge(pro_vec, v0 + 10)
                    act.activation(to_next[:], to_next[:], ACT.Exp).then_inc(pro_act, 1)
                    act.activation(seq_end[:], cum[:, 0:NS].rearrange("p (b w) -> p b w", b=SEQS)[:, :, STEPS - 1], ACT.Exp).then_inc(pro_act, 1)

                def body(gi, ci, c, n):
                    act.wait_ge(s_done, ci)
                    act.activation(v_fix[:, 0:n, :], group_cols(v, c, n), ACT.Copy).then_inc(v_ready, 1)
                    act.wait_ge(turned, gi + 1)
                    for a in range(n):
                        out = act.activation(by_row[:, a, :, :], bank[a][:, 0:3 * P].rearrange("p (a t) -> p a t", a=3), ACT.Copy)
                    out.then_inc(by_row_ready, 1)
                    if n == 1:
                        act.wait_ge(start_done, pair[0] + 1)
                        act.activation(start_rows[:, 0:NS], bank[7][:, 0:NS], ACT.Copy).then_inc(start_ready, 1)
                    for l in range(MERGES):
                        act.wait_ge(x_done, gi * MERGES + (l + 1))
                        act.activation(neg_x[:, 0:2 * n, :], quads(0)[:, 0:2 * n, :], ACT.Copy, scale=-1.0).then_inc(x_ready, 1)
                    for a in range(n):
                        i = ci + a
                        act.wait_ge(rhs_done, i + 1)
                        act.activation(rhs[:], bank[3][:, 0:P], ACT.Copy).then_inc(rhs_ready, 1)
                        act.wait_ge(u_done, i + 1)
                        act.activation(neg_u[:], bank[4][:, 0:P], ACT.Copy, scale=-1.0).then_inc(u_ready, 1)
                        act.wait_ge(y_done, i + 1)
                        col = slice(0, P) if n == 1 else bass.ds((c + a) * P, P)
                        act.activation(y_all[:, col], bank[5][:, 0:P], ACT.Copy).then_inc(y_ready, 1)

                pair = [None]

                def before_pair(j):
                    pair[0] = j
                    before(j)

                def after(j):
                    act.wait_ge(ep_vec, j * EP_VEC + 1)
                    act.activation(cum[:], tmp[:], ACT.Square).then_inc(ep_act, 1)
                    act.wait_ge(ep_vec, j * EP_VEC + 2)
                    act.activation(inv_decay[:], inv_decay[:], ACT.Sqrt).then_inc(ep_act, 1)

                over_groups(act, body, before_pair, after)

            @block.vector
            def _(dve):
                dve.wait_ge(consts_loaded, 16 * CONSTS)
                dve.wait_ge(zeroed, 1)

                def coef(i):
                    return par[:, 3 * P + i:3 * P + i + 1]

                def before(j):
                    a0, v0, s0 = j * PRO_ACT, j * PRO_VEC, j * 2
                    dve.wait_ge(loaded, j * 16 * LOADS + 16 * LOADS)
                    dve.tensor_scalar(kk[:], k[:], coef(C_KK), None, ALU.mult).then_inc(pro_vec, 1)
                    dve.tensor_scalar(one_less_ka[:], coef(C_KA), -1.0, 1.0, ALU.mult, ALU.add).then_inc(pro_vec, 1)
                    dve.wait_ge(pro_act, a0 + 1)
                    dve.tensor_scalar(before_decay[:], before_decay[:], LOG_RATE, None, ALU.mult).then_inc(pro_vec, 1)
                    dve.wait_ge(pro_act, a0 + 2)
                    dve.wait_ge(pro_vec, v0 + 2)
                    dve.tensor_scalar(k_mod[:], b[:], coef(C_KA), one_less_ka[:], ALU.mult, ALU.add).then_inc(pro_vec, 1)
                    dve.wait_ge(pro_vec, v0 + 3)
                    dve.tensor_tensor_scan(cum[:], keep[:], before_decay[:], 0.0, ALU.mult, ALU.add).then_inc(pro_vec, 1)
                    dve.wait_ge(pro_vec, v0 + 5)
                    by_tile = cum[:].rearrange("p (c t) -> p c t", c=NT)
                    dve.tensor_copy(mid[:, 1:NT], by_tile[:, 1:NT, P // 2 - 1]).then_inc(pro_vec, 1)
                    dve.wait_ge(pro_vec, v0 + 6)
                    dve.tensor_tensor(in_decay[:].rearrange("p (c t) -> p c t", c=NT), by_tile,
                                      mid[:, 0:NT].unsqueeze(2).broadcast_to([P, NT, P]), ALU.subtract).then_inc(pro_vec, 1)
                    dve.wait_ge(pro_vec, v0 + 7)
                    dve.tensor_tensor(before_decay[:], in_decay[:], before_decay[:], ALU.subtract).then_inc(pro_vec, 1)
                    dve.tensor_tensor(to_next[:], by_tile[:, :, P - 1], mid[:, 0:NT], ALU.subtract).then_inc(pro_vec, 1)
                    dve.wait_ge(pro_vec, v0 + 9)
                    dve.tensor_tensor(to_next[:], to_next[:], mid[:, 1:NT + 1], ALU.add).then_inc(pro_vec, 1)
                    dve.tensor_tensor(k_mod[:], k_mod[:], k[:], ALU.mult).then_inc(pro_vec, 1)
                    dve.wait_ge(pro_act, a0 + 5)
                    dve.tensor_scalar(tmp[:], tmp[:], 1e-12, None, ALU.max).then_inc(pro_vec, 1)
                    dve.wait_ge(pro_vec, v0 + 12)
                    dve.reciprocal(tmp[:], tmp[:]).then_inc(pro_vec, 1)
                    dve.wait_ge(pro_vec, v0 + 13)
                    dve.tensor_tensor(kk[:], kk[:], tmp[:], ALU.mult).then_inc(pro_vec, 1)
                    dve.wait_ge(pro_vec, v0 + 14)
                    dve.tensor_tensor(b[:], kk[:], b[:], ALU.mult)
                    dve.scalar_tensor_tensor(out=tmp[:], in0=r[:], scalar=coef(C_RK), in1=k_mod[:], op0=ALU.mult, op1=ALU.mult).then_inc(pro_vec, 1)
                    dve.wait_ge(sums_done, s0 + 2)
                    for c in range(3):
                        last = dve.tensor_tensor(thirds(bonus, c), bank[c][:, 0:CH], thirds(v, c), ALU.mult)
                    last.then_inc(pro_vec, 1)
                    dve.wait_ge(pro_vec, v0 + 16)
                    dve.wait_ge(pro_act, a0 + 10)

                def body(gi, ci, c, n):
                    which = 0 if n == 1 else 1
                    dve.wait_ge(s_done, ci)
                    dve.tensor_tensor(queries[:, 0:n, 0, :], group_cols(kk, c, n), group_cols(before_decay, c, n), ALU.mult)
                    dve.tensor_tensor(queries[:, 0:n, 1, :], group_cols(r, c, n), group_cols(in_decay, c, n), ALU.mult)
                    dve.tensor_tensor(keys[:, 0:n, 0, :], group_cols(k_mod, c, n), group_cols(inv_decay, c, n), ALU.mult)
                    dve.tensor_tensor(keys[:, 0:n, 1, :], group_cols(b, c, n), group_cols(inv_decay, c, n), ALU.mult).then_inc(qk_ready, 1)
                    m = 2 * n
                    pair_masks = masks[:, which, :, :]
                    dve.wait_ge(fb_done, gi + 1)
                    for i in range(m):
                        last = dve.tensor_tensor(from_b[:, i, :, :], bank[5 + i % 2][:, i // 2 * 2 * P:(i // 2 + 1) * 2 * P].rearrange("p (a t) -> p a t", a=2), pair_masks, ALU.mult)
                    last.then_inc(fb_ready, 1)
                    dve.wait_ge(l_done, gi + 1)
                    for h in range(2):
                        last = dve.tensor_tensor(inv[:].rearrange("p (a h) t -> p a h t", h=2)[:, 0:n, h, :],
                                                 bank[(2, 7)[h]][:, 0:n * P].rearrange("p (a t) -> p a t", a=n),
                                                 level0_t[:].unsqueeze(1).broadcast_to([P, n, P]), ALU.mult)
                    last.then_inc(inv_step, 1)
                    dve.wait_ge(fb_ready, gi + 1)
                    dve.tensor_tensor(inv_t[:, 0:m, :], from_b[:, 0:m, 0, :], level[:, 1, 0:1, :].broadcast_to([P, m, P]), ALU.mult).then_inc(inv_step, 1)
                    dve.wait_ge(inv_step, gi * 2 + 2)
                    eyes = eye[:].unsqueeze(1).broadcast_to([P, m, P])
                    dve.tensor_tensor(inv[:, 0:m, :], eyes, inv[:, 0:m, :], ALU.subtract)
                    dve.tensor_tensor(inv_t[:, 0:m, :], eyes, inv_t[:, 0:m, :], ALU.subtract).then_inc(inv_ready, 1)
                    dve.wait_ge(fk_done, gi + 1)
                    for i in range(m):
                        last = dve.tensor_tensor(from_k[:, i, :, :], bank[3 + i % 2][:, i // 2 * 2 * P:(i // 2 + 1) * 2 * P].rearrange("p (a t) -> p a t", a=2), pair_masks, ALU.mult)
                    last.then_inc(fk_ready, 1)
                    dve.wait_ge(inv_ready, gi + 1)
                    for l in range(1, LEVELS):
                        dve.wait_ge(z_done, gi * MERGES + l)
                        if l < LEVELS - 1:
                            t = half_cols(inv[:, 0:m, :], l, 0)
                            dve.tensor_tensor(t, t, half_view(1, m, l), ALU.add)
                        t = half_cols(inv_t[:, 0:m, :], l, 1)
                        dve.tensor_tensor(t, t, half_view(2, m, l), ALU.add).then_inc(merged, 1)
                        dve.wait_ge(merged, gi * MERGES + l)
                    if n == 1:
                        dve.wait_ge(by_row_ready, gi + 1)
                        dve.wait_ge(u_ready, ci + 1)
                        for bb in range(SEQS + 1):
                            dve.tensor_scalar(v_block[:, bb, :], by_row[:, 0, 2, :], block_row[:, bb:bb + 1], None, ALU.mult)
                            last = dve.tensor_scalar(u_block[:, bb, :], neg_u[:], block_row[:, bb:bb + 1], None, ALU.mult)
                        last.then_inc(blocks_ready, 1)
                        dve.wait_ge(s_done, ci + 1)
                        for bb in range(SEQS):
                            last = dve.scalar_tensor_tensor(out=s_new[:, bb, :], in0=bank[bb // 3][:, bb % 3 * P:bb % 3 * P + P],
                                                            scalar=seq_end[:, bb:bb + 1], in1=head_pair[:], op0=ALU.mult, op1=ALU.mult)
                        last.then_inc(seq_ready, 1)
                        dve.scalar_tensor_tensor(out=s[:], in0=bank[2][:, 2 * P:3 * P], scalar=to_next[:, 0:1],
                                                 in1=head_pair[:], op0=ALU.mult, op1=ALU.mult).then_inc(s_ready, 1)
                    else:
                        for a in range(n):
                            dve.wait_ge(s_done, ci + (a + 1))
                            dve.scalar_tensor_tensor(out=s[:], in0=bank[6][:, 0:P], scalar=to_next[:, bass.ds(c + a, 1)],
                                                     in1=head_pair[:], op0=ALU.mult, op1=ALU.mult).then_inc(s_ready, 1)

                def half_view(i, m, l):
                    return halves(i)[:, 0:m, :].rearrange("p m (a w) -> p m a w", w=1 << l)

                def after(j):
                    e0 = j * EP_VEC
                    dve.wait_ge(ep_pe, j * 2 + 1)
                    for c in range(3):
                        last = dve.scalar_tensor_tensor(out=thirds(tmp, c), in0=bank[c][:, 0:CH], scalar=-1.0 / HD,
                                                        in1=thirds(y_all, c), op0=ALU.mult, op1=ALU.add)
                    last.then_inc(ep_vec, 1)
                    dve.wait_ge(ep_pe, j * 2 + 2)
                    for c in range(3):
                        last = dve.tensor_scalar(thirds(inv_decay, c), bank[3 + c][:, 0:CH], 1.0 / HD, GN_EPS, ALU.mult, ALU.add)
                    last.then_inc(ep_vec, 1)
                    dve.wait_ge(ep_act, j * 2 + 2)
                    dve.reciprocal(inv_decay[:], inv_decay[:]).then_inc(ep_vec, 1)
                    dve.wait_ge(ep_vec, e0 + 3)
                    dve.tensor_tensor(tmp[:], tmp[:], inv_decay[:], ALU.mult).then_inc(ep_vec, 1)
                    dve.wait_ge(ep_vec, e0 + 4)
                    dve.tensor_scalar(tmp[:], tmp[:], coef(C_LNW), coef(C_LNB), ALU.mult, ALU.add).then_inc(ep_vec, 1)
                    dve.wait_ge(ep_vec, e0 + 5)
                    dve.tensor_tensor(tmp[:], tmp[:], bonus[:], ALU.add).then_inc(ep_vec, 1)
                    dve.wait_ge(ep_vec, e0 + 6)
                    dve.tensor_tensor(y_all[:], tmp[:], gate[:], ALU.mult).then_inc(ep_vec, 1)

                over_groups(dve, body, before, after)

            @block.tensor
            def _(pe):
                pe.wait_ge(consts_loaded, 16 * CONSTS)
                pe.wait_ge(lora_ready, 1)
                pe.wait_ge(zeroed, 1)

                def lora(j, which, first_bank):
                    src = gate_in if which == 2 else lora_in
                    for c in range(3):
                        mm = pe.matmul(bank[first_bank + c][:, 0:CH], par[:, which * P:which * P + P], thirds(src, c), start=True, stop=True)
                    mm.then_inc(lora_done, 1)

                def head_sums(src, first_bank, done):
                    for c in range(3):
                        mm = pe.matmul(bank[first_bank + c][:, 0:CH], head_pair[:], thirds(src, c), start=True, stop=True)
                    mm.then_inc(done, 1)

                def before(j):
                    pair[0] = j
                    pe.wait_ge(loaded, j * 16 * LOADS + 16 * LOADS)
                    lora(j, 0, 0)
                    lora(j, 1, 3)
                    pe.wait_ge(pro_act, j * PRO_ACT + 1)
                    lora(j, 2, 0)
                    pe.wait_ge(pro_act, j * PRO_ACT + 4)
                    head_sums(tmp, 3, sums_done)
                    pe.wait_ge(pro_vec, j * PRO_VEC + 15)
                    head_sums(tmp, 0, sums_done)

                pair = [None]

                def body(gi, ci, c, n):
                    m = 2 * n
                    pe.wait_ge(qk_ready, gi + 1)
                    pe.wait_ge(v_ready, gi + 1)
                    pe.wait_ge(s_ready, ci)
                    pe.wait_ge(y_ready, ci)
                    for a in range(n):
                        for i, src in enumerate((keys[:, a, 0, :], keys[:, a, 1, :], v_fix[:, a, :])):
                            mm = pe.transpose(bank[a][:, i * P:i * P + P], src, eye[:])
                    mm.then_inc(turned, 1)

                    def head(buf, i):
                        lo = i % 2 * HD
                        return buf[lo:lo + HD, i // 2]

                    for which, first_bank, done in ((1, 5, fb_done), (0, 3, fk_done)):
                        for i in range(m):
                            mm = pe.matmul(bank[first_bank + i % 2][:, i // 2 * 2 * P:(i // 2 + 1) * 2 * P], head(keys, i)[:, which, :],
                                           head(queries, i).rearrange("p a t -> p (a t)"), start=True, stop=True)
                        mm.then_inc(done, 1)
                        if which == 1:
                            for i in range(m):
                                mm = pe.matmul(bank[(2, 7)[i % 2]][:, i // 2 * P:i // 2 * P + P], head(queries, i)[:, 0, :], head(keys, i)[:, 1, :], start=True, stop=True)
                            mm.then_inc(l_done, 1)
                    if n == 1:
                        pe.wait_ge(inv_ready, gi + 1)
                        for bb in range(SEQS):
                            t = slice(bb * STEPS, bb * STEPS + STEPS)
                            mm = pe.matmul(bank[7][:, t], s_seq[:, bb, :], queries[:, 0, 0, t], start=True, stop=True)
                        mm.then_inc(start_done, 1)
                    pe.wait_ge(by_row_ready, gi + 1)
                    for l in range(1, LEVELS):
                        k0 = gi * MERGES + l
                        pe.wait_ge(joins_ready, k0)
                        if l == 1:
                            pe.wait_ge(inv_ready, gi + 1)
                        else:
                            pe.wait_ge(merged, k0 - 1)
                        for i in range(m):
                            mm = pe.matmul(quads(0)[:, i, :], joins[:, l - 1, i, :], inv[:, i, :], start=True, stop=True)
                        mm.then_inc(x_done, 1)
                        pe.wait_ge(x_ready, k0)
                        if l < LEVELS - 1:
                            for i in range(m):
                                pe.matmul(halves(1)[:, i, :], inv_t[:, i, :], half_cols(neg_x[:, i:i + 1, :], l, 0)[:, 0], start=True, stop=True)
                        for i in range(m):
                            mm = pe.matmul(halves(2)[:, i, :], neg_x[:, i, :], half_cols(inv_t[:, i:i + 1, :], l, 1)[:, 0], start=True, stop=True)
                        mm.then_inc(z_done, 1)
                    pe.wait_ge(merged, gi * MERGES + MERGES)
                    pe.wait_ge(fk_ready, gi + 1)
                    for a in range(n):
                        i = ci + a
                        heads = (0, 1)

                        def cols(h):
                            return slice(h * HD, h * HD + HD)

                        if a == 1:
                            pe.wait_ge(s_ready, i)
                        if n == 1:
                            pe.wait_ge(start_ready, pair[0] + 1)
                            pe.matmul(bank[3][:, 0:P], start_rows[:], eye[:], start=True, stop=False, skip_group_check=True)
                        else:
                            pe.matmul(bank[3][:, 0:P], queries[:, a, 0, :], s[:], start=True, stop=False, skip_group_check=True)
                        for h in heads:
                            mm = pe.matmul(bank[3][:, cols(h)], from_k[:, 2 * a + h, 0, :], by_row[:, a, 2, cols(h)], start=False, stop=True,
                                           skip_group_check=True)
                        mm.then_inc(rhs_done, 1)
                        pe.wait_ge(rhs_ready, i + 1)
                        for h in heads:
                            mm = pe.matmul(bank[4][:, cols(h)], inv_t[:, 2 * a + h, :], rhs[:, cols(h)], start=True, stop=True)
                        mm.then_inc(u_done, 1)
                        pe.wait_ge(u_ready, i + 1)
                        if a == 1:
                            pe.wait_ge(y_ready, i)
                        for h in heads:
                            pe.matmul(bank[5][cols(h), 0:P], by_row[:, a, 2, cols(h)], from_k[:, 2 * a + h, 1, :], start=True, stop=False,
                                      skip_group_check=True)
                            pe.matmul(bank[5][cols(h), 0:P], neg_u[:, cols(h)], from_b[:, 2 * a + h, 1, :], start=False, stop=False,
                                      skip_group_check=True)
                        if n == 1:
                            for bb in range(SEQS):
                                t = slice(bb * STEPS, bb * STEPS + STEPS)
                                mm = pe.matmul(bank[5][:, t], s_seq[:, bb, :], queries[:, 0, 1, t], start=False, stop=(bb == SEQS - 1),
                                               skip_group_check=True)
                        else:
                            mm = pe.matmul(bank[5][:, 0:P], s[:], queries[:, a, 1, :], start=False, stop=True, skip_group_check=True)
                        mm.then_inc(y_done, 1)
                        if n == 1:
                            pe.wait_ge(blocks_ready, pair[0] + 1)
                            for g in range(3):
                                out = bank[g][:, 0:3 * P]
                                flat = slice(3 * g, 3 * g + 3)
                                pe.matmul(out, by_row[:, 0, 0, :], v_block[:, flat, :].rearrange("p a v -> p (a v)"), start=True, stop=False,
                                          skip_group_check=True)
                                pe.matmul(out, by_row[:, 0, 1, :], u_block[:, flat, :].rearrange("p a v -> p (a v)"), start=False, stop=False,
                                          skip_group_check=True)
                                had = min(3, SEQS - 3 * g)
                                mm = pe.matmul(bank[g][:, 0:had * P], eye[:], s_seq[:, 3 * g:3 * g + had, :].rearrange("p a v -> p (a v)"),
                                               start=False, stop=True, skip_group_check=True)
                        else:
                            pe.matmul(bank[6][:, 0:P], by_row[:, a, 0, :], by_row[:, a, 2, :], start=True, stop=False, skip_group_check=True)
                            pe.matmul(bank[6][:, 0:P], by_row[:, a, 1, :], neg_u[:], start=False, stop=False, skip_group_check=True)
                            mm = pe.matmul(bank[6][:, 0:P], eye[:], s[:], start=False, stop=True, skip_group_check=True)
                        mm.then_inc(s_done, 1)

                def after(j):
                    pe.wait_ge(s_ready, j * NT + NT)
                    pe.wait_ge(y_ready, j * NT + NT)
                    head_sums(y_all, 0, ep_pe)
                    pe.wait_ge(ep_act, j * 2 + 1)
                    head_sums(cum, 3, ep_pe)

                over_groups(pe, body, before, after)


KEPT_CHUNKS = ((0, CH), (CH, CH), (2 * CH, KEPT - 2 * CH))
ROW_TILES = [(lo, min(P, KEPT - lo)) for lo in range(0, KEPT, P)]
RT = len(ROW_TILES)
PEER_HEADS = 8
TOPK = 16
N_KEYS = 128
LOWEST = -3.0e38


def inverse_rms_steps(dve, act_sqrt_done, src_banks, dst, chunks, width, step, base):
    for c, (lo, n) in enumerate(chunks):
        last = dve.tensor_scalar(dst[:, lo:lo + n], src_banks[c][:, 0:n], 1.0 / width, RMS_EPS, ALU.mult, ALU.add)
    last.then_inc(step, 1)
    dve.wait_ge(act_sqrt_done, 1)
    dve.reciprocal(dst[:], dst[:]).then_inc(step, 1)
    dve.wait_ge(step, base + 2)


def output_projection(nc, h, u, x_kept_d, y_d, w_out_d, norm_g_d):
    with Stage(nc, "outp") as st:
        sb, psum, sem = st.sb, st.psum, st.sem
        y = sb("y", [P, KD, KEPT])
        w = [sb(f"w_out_{s}", [P, WCOLS]) for s in range(2)]
        squares = sb("squares", [P, 2, KEPT])
        inv_rms = sb("inv_rms", [P, KEPT])
        norm_g, ones = sb("norm_ffn_g", [P, KD]), sb("ones", [P, P])
        out = [[psum(f"out_{s}{c}", BANK) for c in range(3)] for s in range(2)]
        x_loaded, g_loaded, ones_ready = sem("xk_loaded"), sem("g_loaded"), sem("ones_ready")
        y_loaded = [sem(f"y_loaded_{k}") for k in range(KD)]
        w_loaded = [sem(f"w_out_loaded_{s}") for s in range(2)]
        out_done, h_ready, squared, sum_done, rms_step, rooted, u_ready = (
            sem("out_done"), sem("h_ready"), sem("squared"), sem("sum_done"), sem("rms_step"), sem("rooted"), sem("u_ready"))

        def over_tiles(eng, body):
            with eng.Fori(0, KD // 2) as q:
                for s in range(2):
                    body(q, s, q * 2 + s)

        with nc.Block() as block:
            @block.sync
            def _(sp):
                for k in range(KD):
                    sp.dma_start(y[:, k, :], y_d[k]).then_inc(y_loaded[k], 16)
                sp.dma_start(norm_g[:], norm_g_d).then_inc(g_loaded, 16)
                sp.dma_start(h[:], x_kept_d.rearrange("k p t -> p k t")).then_inc(x_loaded, 16)

            @block.gpsimd
            def _(pool):
                pool.memset(ones[:], 1.0).then_inc(ones_ready, 1)

                def load(q, s, m):
                    pool.wait_ge(out_done, q * 6)
                    pool.dma_start(w[s][:], at(w_out_d, m)).then_inc(w_loaded[s], 16)

                pool.wait_ge(ones_ready, 1)
                over_tiles(pool, load)

            @block.tensor
            def _(pe):
                def project(q, s, m):
                    pe.wait_ge(w_loaded[s], q * 16 + 16)
                    pe.wait_ge(h_ready, q * 6)
                    for c, (lo, n) in enumerate(KEPT_CHUNKS):
                        for k in range(KD):
                            mm = pe.matmul(out[s][c][:, 0:n], w[s][:, k * P:k * P + P], y[:, k, lo:lo + n], start=(k == 0), stop=(k == KD - 1))
                        mm.then_inc(out_done, 1)

                for k in range(KD):
                    pe.wait_ge(y_loaded[k], 16)
                over_tiles(pe, project)
                pe.wait_ge(ones_ready, 1)
                pe.wait_ge(h_ready, 3 * KD)
                for k in range(KD):
                    pe.wait_ge(squared, k + 1)
                    for c, (lo, n) in enumerate(KEPT_CHUNKS):
                        mm = pe.matmul(out[0][c][:, 0:n], ones[:], squares[:, k % 2, lo:lo + n], start=(k == 0), stop=(k == KD - 1))
                    mm.then_inc(sum_done, 1)

            @block.scalar
            def _(act):
                act.wait_ge(h_ready, 3 * KD)
                for k in range(KD):
                    if k >= 2:
                        act.wait_ge(sum_done, k - 1)
                    act.activation(squares[:, k % 2, :], h[:, k, :], ACT.Square).then_inc(squared, 1)
                act.wait_ge(rms_step, 1)
                act.activation(inv_rms[:], inv_rms[:], ACT.Sqrt).then_inc(rooted, 1)

            @block.vector
            def _(dve):
                dve.wait_ge(x_loaded, 16)
                dve.wait_ge(g_loaded, 16)

                def add(q, s, m):
                    row = h[:, bass.ds(m, 1), :].rearrange("p a t -> p (a t)")
                    for c, (lo, n) in enumerate(KEPT_CHUNKS):
                        dve.wait_ge(out_done, q * 6 + (3 * s + c + 1))
                        dve.tensor_tensor(row[:, lo:lo + n], row[:, lo:lo + n], out[s][c][:, 0:n], ALU.add).then_inc(h_ready, 1)

                over_tiles(dve, add)
                dve.wait_ge(sum_done, KD)
                inverse_rms_steps(dve, rooted, out[0], inv_rms, KEPT_CHUNKS, D, rms_step, 0)
                for k in range(KD):
                    dve.scalar_tensor_tensor(out=u[:, k, :], in0=h[:, k, :], scalar=norm_g[:, k:k + 1], in1=inv_rms[:],
                                             op0=ALU.mult, op1=ALU.mult).then_inc(u_ready, 1)


def pick_experts(nc, u, picks, w_query_d, keys_d, iota_d):
    with Stage(nc, "pick") as st:
        sb, psum, sem = st.sb, st.psum, st.sem
        w = [sb(f"w_query_{s}", [P, WCOLS]) for s in range(2)]
        keys = sb("sub_keys", [P, 2, N_KEYS])
        q_cols = [sb(f"q_{s}", [P, KEPT]) for s in range(2)]
        scores = [sb(f"scores_{s}", [P, RT, 2, N_KEYS]) for s in range(2)]
        rest = sb("rest", [P, 2, N_KEYS])
        top = sb("top", [P, RT, 2, TOPK])
        top_at = sb("top_at", [P, RT, 2, TOPK], U32)
        top_key = sb("top_key", [P, RT, 2, TOPK])
        sums = sb("sums", [P, 2, TOPK, TOPK])
        best = sb("best", [P, RT, TOPK])
        expo = sb("expo", [P, RT, TOPK])
        best_at = sb("best_at", [P, RT, TOPK], U32)
        half_at = sb("half_at", [P, 2, RT, TOPK], U32)
        half_f = sb("half_f", [P, 2, RT, TOPK])
        hit = sb("hit", [P, RT, TOPK, TOPK])
        total = sb("total", [P, RT])
        iota = sb("iota", [P, P])
        q_ps = [psum(f"q_ps_{c}", BANK) for c in range(3)]
        s_ps = [psum(f"s_ps_{i}", BANK) for i in range(4)]
        iota_loaded, keys_loaded = sem("iota_loaded"), sem("keys_loaded")
        w_loaded = [sem(f"w_query_loaded_{s}") for s in range(2)]
        q_done, q_ready, s_done, s_ready = sem("q_done"), sem("q_ready"), sem("s_done"), sem("s_ready")
        vec, topped, shifted, exped = sem("pick_vec"), sem("topped"), sem("shifted"), sem("exped")
        SCORE_BANKS = -(-RT // 2)

        with nc.Block() as block:
            @block.sync
            def _(sp):
                sp.dma_start(iota[:], iota_d).then_inc(iota_loaded, 16)
                with sp.Fori(0, PEER_HEADS) as i:
                    for s in range(2):
                        sp.wait_ge(q_done, i * 6)
                        sp.dma_start(w[s][:], w_query_d[bass.ds(i * 2 + s, 1)].rearrange("a p c -> (a p) c")).then_inc(w_loaded[s], 16)
                    sp.wait_ge(s_done, i * SCORE_BANKS)
                    sp.dma_start(keys[:], keys_d[bass.ds(i, 1)].rearrange("a p h k -> (a p) h k")).then_inc(keys_loaded, 16)

            @block.tensor
            def _(pe):
                with pe.Fori(0, PEER_HEADS) as i:
                    for s in range(2):
                        pe.wait_ge(w_loaded[s], i * 16 + 16)
                        for c, (lo, n) in enumerate(KEPT_CHUNKS):
                            pe.wait_ge(q_ready, i * 6 + 3 * s)
                            for k in range(KD):
                                mm = pe.matmul(q_ps[c][:, 0:n], w[s][:, k * P:k * P + P], u[:, k, lo:lo + n], start=(k == 0), stop=(k == KD - 1))
                            mm.then_inc(q_done, 1)
                    pe.wait_ge(q_ready, i * 6 + 6)
                    pe.wait_ge(keys_loaded, i * 16 + 16)
                    for b in range(SCORE_BANKS):
                        if b >= 4:
                            pe.wait_ge(s_ready, i * SCORE_BANKS + (b - 3))
                        else:
                            pe.wait_ge(s_ready, i * SCORE_BANKS)
                        for a in range(2 * b, min(2 * b + 2, RT)):
                            lo, n = ROW_TILES[a]
                            for s in range(2):
                                col = (a % 2 * 2 + s) * N_KEYS
                                mm = pe.matmul(s_ps[b % 4][0:n, col:col + N_KEYS], q_cols[s][:, lo:lo + n], keys[:, s, :], start=True, stop=True)
                        mm.then_inc(s_done, 1)

            @block.scalar
            def _(act):
                def head(i, slot, even):
                    for s in range(2):
                        act.wait_ge(s_done, i * SCORE_BANKS)
                        for c, (lo, n) in enumerate(KEPT_CHUNKS):
                            act.wait_ge(q_done, i * 6 + (3 * s + c + 1))
                            act.activation(q_cols[s][:, lo:lo + n], q_ps[c][:, 0:n], ACT.Copy).then_inc(q_ready, 1)
                    act.wait_ge(topped, even)
                    for b in range(SCORE_BANKS):
                        act.wait_ge(s_done, i * SCORE_BANKS + (b + 1))
                        tiles = ROW_TILES[2 * b:2 * b + 2]
                        n = tiles[0][1]
                        act.activation(scores[slot][0:n, 2 * b:2 * b + len(tiles), :, :],
                                       s_ps[b % 4][0:n, 0:len(tiles) * 2 * N_KEYS].rearrange("p (a h k) -> p a h k", a=len(tiles), h=2),
                                       ACT.Copy).then_inc(s_ready, 1)

                def softmax(i):
                    act.wait_ge(shifted, i + 1)
                    act.activation(expo[:], expo[:], ACT.Exp).then_inc(exped, 1)

                head(0, 0, 0)
                head(1, 1, 0)
                softmax(0)
                with act.Fori(1, PEER_HEADS // 2) as q:
                    head(q * 2, 0, q * 2 - 1)
                    softmax(q * 2 - 1)
                    head(q * 2 + 1, 1, q * 2)
                    softmax(q * 2)
                softmax(PEER_HEADS - 1)

            @block.vector
            def _(dve):
                dve.memset(best[:], 0.0)
                dve.memset(total[:], 0.0)
                dve.memset(best_at[:], 0)
                dve.memset(top_at[:], 0).then_inc(vec, 1)
                dve.wait_ge(iota_loaded, 16)
                dve.wait_ge(vec, 1)

                def head(i, slot):
                    dve.sem_clear(vec)
                    steps = [0]

                    def step(last):
                        steps[0] += 1
                        last.then_inc(vec, 1)
                        dve.wait_ge(vec, steps[0])

                    for a, (_, n) in enumerate(ROW_TILES):
                        if a == 0:
                            dve.wait_ge(s_ready, i * SCORE_BANKS + 1)
                            step(dve.tensor_copy(best[:, 0, 0:1], total[:, 0:1]))
                        for s in range(2):
                            last = dve.max(top[0:n, a, s, 0:8], scores[slot][0:n, a, s, :])
                        step(last)
                        for s in range(2):
                            dve.max_index(top_at[0:n, a, s, 0:8], top[0:n, a, s, 0:8], scores[slot][0:n, a, s, :])
                            last = dve.match_replace(rest[0:n, s, :], top[0:n, a, s, 0:8], scores[slot][0:n, a, s, :], LOWEST)
                        step(last)
                        for s in range(2):
                            last = dve.max(top[0:n, a, s, 8:16], rest[0:n, s, :])
                        step(last)
                        for s in range(2):
                            last = dve.max_index(top_at[0:n, a, s, 8:16], top[0:n, a, s, 8:16], rest[0:n, s, :])
                        if a + 1 < RT:
                            dve.wait_ge(s_ready, i * SCORE_BANKS + ((a + 1) // 2 + 1))
                        last = dve.tensor_tensor(sums[0:n, 0, :, :], top[0:n, a, 0, :].unsqueeze(2).broadcast_to([n, TOPK, TOPK]),
                                                 top[0:n, a, 1, :].unsqueeze(1).broadcast_to([n, TOPK, TOPK]), ALU.add)
                        step(last)
                        every = sums[0:n].rearrange("p s i j -> p s (i j)")
                        step(dve.max(best[0:n, a, 0:8], every[:, 0, :]))
                        dve.max_index(best_at[0:n, a, 0:8], best[0:n, a, 0:8], every[:, 0, :])
                        step(dve.match_replace(every[:, 1, :], best[0:n, a, 0:8], every[:, 0, :], LOWEST))
                        step(dve.max(best[0:n, a, 8:16], every[:, 1, :]))
                        last = dve.max_index(best_at[0:n, a, 8:16], best[0:n, a, 8:16], every[:, 1, :])
                    last.then_inc(topped, 1)
                    dve.wait_ge(topped, i + 1)
                    dve.tensor_tensor(expo[:], best[:], best[:, :, 0:1].broadcast_to([P, RT, TOPK]), ALU.subtract).then_inc(shifted, 1)
                    dve.tensor_copy(top_key[:], top_at[:])
                    dve.tensor_scalar(half_at[:, 0, :, :], best_at[:], 4, None, ALU.logical_shift_right)
                    step(dve.tensor_scalar(half_at[:, 1, :, :], best_at[:], 15, None, ALU.bitwise_and))
                    step(dve.tensor_copy(half_f[:], half_at[:]))
                    for s in range(2):
                        cube = [P, RT, TOPK, TOPK]
                        step(dve.tensor_tensor(hit[:], iota[:, 0:TOPK].unsqueeze(1).unsqueeze(1).broadcast_to(cube),
                                               half_f[:, s, :, :].unsqueeze(3).broadcast_to(cube), ALU.is_equal))
                        step(dve.tensor_tensor(hit[:], hit[:], top_key[:, :, s, :].unsqueeze(2).broadcast_to(cube), ALU.mult))
                        step(dve.tensor_reduce(picks[:, s, :, bass.ds(i * TOPK, TOPK)], hit[:], AX_X, ALU.add))
                    dve.wait_ge(exped, i + 1)
                    step(dve.tensor_reduce(total[:], expo[:], AX_X, ALU.add))
                    step(dve.reciprocal(total[:], total[:]))
                    step(dve.tensor_tensor(picks[:, 2, :, bass.ds(i * TOPK, TOPK)], expo[:], total[:].unsqueeze(2).broadcast_to([P, RT, TOPK]), ALU.mult))

                with dve.Fori(0, PEER_HEADS // 2) as q:
                    head(q * 2, 0)
                    head(q * 2 + 1, 1)


GROUP_ROWS = 64
ROW_GROUPS = KEPT // GROUP_ROWS
BATCH = 8


def spread_gates(nc, picks, gates_d, eye_d, iota_d):
    with Stage(nc, "spread") as st:
        sb, psum, sem = st.sb, st.psum, st.sem
        eye, iota = sb("eye", [P, P]), sb("iota", [P, P])
        by_pick = sb("by_pick", [P, 3, KEPT])
        hot_i = [sb(f"hot_i_{s}", [P, BATCH, P]) for s in range(2)]
        hot_j = [sb(f"hot_j_{s}", [P, BATCH, P]) for s in range(2)]
        spread = [sb(f"spread_{s}", [P, N_KEYS, GROUP_ROWS]) for s in range(2)]
        g_ps = [psum(f"g_ps_{s}", BATCH, P) for s in range(2)]
        t_ps = [psum(f"t_ps_{s}", BANK) for s in range(2)]
        consts_loaded, turned, turned_out = sem("consts_loaded"), sem("turned"), sem("turned_out")
        hot_ready, g_done, g_out = sem("hot_ready"), sem("g_done"), sem("g_out")
        stored = [sem(f"g_stored_{s}") for s in range(2)]
        PER_GROUP = GROUP_ROWS // BATCH

        def over_groups(eng, before, batch, after):
            def group(q, s, g):
                before(q, s, g)
                with eng.Fori(0, PER_GROUP // 2) as b:
                    for a in range(2):
                        batch(s, a, g * PER_GROUP + b * 2 + a, b * 2 + a)
                after(q, s, g)

            with eng.Fori(0, ROW_GROUPS // 2) as q:
                for s in range(2):
                    group(q, s, q * 2 + s)
            group(ROW_GROUPS // 2, 0, ROW_GROUPS - 1)

        nothing = lambda *_: None
        with nc.Block() as block:
            @block.sync
            def _(sp):
                sp.dma_start(eye[:], eye_d).then_inc(consts_loaded, 16)
                sp.dma_start(iota[:], iota_d).then_inc(consts_loaded, 16)

                def store(q, s, g):
                    sp.wait_ge(g_out, g * PER_GROUP + PER_GROUP)
                    sp.dma_start(at(gates_d, g), spread[s][:].rearrange("p j t -> p (j t)")).then_inc(stored[s], 16)

                over_groups(sp, nothing, lambda *_: None, store)
                for s in range(2):
                    sp.wait_ge(stored[s], 16 * ((ROW_GROUPS + 1 - s) // 2))

            @block.tensor
            def _(pe):
                pe.wait_ge(consts_loaded, 32)
                for a, (lo, n) in enumerate(ROW_TILES):
                    if a >= 2:
                        pe.wait_ge(turned_out, a - 1)
                    for s in range(3):
                        mm = pe.transpose(t_ps[a % 2][:, s * P:s * P + n], picks[0:n, s, a, :], eye[0:n, 0:n])
                    mm.then_inc(turned, 1)

                def batch(s, a, i, b):
                    pe.wait_ge(hot_ready, i + 1)
                    if a == 0:
                        pe.wait_ge(g_out, i)
                    else:
                        pe.wait_ge(g_out, i - 1)
                    for t in range(BATCH):
                        mm = pe.matmul(g_ps[a][:, t, :], hot_i[a][:, t, :], hot_j[a][:, t, :], start=True, stop=True)
                    mm.then_inc(g_done, 1)

                over_groups(pe, nothing, batch, nothing)

            @block.scalar
            def _(act):
                for a, (lo, n) in enumerate(ROW_TILES):
                    act.wait_ge(turned, a + 1)
                    act.activation(by_pick[:, :, lo:lo + n], t_ps[a % 2][:, 0:3 * P].rearrange("p (s t) -> p s t", s=3)[:, :, 0:n],
                                   ACT.Copy).then_inc(turned_out, 1)

                def before(q, s, g):
                    act.wait_ge(stored[s], q * 16)

                def batch(s, a, i, b):
                    act.wait_ge(g_done, i + 1)
                    act.activation(spread[s][:, :, bass.ds(b * BATCH, BATCH)], g_ps[a].rearrange("p t j -> p j t"), ACT.Copy).then_inc(g_out, 1)

                over_groups(act, before, batch, nothing)

            @block.vector
            def _(dve):
                dve.wait_ge(consts_loaded, 32)
                dve.wait_ge(turned_out, RT)

                def batch(s, a, i, b):
                    if a == 0:
                        dve.wait_ge(g_done, i)
                    else:
                        dve.wait_ge(g_done, i - 1)
                    for t in range(BATCH):
                        row = bass.ds(i * BATCH + t, 1)
                        dve.tensor_scalar(hot_i[a][:, t, :], iota[:], by_pick[:, 0, row], None, ALU.is_equal)
                        last = dve.tensor_scalar(hot_j[a][:, t, :], iota[:], by_pick[:, 1, row], by_pick[:, 2, row], ALU.is_equal, ALU.mult)
                    last.then_inc(hot_ready, 1)

                over_groups(dve, nothing, batch, nothing)


SET = 4
SETS = N_KEYS // SET


def run_experts(nc, h, u, gates_d, up_d, down_d, norm_g_d, out_d):
    with Stage(nc, "experts") as st:
        sb, psum, sem = st.sb, st.psum, st.sem
        up = [sb(f"up_{s}", [P, WCOLS]) for s in range(2)]
        down = [sb(f"down_{s}", [P, SET, D]) for s in range(2)]
        gates = [sb(f"gates_{s}", [P, ROW_GROUPS, SET, GROUP_ROWS]) for s in range(2)]
        act_v = [sb(f"act_v_{s}", [P, SET, KEPT]) for s in range(2)]
        inv_rms = gates[0][:].rearrange("p g j t -> p (g j t)")[:, 0:KEPT]
        norm_g, ones = sb("norm_final_g", [P, KD]), sb("ones", [P, P])
        up_ps = [[psum(f"up_ps_{s}{c}", BANK) for c in range(3)] for s in range(2)]
        down_ps = [psum(f"down_ps_{s}", BANK) for s in range(2)]
        up_loaded = [sem(f"up_loaded_{s}") for s in range(2)]
        down_loaded = [sem(f"down_loaded_{s}") for s in range(2)]
        gates_loaded = [sem(f"gates_loaded_{s}") for s in range(2)]
        ones_ready, g_loaded = sem("ones_ready"), sem("g_loaded")
        up_done, gelu_ready, gated, down_done, added = sem("up_done"), sem("gelu_ready"), sem("gated"), sem("down_done"), sem("added")
        squared, sum_done, rms_step, rooted, out_ready, out_stored = (
            sem("squared"), sem("sum_done"), sem("rms_step"), sem("rooted"), sem("out_ready"), sem("out_stored"))
        UNITS = KD * 3

        def over_sets(eng, first, second):
            first(0, 0)
            with eng.Fori(0, SETS // 2 - 1) as q:
                first(q * 2 + 1, 1)
                second(q * 2, 0)
                first(q * 2 + 2, 0)
                second(q * 2 + 1, 1)
            first(SETS - 1, 1)
            second(SETS - 2, 0)
            second(SETS - 1, 1)

        nothing = lambda *_: None
        with nc.Block() as block:
            @block.sync
            def _(sp):
                def first(g, slot):
                    i0 = g * SET
                    early = isinstance(g, int) and g == 0
                    if not early:
                        sp.wait_ge(gated, i0 - SET)
                    src = gates_d[:, :, g * SET:g * SET + SET, :] if isinstance(g, int) else gates_d[:, :, bass.ds(g * SET, SET), :]
                    sp.dma_start(gates[slot][:], src.rearrange("g p j t -> p g j t")).then_inc(gates_loaded[slot], 16)
                    for e in range(SET):
                        s = e % 2
                        if not (early and e < 2):
                            sp.wait_ge(up_done, i0 * 3 + (3 * e - 3))
                        sp.dma_start(up[s][:], at(up_d, i0 + e)).then_inc(up_loaded[s], 16)
                    if not (isinstance(g, int) and g == 0):
                        sp.wait_ge(down_done, (g - 1) * UNITS)
                    src = down_d[g * SET:g * SET + SET] if isinstance(g, int) else down_d[bass.ds(g * SET, SET)]
                    sp.dma_start(down[slot][:], src.rearrange("j p d -> p j d")).then_inc(down_loaded[slot], 16)

                over_sets(sp, first, nothing)
                sp.wait_ge(out_ready, KD)
                sp.dma_start(out_d.rearrange("k p t -> p k t"), h[:]).then_inc(out_stored, 16)
                sp.wait_ge(out_stored, 16)

            @block.gpsimd
            def _(pool):
                pool.memset(ones[:], 1.0).then_inc(ones_ready, 1)
                pool.dma_start(norm_g[:], norm_g_d).then_inc(g_loaded, 16)

            @block.tensor
            def _(pe):
                def first(g, slot):
                    i0 = g * SET
                    for e in range(SET):
                        s = e % 2
                        pe.wait_ge(up_loaded[s], i0 * 8 + (e // 2 * 16 + 16))
                        for c, (lo, n) in enumerate(KEPT_CHUNKS):
                            if not (isinstance(g, int) and e < 2):
                                pe.wait_ge(gelu_ready, i0 * 3 + (3 * e - 5 + c))
                            for k in range(KD):
                                mm = pe.matmul(up_ps[s][c][:, 0:n], up[s][:, k * P:k * P + P], u[:, k, lo:lo + n], start=(k == 0), stop=(k == KD - 1))
                            mm.then_inc(up_done, 1)

                def second(g, slot):
                    pe.wait_ge(down_loaded[slot], g * 8 + (16 - 8 * slot))
                    pe.wait_ge(gated, g * SET + SET)
                    for m in range(KD):
                        for c, (lo, n) in enumerate(KEPT_CHUNKS):
                            i = 3 * m + c
                            if i >= 2:
                                pe.wait_ge(added, g * UNITS + (i - 1))
                            else:
                                pe.wait_ge(added, g * UNITS)
                            for e in range(SET):
                                mm = pe.matmul(down_ps[i % 2][:, 0:n], down[slot][:, e, m * P:m * P + P], act_v[slot][:, e, lo:lo + n],
                                               start=(e == 0), stop=(e == SET - 1))
                            mm.then_inc(down_done, 1)

                over_sets(pe, first, second)
                pe.wait_ge(ones_ready, 1)
                for k in range(KD):
                    pe.wait_ge(squared, k + 1)
                    for c, (lo, n) in enumerate(KEPT_CHUNKS):
                        mm = pe.matmul(up_ps[0][c][:, 0:n], ones[:], act_v[0][:, k % 2, lo:lo + n], start=(k == 0), stop=(k == KD - 1))
                    mm.then_inc(sum_done, 1)

            @block.scalar
            def _(act):
                def first(g, slot):
                    i0 = g * SET
                    if not (isinstance(g, int) and g == 0):
                        act.wait_ge(down_done, (g - 1) * UNITS)
                    for e in range(SET):
                        for c, (lo, n) in enumerate(KEPT_CHUNKS):
                            act.wait_ge(up_done, i0 * 3 + (3 * e + c + 1))
                            act.activation(act_v[slot][:, e, lo:lo + n], up_ps[e % 2][c][:, 0:n], ACT.Gelu).then_inc(gelu_ready, 1)

                over_sets(act, first, nothing)
                act.wait_ge(added, SETS * UNITS)
                for k in range(KD):
                    if k >= 2:
                        act.wait_ge(sum_done, k - 1)
                    act.activation(act_v[0][:, k % 2, :], h[:, k, :], ACT.Square).then_inc(squared, 1)
                act.wait_ge(rms_step, 1)
                act.activation(inv_rms, inv_rms, ACT.Sqrt).then_inc(rooted, 1)

            @block.vector
            def _(dve):
                def first(g, slot):
                    dve.wait_ge(gates_loaded[slot], g * 8 + (16 - 8 * slot))
                    for e in range(SET):
                        dve.wait_ge(gelu_ready, g * (3 * SET) + (3 * e + 3))
                        a = act_v[slot][:, e, :].rearrange("p (g t) -> p g t", g=ROW_GROUPS)
                        dve.tensor_tensor(a, a, gates[slot][:, :, e, :], ALU.mult).then_inc(gated, 1)

                def second(g, slot):
                    for m in range(KD):
                        for c, (lo, n) in enumerate(KEPT_CHUNKS):
                            i = 3 * m + c
                            dve.wait_ge(down_done, g * UNITS + (i + 1))
                            dve.tensor_tensor(h[:, m, lo:lo + n], h[:, m, lo:lo + n], down_ps[i % 2][:, 0:n], ALU.add).then_inc(added, 1)

                over_sets(dve, first, second)
                dve.wait_ge(sum_done, KD)
                dve.wait_ge(g_loaded, 16)
                inverse_rms_steps(dve, rooted, up_ps[0], inv_rms, KEPT_CHUNKS, D, rms_step, 0)
                for k in range(KD):
                    dve.scalar_tensor_tensor(out=h[:, k, :], in0=h[:, k, :], scalar=norm_g[:, k:k + 1], in1=inv_rms,
                                             op0=ALU.mult, op1=ALU.mult).then_inc(out_ready, 1)


def pack_w_in(inputs):
    w_in = np.asarray(inputs["w_in"])[0]
    gate, conv, dt, shift = np.split(w_in, [512, 1536, 1544], axis=1)
    out = np.zeros((IN_TILES, P, WCOLS + 8), w_in.dtype)
    w_cols = np.zeros((D, IN_TILES * P), w_in.dtype)
    w_cols[:, :1024] = conv
    w_cols[:, 1024:2816] = shift
    w_cols[:, 2816:3328] = gate
    w_cols[:, 3328:3336] = dt
    out[:, :, :WCOLS] = w_cols.reshape(KD, P, IN_TILES, P).transpose(2, 1, 0, 3).reshape(IN_TILES, P, WCOLS)
    out[:8, :, WCOLS:WCOLS + 4] = np.asarray(inputs["conv_w"])[0].T.reshape(8, P, 4)
    out[:8, :, WCOLS + 4] = np.asarray(inputs["conv_b"])[0].reshape(8, P)
    out[8:22, :, WCOLS] = np.asarray(inputs["shift_mu"])[0].reshape(14, P)
    return out


def pack_hist(inputs):
    conv = np.asarray(inputs["state_conv"])[0]
    shift = np.asarray(inputs["state_shift"])[0]
    out = np.zeros((CONV_TILES + SHIFT_TILES, P, SEQS, HIST), conv.dtype)
    out[:8] = conv.transpose(2, 0, 1).reshape(8, P, SEQS, HIST)
    out[8:, :, :, HIST - 1] = shift.T.reshape(14, P, SEQS)
    return out


def pack_ssd_par(inputs):
    a = np.asarray
    by_head = np.stack([a(inputs["dt_bias"])[0], a(inputs["a_log"])[0]], axis=1)
    d = np.repeat(a(inputs["d_skip"])[0], HD).reshape(4, P).T
    g = a(inputs["ssm_norm"])[0].reshape(4, P).T
    return by_head, np.stack([d, g], axis=1)


def pack_ssd_state(inputs):
    return np.asarray(inputs["state_ssd"])[0].transpose(3, 0, 1, 2).reshape(STATE, SEQS, SSD_W)


def pack_pair_par(inputs):
    a = lambda name: np.asarray(inputs[name])[0]
    out = np.zeros((PAIRS, P, 3 * P + COEFS), a("decay_w2").dtype)
    cut = lambda w: w.reshape(w.shape[0], PAIRS, P).transpose(1, 0, 2)
    out[:, 0:HD, 0:P] = cut(a("decay_w2"))
    out[:, HD:P, P:2 * P] = cut(a("iclr_a2"))
    out[:, :, 2 * P:3 * P] = cut(a("gate_g2"))
    for i, name in enumerate(("decay_w0", "iclr_a0", "k_k", "k_a", "r_k", "lnx_w", "lnx_b")):
        out[:, :, 3 * P + i] = a(name).reshape(PAIRS, P)
    return out


def pack_wkv(inputs):
    w = np.asarray(inputs["state_wkv"])[0]
    return w.reshape(SEQS, PAIRS, 2, HD, HD).transpose(1, 2, 4, 0, 3).reshape(PAIRS, P, SEQS, HD)


def tile_weights(w):
    return np.ascontiguousarray(w.reshape(KD, P, -1, P).transpose(2, 1, 0, 3).reshape(-1, P, WCOLS))


def pack_keys(inputs):
    return np.ascontiguousarray(np.asarray(inputs["sub_keys"])[0].transpose(1, 3, 0, 2))


def pack_up(inputs):
    w = np.asarray(inputs["expert_u"])[0].reshape(N_KEYS, N_KEYS, KD, P)
    return np.ascontiguousarray(w.transpose(1, 3, 2, 0).reshape(N_KEYS, P, WCOLS))


def pack_down(inputs):
    return np.ascontiguousarray(np.asarray(inputs["expert_v"])[0].reshape(N_KEYS, N_KEYS, D).transpose(1, 0, 2))


def decoder_step(nc, i, o):
    def scratch(name, *shape):
        return nc.dram_tensor(name, shape, F32, kind="Internal").ap()

    cols = scratch("cols", IN_TILES, P, T)
    y = scratch("mixed", KD, P, KEPT)
    gates = scratch("gates", ROW_GROUPS, P, N_KEYS * GROUP_ROWS)
    input_projection(nc, i["x_t"], i["norm_mix"], i["w_in"], i["hist"], cols, o["conv_s"], o["conv_p"], o["shift_s"], o["shift_p"])
    ssd_heads(nc, cols, i["dt_par"], i["ssd_par"], i["state_ssd"], i["eye"], i["causal"], i["last_row"], i["keep"],
              i["block_row"], i["head_row"], y, o["ssd_s"], o["ssd_p"])
    rwkv_heads(nc, cols, i["pair_par"], i["state_wkv"], i["eye"], i["causal"], i["before"], i["level"], i["level0_t"], i["keep"],
               i["block_row"], i["head_pair"], y, o["wkv_s"], o["wkv_p"])
    with Stage(nc, "kept") as st:
        h, u = st.sb("h", [P, KD, KEPT]), st.sb("u", [P, KD, KEPT])
        picks = st.sb("picks", [P, 3, RT, P])
        output_projection(nc, h, u, i["x_kept"], y, i["w_out"], i["norm_ffn"])
        pick_experts(nc, u, picks, i["w_query"], i["keys"], i["iota"])
        spread_gates(nc, picks, gates, i["eye"], i["iota"])
        run_experts(nc, h, u, gates.rearrange("g p (j t) -> g p j t", j=N_KEYS), i["up"], i["down"], i["norm_final"], o["y"])


OUTS = {
    "y": (KD, P, KEPT),
    "conv_s": (CONV_TILES, P, SEQS, HIST), "conv_p": (CONV_TILES, P, HIST),
    "shift_s": (SHIFT_TILES, P, SEQS, HIST), "shift_p": (SHIFT_TILES, P, HIST),
    "ssd_s": (SEQS, STATE, SSD_W), "ssd_p": (STATE, SSD_W),
    "wkv_s": (PAIRS, P, SEQS, HD), "wkv_p": (PAIRS, P, HD),
}


def by_channel(g):
    return g.reshape(-1, P).T


def lay_out(inputs):
    a = {name: np.asarray(value) for name, value in inputs.items()}
    samples, prompt = a["x_sample"].reshape(NS, D), a["x_prompt"].reshape(PROMPT, D)
    padding = np.zeros((P - NS - META, D), prompt.dtype)
    rows = np.concatenate([samples, padding, a["meta_tokens"], prompt])
    dt_par, ssd_par = pack_ssd_par(a)
    arrays = {
        "x_t": rows.T.reshape(KD, P, T), "x_kept": np.concatenate([samples, prompt]).T.reshape(KD, P, KEPT),
        "norm_mix": by_channel(a["norm_mix"][0]), "norm_ffn": by_channel(a["norm_ffn"][0]), "norm_final": by_channel(a["norm_final"]),
        "w_in": pack_w_in(a), "hist": pack_hist(a), "dt_par": dt_par, "ssd_par": ssd_par, "state_ssd": pack_ssd_state(a),
        "pair_par": pack_pair_par(a), "state_wkv": pack_wkv(a), "w_out": tile_weights(a["w_out"][0]),
        "w_query": tile_weights(a["w_query"][0]), "keys": pack_keys(a), "up": pack_up(a), "down": pack_down(a),
        **constants(),
    }
    return {name: np.ascontiguousarray(value) for name, value in arrays.items()}


def kernel(**inputs):
    import concourse.bacc as bacc
    from concourse.bass_utils import run_bass_kernel_spmd

    nc = bacc.Bacc("TRN2", target_bir_lowering=False, num_devices=1)
    arrays = lay_out(inputs)
    ins = {name: nc.dram_tensor("in_" + name, value.shape, mybir.dt.from_np(value.dtype), kind="ExternalInput").ap()
           for name, value in arrays.items()}
    outs = {name: nc.dram_tensor("out_" + name, shape, F32, kind="ExternalOutput").ap() for name, shape in OUTS.items()}
    decoder_step(nc, ins, outs)
    ran = run_bass_kernel_spmd(nc, [{"in_" + name: value for name, value in arrays.items()}], core_ids=[0])
    r = {name: np.asarray(ran.results[0]["out_" + name]) for name in OUTS}

    y = r["y"].reshape(D, KEPT).T
    conv_dim, rwkv_in = CONV_TILES * P, SHIFT_TILES * P
    return (
        y[NS:].reshape(1, PROMPT, D), y[:NS].reshape(SEQS, STEPS, D),
        r["conv_p"].reshape(conv_dim, HIST).T[None, None],
        r["ssd_p"].T.reshape(1, 1, HEADS, HD, STATE),
        r["shift_p"][:, :, HIST - 1].reshape(1, 1, rwkv_in),
        r["wkv_p"].reshape(HEADS, HD, HD).transpose(0, 2, 1)[None, None],
        r["conv_s"].reshape(conv_dim, SEQS, HIST).transpose(1, 2, 0)[None],
        r["ssd_s"].transpose(0, 2, 1).reshape(1, SEQS, HEADS, HD, STATE),
        r["shift_s"][:, :, :, HIST - 1].reshape(rwkv_in, SEQS).T[None],
        r["wkv_s"].reshape(HEADS, HD, SEQS, HD).transpose(2, 0, 3, 1)[None],
    )
```

```python
from contextlib import ExitStack

import numpy as np

import concourse.bass as bass
from concourse import mybir

F32 = mybir.dt.float32
F32R = mybir.dt.float32r
U32 = mybir.dt.uint32
BF16 = mybir.dt.bfloat16
ALU = mybir.AluOpType
ACT = mybir.ActivationFunctionType
AX_X = mybir.AxisListType.X

P = 128
D = 1024
KD = D // P
SEQS, STEPS = 8, 8
NS = SEQS * STEPS
META = 16
PROMPT = 1024
T = P + PROMPT
NT = T // P
KEPT = NS + PROMPT
HIST = 3
CONV_TILES, SHIFT_TILES, GATE_TILES = 8, 14, 4
IN_TILES = CONV_TILES + SHIFT_TILES + GATE_TILES + 1
COEFS_IN = 8
CH = T // 3
E_SAMPLE = SEQS * (HIST + STEPS)
E_COLS = E_SAMPLE + HIST + T - NS
WCOLS = KD * P
RMS_EPS = 1e-6
GN_EPS = 64e-5
HEADS = 8
HD = 64
STATE = 128
BANK = 512
START = 2


class Stage:

    def __init__(self, nc, name):
        self.nc, self.name, self.ctx, self.sems = nc, name, ExitStack(), []

    def __enter__(self):
        self.ctx.__enter__()
        return self

    def __exit__(self, *failure):
        self.ctx.__exit__(*failure)
        if failure[0] is None:
            self.nc.clear_and_free_semaphores(self.sems)
            self.nc.all_engine_barrier()

    def sb(self, name, shape, dt=F32):
        return self.ctx.enter_context(self.nc.sbuf_tensor(f"{self.name}_{name}", shape, dt))

    def psum(self, name, *shape):
        n = int(np.prod(shape))
        banks = self.ctx.enter_context(self.nc.psum_tensor(f"{self.name}_{name}", [P, -(-n // BANK) * BANK], F32))
        used = banks[:, 0:n]
        return used if len(shape) == 1 else used.rearrange("p (a b) -> p a b", a=shape[0])

    def sem(self, name):
        self.sems.append(self.nc.alloc_semaphore(f"{self.name}_{name}"))
        return self.sems[-1]

    def start(self, eng, *but):
        for s in self.sems:
            if s not in but:
                eng.sem_inc(s, START)


def sample_cols(buf):
    return buf[:, 0:NS].rearrange("p (b w) -> p b w", b=SEQS)


def at(dram, m):
    return dram[m] if isinstance(m, int) else dram[bass.ds(m, 1)].rearrange("a p c -> (a p) c")


def product(pe, out, w_hi, w_lo, x_hi, x_lo, start, stop):
    pe.matmul(out, w_hi, x_hi, start=start, stop=False)
    pe.matmul(out, w_hi, x_lo, start=False, stop=False)
    return pe.matmul(out, w_lo, x_hi, start=False, stop=stop)


def input_projection(nc, x_t, norm_g_d, w_pack, coef_d, hist_d, cols_d, new_conv_s, new_conv_p, new_shift_s, new_shift_p):
    with Stage(nc, "inp") as st:
        sb, sem = st.sb, st.sem
        u = sb("u", [P, KD, T])
        squares = sb("squares", [P, 2, T])
        inv_rms = sb("inv_rms", [P, T])
        ones = sb("in_ones", [P, P])
        norm_g = sb("norm_mix_g", [P, KD])
        u_hi, u_lo = sb("u_hi", [P, KD, T], F32R), sb("u_lo", [P, KD, T], F32R)
        w = [sb(f"w_in_{s}", [P, WCOLS]) for s in range(2)]
        w_hi = [sb(f"w_in_hi_{s}", [P, WCOLS], F32R) for s in range(2)]
        w_lo = [sb(f"w_in_lo_{s}", [P, WCOLS], F32R) for s in range(2)]
        coefs = sb("coefs", [P, IN_TILES * COEFS_IN])
        raw = [sb(f"raw_{s}", [P, E_COLS]) for s in range(2)]
        mid = [sb(f"mid_{s}", [P, T]) for s in range(2)]
        done = [sb(f"done_{s}", [P, T]) for s in range(2)]
        proj = [st.psum(f"proj_{s}", 3, BANK) for s in range(2)]

        x_loaded = [sem(f"x_loaded_{k}") for k in range(KD)]
        g_loaded = sem("norm_g_loaded")
        w_loaded = [sem(f"w_in_loaded_{s}") for s in range(2)]
        hist_loaded = [sem(f"hist_loaded_{s}") for s in range(2)]
        consts_ready = sem("in_consts_ready")
        square_ready = sem("square_ready")
        sum_done = sem("sum_done")
        rms_step = sem("rms_step")
        u_ready, u_rounded, u_split = sem("u_ready"), sem("u_rounded"), sem("u_split")
        w_rounded, w_split, coefs_loaded = sem("w_rounded"), sem("w_split"), sem("coefs_loaded")
        proj_ready = sem("proj_ready")
        raw_ready = sem("raw_ready")
        vec_step = sem("in_vec_step")
        act_out = sem("in_act_out")
        stored = [sem(f"in_stored_{s}") for s in range(2)]
        edge_stored = [sem(f"edge_stored_{s}") for s in range(2)]

        def tap_sample(s, j):
            return raw[s][:, 0:E_SAMPLE].rearrange("p (b w) -> p b w", b=SEQS)[:, :, j:j + STEPS]

        def tap_rest(s, j):
            return raw[s][:, E_SAMPLE + j:E_SAMPLE + j + T - NS]

        CONV_OPS, SHIFT_OPS = 8, 4

        def vec_before(m, kind):
            return m * CONV_OPS if kind == "conv" else m * SHIFT_OPS + CONV_TILES * (CONV_OPS - SHIFT_OPS)

        def over_tiles(eng, body):
            body(0, 0, 0, "conv")
            body(0, 1, 1, "conv")
            lo = 1
            for kind, tiles in (("conv", CONV_TILES - 2), ("shift", SHIFT_TILES), ("gate", GATE_TILES)):
                with eng.Fori(lo, lo + tiles // 2) as q:
                    for s in range(2):
                        body(q, s, q * 2 + s, kind)
                lo += tiles // 2
            body(lo, 0, 2 * lo, "dt")

        with nc.Block() as block:
            @block.sync
            def _(sp):
                sp.dma_start(norm_g[:], norm_g_d).then_inc(g_loaded, 16)
                for k in range(KD):
                    sp.dma_start(u[:, k, :], x_t[k]).then_inc(x_loaded[k], 16)

                sp.dma_start(coefs[:], coef_d).then_inc(coefs_loaded, 16)

                def load(q, s, m, kind):
                    sp.wait_ge(w_split, START + m - 1)
                    sp.dma_start(w[s][:], at(w_pack, m)).then_inc(w_loaded[s], 16)

                over_tiles(sp, load)

            @block.gpsimd
            def _(pool):
                st.start(pool, *edge_stored, *stored, *hist_loaded)
                for s in range(2):
                    pool.memset(raw[s][:, E_SAMPLE:E_SAMPLE + HIST], 0.0).then_inc(consts_ready, 1)
                pool.memset(ones[:], 1.0).then_inc(consts_ready, 1)

                def load_hist(s, m):
                    dst = raw[s][:, 0:E_SAMPLE].rearrange("p (b w) -> p b w", b=SEQS)[:, :, 0:HIST]
                    src = hist_d[m] if isinstance(m, int) else hist_d[bass.ds(m, 1)].rearrange("a p b w -> (a p) b w")
                    pool.dma_start(dst, src).then_inc(hist_loaded[s], 16)

                load_hist(0, 0)

                def store(q, s, m, kind):
                    if kind in ("conv", "shift"):
                        if not (isinstance(m, int) and m == 0):
                            pool.wait_ge(edge_stored[1 - s], (q + s) * 32)
                            pool.wait_ge(stored[1 - s], (q + s) * 16)
                        pool.wait_ge(raw_ready, START + m + 1)
                        load_hist(1 - s, m + 1)
                        out_s, out_p = (new_conv_s, new_conv_p) if kind == "conv" else (new_shift_s, new_shift_p)
                        i = m if kind == "conv" else m - CONV_TILES
                        src = raw[s][:, 0:E_SAMPLE].rearrange("p (b w) -> p b w", b=SEQS)[:, :, STEPS:STEPS + HIST]
                        dst = out_s[i] if isinstance(i, int) else out_s[bass.ds(i, 1)].rearrange("a p b w -> (a p) b w")
                        pool.dma_start(dst, src).then_inc(edge_stored[s], 16)
                        pool.dma_start(at(out_p, i), raw[s][:, E_COLS - HIST:E_COLS]).then_inc(edge_stored[s], 16)
                    if kind == "shift":
                        pool.wait_ge(vec_step, START + vec_before(m + 1, kind))
                    else:
                        pool.wait_ge(act_out, START + (m + 1 if kind == "conv" else m + 1 - SHIFT_TILES))
                    pool.dma_start(at(cols_d, m), done[s][:]).then_inc(stored[s], 16)

                over_tiles(pool, store)
                pool.wait_ge(hist_loaded[0], 16 * (CONV_TILES + SHIFT_TILES + 2) // 2)
                for s in range(2):
                    pool.wait_ge(edge_stored[s], 16 * (CONV_TILES + SHIFT_TILES))
                    pool.wait_ge(stored[s], 16 * ((IN_TILES + 1 - s) // 2))

            @block.scalar
            def _(act):
                for k in range(KD):
                    act.wait_ge(x_loaded[k], START + 16)
                    if k >= 2:
                        act.wait_ge(sum_done, START + k - 1)
                    act.activation(squares[:, k % 2, :], u[:, k, :], ACT.Square).then_inc(square_ready, 1)
                act.wait_ge(rms_step, START + 3)
                act.activation(inv_rms[:], inv_rms[:], ACT.Sqrt).then_inc(rms_step, 1)

                act.wait_ge(w_loaded[0], START + 16)
                act.activation(w_hi[0][:], w[0][:], ACT.Copy).then_inc(w_rounded, 1)
                for k in range(KD):
                    act.wait_ge(u_ready, START + k + 1)
                    act.activation(u_hi[:, k, :], u[:, k, :], ACT.Copy).then_inc(u_rounded, 1)

                def evacuate(q, s, m, kind):
                    if kind != "dt":
                        act.wait_ge(w_loaded[1 - s], START + (q + 1 + s) * 16)
                        act.wait_ge(proj_ready, START + m * 3)
                        act.activation(w_hi[1 - s][:], w[1 - s][:], ACT.Copy).then_inc(w_rounded, 1)
                    first = isinstance(m, int) and m < 2
                    if not first:
                        act.wait_ge(stored[s], q * 16)
                    if kind in ("conv", "shift"):
                        act.wait_ge(hist_loaded[s], q * 16 + 16)
                        if first:
                            act.wait_ge(consts_ready, START + 2)
                        for c in range(3):
                            act.wait_ge(proj_ready, START + m * 3 + c + 1)
                            lo = NS if c == 0 else 0
                            if c == 0:
                                act.activation(tap_sample(s, HIST), sample_cols(proj[s][:, 0, :]), ACT.Copy)
                            at0 = E_SAMPLE + HIST - NS + c * CH
                            out = act.activation(raw[s][:, at0 + lo:at0 + CH], proj[s][:, c, lo:CH], ACT.Copy)
                        out.then_inc(raw_ready, 1)
                    if kind == "conv":
                        act.wait_ge(vec_step, START + vec_before(m + 1, kind))
                        act.activation(done[s][:], mid[s][:], ACT.Silu).then_inc(act_out, 1)
                    if kind in ("gate", "dt"):
                        for c in range(3):
                            act.wait_ge(proj_ready, START + m * 3 + c + 1)
                            out = act.activation(done[s][:, c * CH:c * CH + CH], proj[s][:, c, 0:CH],
                                                 ACT.Silu if kind == "gate" else ACT.Copy)
                        out.then_inc(act_out, 1)

                over_tiles(act, evacuate)

            @block.vector
            def _(dve):
                def rest_of_u(k):
                    dve.wait_ge(u_rounded, START + k + 1)
                    dve.tensor_tensor(u_lo[:, k, :], u[:, k, :], u_hi[:, k, :], ALU.subtract).then_inc(u_split, 1)

                dve.wait_ge(sum_done, START + KD)
                for c in range(3):
                    dve.tensor_scalar(inv_rms[:, c * CH:c * CH + CH], proj[0][:, c, 0:CH], 1.0 / D, RMS_EPS,
                                      ALU.mult, ALU.add).then_inc(rms_step, 1)
                dve.wait_ge(rms_step, START + 4)
                dve.reciprocal(inv_rms[:], inv_rms[:]).then_inc(rms_step, 1)
                dve.wait_ge(rms_step, START + 5)
                dve.wait_ge(g_loaded, START + 16)
                for k in range(KD):
                    dve.scalar_tensor_tensor(out=u[:, k, :], in0=u[:, k, :], scalar=norm_g[:, k:k + 1],
                                             in1=inv_rms[:], op0=ALU.mult, op1=ALU.mult).then_inc(u_ready, 1)
                    if k == 0:
                        dve.wait_ge(w_rounded, START + 1)
                        dve.tensor_tensor(w_lo[0][:], w[0][:], w_hi[0][:], ALU.subtract).then_inc(w_split, 1)
                    else:
                        rest_of_u(k - 1)
                rest_of_u(KD - 1)
                dve.wait_ge(coefs_loaded, START + 16)

                def column_work(q, s, m, kind):
                    if kind != "dt":
                        dve.wait_ge(w_rounded, START + m + 2)
                        dve.tensor_tensor(w_lo[1 - s][:], w[1 - s][:], w_hi[1 - s][:], ALU.subtract).then_inc(w_split, 1)
                    if kind not in ("conv", "shift"):
                        return

                    def coef(i):
                        return coefs[:, bass.ds(m * COEFS_IN + i, 1)]

                    before = vec_before(m, kind)
                    dve.wait_ge(raw_ready, START + m + 1)
                    if kind == "conv":
                        for j in range(HIST + 1):
                            for r, (src, dst) in enumerate(((tap_sample(s, j), sample_cols(mid[s])),
                                                            (tap_rest(s, j), mid[s][:, NS:T]))):
                                if j == 0:
                                    if r == 0 and not (isinstance(m, int) and m < 2):
                                        dve.wait_ge(act_out, START + m - 1)
                                    dve.tensor_scalar(dst, src, coef(0), coef(HIST + 1), ALU.mult,
                                                      ALU.add).then_inc(vec_step, 1)
                                else:
                                    dve.wait_ge(vec_step, START + before + (2 * j - 1 + r))
                                    dve.scalar_tensor_tensor(out=dst, in0=src, scalar=coef(j), in1=dst,
                                                             op0=ALU.mult, op1=ALU.add).then_inc(vec_step, 1)
                    else:
                        sides = ((tap_sample(s, HIST), tap_sample(s, HIST - 1), sample_cols(mid[s]), sample_cols(done[s])),
                                 (tap_rest(s, HIST), tap_rest(s, HIST - 1), mid[s][:, NS:T], done[s][:, NS:T]))
                        dve.wait_ge(act_out, START + CONV_TILES)
                        dve.wait_ge(stored[s], q * 16)
                        for now, prev, diff, _ in sides:
                            dve.tensor_tensor(diff, prev, now, ALU.subtract).then_inc(vec_step, 1)
                        for r, (now, _, diff, out) in enumerate(sides):
                            dve.wait_ge(vec_step, START + before + (1 + r))
                            dve.scalar_tensor_tensor(out=out, in0=diff, scalar=coef(0), in1=now,
                                                     op0=ALU.mult, op1=ALU.add).then_inc(vec_step, 1)

                over_tiles(dve, column_work)

            @block.tensor
            def _(pe):
                pe.wait_ge(consts_ready, START + 3)
                for k in range(KD):
                    pe.wait_ge(square_ready, START + k + 1)
                    for c in range(3):
                        mm = pe.matmul(proj[0][:, c, 0:CH], ones[:], squares[:, k % 2, c * CH:c * CH + CH],
                                       start=(k == 0), stop=(k == KD - 1))
                    mm.then_inc(sum_done, 1)
                pe.wait_ge(rms_step, START + 3)

                def project(q, s, m, kind):
                    pe.wait_ge(w_split, START + m + 1)
                    if not (isinstance(m, int) and m < 2):
                        if kind in ("conv", "shift"):
                            pe.wait_ge(raw_ready, START + m - 1)
                        else:
                            pe.wait_ge(raw_ready, START + CONV_TILES + SHIFT_TILES)
                            if kind == "gate":
                                pe.wait_ge(act_out, START + m - (SHIFT_TILES + 1))
                            else:
                                pe.wait_ge(act_out, START + m - SHIFT_TILES - 1)
                    for c in range(3):
                        for k in range(KD):
                            if isinstance(m, int) and m == 0 and c == 0:
                                pe.wait_ge(u_split, START + k + 1)
                            rows, cut = slice(c * CH, c * CH + CH), slice(k * P, k * P + P)
                            mm = product(pe, proj[s][:, c, 0:CH], w_hi[s][:, cut], w_lo[s][:, cut],
                                         u_hi[:, k, rows], u_lo[:, k, rows], k == 0, k == KD - 1)
                        mm.then_inc(proj_ready, 1)

                over_tiles(pe, project)


LEVELS = 7


def constants():
    r = np.arange(P)
    blocks = [np.where(r < NS, r // STEPS, SEQS), np.zeros(P, int)]
    same = [b[:, None] == b[None, :] for b in blocks]
    s, t = r[:, None], r[None, :]
    causal = np.stack([(s <= t) & m for m in same]).astype(np.float32)
    before = np.stack([(s < t) & m for m in same]).astype(np.float32)
    last = np.stack([m & ~np.roll(m, -1, 0) & (s >= t) if b.any() else m & (s == P - 1)
                     for m, b in zip(same, blocks)])
    last[0] = same[0] & np.isin(s, list(range(STEPS - 1, NS, STEPS)) + [P - 1])
    level = np.stack([np.stack([(s < t) & m & (s >> (l + 1) == t >> (l + 1)) & (s >> l != t >> l)
                                for l in range(LEVELS)]) for m in same]).astype(np.float32)
    keep = np.ones((P, T), np.float32)
    keep[:, [STEPS * b for b in range(SEQS)] + [P * c for c in range(NT)] + [NS]] = 0.0
    head_row = (r[:HEADS, None, None] == r[None, :HEADS, None]) * np.ones((1, 1, P))
    return {
        "eye": np.eye(P, dtype=np.float32),
        "causal": causal, "before": before, "last_row": last.astype(np.float32), "level": level, "keep": keep,
        "block_row": (blocks[0][:, None] == np.arange(SEQS + 1)[None, :]).astype(np.float32),
        "head_row": head_row.astype(np.float32),
        "head_pair": (s // HD == t // HD).astype(np.float32),
        "level0_t": level[1, 0].T.copy(),
        "iota": np.broadcast_to(r.astype(np.float32), (P, P)).copy(),
    }


def tile_cols(c):
    return slice(c * P, c * P + P) if isinstance(c, int) else bass.ds(c * P, P)


def over_chunks(eng, front, back):
    front(0, 0, 0)
    front(0, 1, 1)
    back(0, 0, 0)
    with eng.Fori(1, (NT - 1) // 2) as q:
        front(q, 0, q * 2)
        back(q - 1, 1, q * 2 - 1)
        front(q, 1, q * 2 + 1)
        back(q, 0, q * 2)
    last = NT - 1
    front(last // 2, 0, last)
    back(last // 2 - 1, 1, last - 1)
    back(last // 2, 0, last)


def is_tile(c, n):
    return isinstance(c, int) and c == n


SSD_W = HEADS * HD
GROUPS = 2
PER_GROUP = HEADS // GROUPS


def ssd_heads(nc, cols_d, dt_par_d, ssd_par_d, state_d, eye_d, causal_d, last_row_d, keep_d, block_row_d, head_row_d,
              y_d, new_state_s, new_state_p):
    with Stage(nc, "ssd") as st:
        sb, psum, sem = st.sb, st.psum, st.sem
        eye, ones = sb("eye", [P, P]), sb("ones", [P, P])
        causal = sb("causal", [P, 2, P])
        last_row = sb("last_row", [P, 2, P])
        keep = sb("keep", [HEADS, T])
        block_row = sb("block_row", [P, SEQS + 1])
        head_row = sb("head_row", [HEADS, HEADS, P])
        dt_par = sb("dt_par", [HEADS, 2])
        ssd_par = sb("ssd_par", [P, 2, 4])
        dt = sb("dt", [HEADS, T])
        dt_abs = sb("dt_abs", [HEADS, T])
        log_decay = sb("log_decay", [HEADS, T])
        cum = sb("cum", [HEADS, T])
        xbc = [sb(f"xbc_{s}", [P, CONV_TILES, P]) for s in range(2)]
        gate = [sb(f"gate_{s}", [P, GATE_TILES, P]) for s in range(2)]
        dt_cum = sb("dt_cum", [HEADS, 2, P])
        by_row = sb("by_row", [P, 2, HEADS])
        to_end = sb("to_end", [P, HEADS])
        decay = sb("decay", [P, HEADS, P])
        from_start_of = [sb(f"from_start_{s}", [P, HEADS, P]) for s in range(2)]
        x_dt_of = [sb(f"x_dt_{s}", [P, HEADS, HD]) for s in range(2)]
        x_end_of = [sb(f"x_end_{s}", [P, HEADS, HD]) for s in range(2)]
        x_kept = [sb(f"x_kept_{s}", [P, GATE_TILES, P]) for s in range(2)]
        b_rows_of = [sb(f"b_rows_{s}", [P, GROUPS, STATE]) for s in range(2)]
        weights_of = [sb(f"weights_{s}", [P, HEADS, P]) for s in range(2)]
        c_start_of = [sb(f"c_start_{s}", [P, HEADS, P]) for s in range(2)]
        x_block = sb("x_block", [P, SEQS + 1, SSD_W])
        scores = sb("scores", [P, GROUPS, P])
        h_seq = sb("h_seq", [P, SEQS, SSD_W])
        h_next = sb("h_next", [P, 2, SSD_W])
        h = sb("h", [P, SSD_W])
        h_kept = sb("h_kept", [P, SSD_W])
        y = sb("y", [P, GATE_TILES, P])
        y_sq = sb("y_sq", [P, GATE_TILES, P])
        y_rms = sb("y_rms", [P, P])
        y_out = sb("y_out", [P, GATE_TILES, P])
        x_ps = psum("x_ps", HEADS, HD)
        b_ps = psum("b_ps", GROUPS, STATE)
        small_ps = psum("small_ps", 3, HEADS)
        rows_ps = psum("rows_ps", HEADS, P)
        scores_ps = psum("scores_ps", GROUPS, P)
        y_ps = psum("y_ps", GATE_TILES, P)
        h_ps = psum("h_ps", SSD_W)

        consts_loaded, par_loaded, dt_loaded = sem("ssd_consts_loaded"), sem("ssd_par_loaded"), sem("dt_loaded")
        seq_loaded = sem("h_seq_loaded")
        loaded = [sem(f"xbc_loaded_{s}") for s in range(2)]
        gate_loaded, kept_ready = [sem(f"gate_loaded_{s}") for s in range(2)], sem("x_kept_ready")
        ones_ready = sem("ssd_ones_ready")
        dt_step, dt_act = sem("dt_step"), sem("dt_act")
        fix_ready, small_done, by_row_ready, end_done = sem("fix_ready"), sem("small_done"), sem("by_row_ready"), sem("end_done")
        x_done, b_done, b_ready, rows_done = sem("x_rows_done"), sem("b_rows_done"), sem("b_rows_ready"), sem("rows_done")
        scores_done, start_ready, end_diff, end_ready = sem("scores_done"), sem("from_start_ready"), sem("end_diff"), sem("to_end_ready")
        seg_ready, decay_ready, xdt_ready, xend_ready = sem("seg_ready"), sem("decay_ready"), sem("x_dt_ready"), sem("x_end_ready")
        masked, c_ready, w_ready = sem("scores_masked"), sem("c_start_ready"), sem("weights_ready")
        y_done, h_done, h_step, h_ready = sem("y_done"), sem("h_done"), sem("h_step"), sem("h_ready")
        skip_done, gated, squared, var_done = sem("skip_done"), sem("gated"), sem("squared"), sem("var_done")
        mean_ready, root_ready, inv_ready, y_ready = sem("mean_ready"), sem("root_ready"), sem("inv_ready"), sem("ssd_y_ready")
        y_stored, h_stored = sem("ssd_y_stored"), [sem(f"h_stored_{s}") for s in range(2)]
        block_ready, seq_done, seq_step, seq_ready = sem("x_block_ready"), sem("seq_done"), sem("seq_step"), sem("seq_ready")
        var_ps = b_ps[:, 0, :]
        CONSTS = 6

        def of_head(buf, hh):
            return buf[:, hh * HD:hh * HD + HD]

        def y_rows(hh):
            lo = hh % 2 * HD
            return y_ps[lo:lo + HD, hh // 2, :]

        with nc.Block() as block:
            @block.sync
            def _(sp):
                sp.dma_start(dt[:], cols_d[IN_TILES - 1, 0:HEADS, :]).then_inc(dt_loaded, 16)
                sp.dma_start(dt_par[:], dt_par_d).then_inc(par_loaded, 16)
                sp.dma_start(keep[:], keep_d[0:HEADS, :]).then_inc(par_loaded, 16)
                sp.dma_start(eye[:], eye_d).then_inc(consts_loaded, 16)
                sp.dma_start(causal[:], causal_d.rearrange("a s t -> s a t")).then_inc(consts_loaded, 16)
                sp.dma_start(last_row[:], last_row_d.rearrange("a s t -> s a t")).then_inc(consts_loaded, 16)
                sp.dma_start(block_row[:], block_row_d).then_inc(consts_loaded, 16)
                sp.dma_start(head_row[:], head_row_d).then_inc(consts_loaded, 16)
                sp.dma_start(ssd_par[:], ssd_par_d).then_inc(consts_loaded, 16)

                def load(k, s, c):
                    sp.wait_ge(c_ready, START + c - 1)
                    sp.wait_ge(kept_ready, START + c - 1)
                    sp.dma_start(xbc[s][:], cols_d[0:CONV_TILES, :, tile_cols(c)].rearrange("m p t -> p m t")).then_inc(loaded[s], 16)
                    if is_tile(c, 0):
                        sp.dma_start(h_seq[:], state_d).then_inc(seq_loaded, 16)
                    sp.wait_ge(y_ready, START + c - 1)
                    sp.dma_start(gate[s][:], cols_d[IN_TILES - 1 - GATE_TILES:IN_TILES - 1, :, tile_cols(c)].rearrange("m p t -> p m t")).then_inc(gate_loaded[s], 16)

                over_chunks(sp, load, lambda *_: None)

            @block.gpsimd
            def _(pool):
                st.start(pool, *h_stored, y_stored)
                pool.memset(ones[:], 1.0).then_inc(ones_ready, 1)

                def store(k, s, c):
                    if is_tile(c, 0):
                        for b in range(SEQS):
                            pool.wait_ge(seq_ready, START + b + 1)
                            pool.dma_start(new_state_s[b], h_next[:, b % 2, :]).then_inc(h_stored[b % 2], 16)
                    pool.wait_ge(y_ready, START + c + 1)
                    if is_tile(c, 0):
                        pool.dma_start(y_d[0:GATE_TILES, :, 0:NS].rearrange("m p t -> p m t"), y_out[:, :, 0:NS]).then_inc(y_stored, 16)
                    else:
                        pool.dma_start(y_d[0:GATE_TILES, :, slice(c * P - NS, c * P - NS + P) if isinstance(c, int) else bass.ds(c * P - NS, P)].rearrange("m p t -> p m t"), y_out[:]).then_inc(y_stored, 16)

                over_chunks(pool, lambda *_: None, store)
                pool.wait_ge(h_ready, START + NT)
                pool.dma_start(new_state_p, h[:]).then_inc(h_stored[0], 16)
                pool.wait_ge(y_stored, 16 * NT)
                pool.wait_ge(h_stored[0], 16 * (SEQS // 2 + 1))
                pool.wait_ge(h_stored[1], 16 * (SEQS // 2))

            @block.scalar
            def _(act):
                act.wait_ge(par_loaded, START + 32)
                act.activation(dt_par[:, 1:2], dt_par[:, 1:2], ACT.Exp).then_inc(dt_act, 1)
                act.wait_ge(dt_step, START + 1)
                act.activation(dt_abs[:], dt[:], ACT.Abs).then_inc(dt_act, 1)
                act.wait_ge(dt_act, START + 2)
                act.activation(dt_abs[:], dt_abs[:], ACT.Exp, scale=-1.0).then_inc(dt_act, 1)
                act.wait_ge(dt_step, START + 2)
                act.activation(dt_abs[:], dt_abs[:], ACT.Ln).then_inc(dt_act, 1)

                def front(k, s, c):
                    first = is_tile(c, 0)
                    if first:
                        act.wait_ge(dt_step, START + 6)
                    else:
                        act.wait_ge(rows_done, START + c)
                    act.activation(dt_cum[:, 0, :], dt[:, tile_cols(c)], ACT.Copy)
                    act.activation(dt_cum[:, 1, :], cum[:, tile_cols(c)], ACT.Copy).then_inc(fix_ready, 1)
                    act.wait_ge(small_done, START + c + 1)
                    if not first:
                        act.wait_ge(seg_ready, START + c)
                        act.wait_ge(xdt_ready, START + c)
                        act.wait_ge(end_done, START + c)
                    act.activation(by_row[:], small_ps[:, 0:2, :], ACT.Copy).then_inc(by_row_ready, 1)
                    act.wait_ge(rows_done, START + c + 1)
                    act.wait_ge(h_ready, START + c - 1)
                    act.activation(from_start_of[s][:], rows_ps[:], ACT.Exp).then_inc(start_ready, 1)
                    act.wait_ge(end_diff, START + c + 1)
                    act.activation(to_end[:], to_end[:], ACT.Exp).then_inc(end_ready, 1)
                    act.wait_ge(b_done, START + c + 1)
                    act.wait_ge(h_done, START + c - 1)
                    act.activation(b_rows_of[s][:], b_ps[:], ACT.Copy).then_inc(b_ready, 1)
                    act.wait_ge(seg_ready, START + c + 1)
                    act.activation(decay[:], decay[:], ACT.Exp).then_inc(decay_ready, 1)
                    act.wait_ge(loaded[s], START + k * 16 + 16)
                    act.activation(x_kept[s][:], xbc[s][:, 0:GATE_TILES, :], ACT.Copy).then_inc(kept_ready, 1)

                def back(k, s, c):
                    act.wait_ge(gated, START + c + 1)
                    act.activation(y_sq[:], y[:], ACT.Square).then_inc(squared, 1)
                    act.wait_ge(mean_ready, START + c + 1)
                    act.activation(y_rms[:], y_rms[:], ACT.Sqrt).then_inc(root_ready, 1)

                over_chunks(act, front, back)

            @block.vector
            def _(dve):
                dve.wait_ge(dt_loaded, START + 16)
                dve.wait_ge(par_loaded, START + 32)
                dve.tensor_scalar(dt[:], dt[:], dt_par[:, 0:1], None, ALU.add).then_inc(dt_step, 1)
                dve.wait_ge(dt_act, START + 3)
                dve.tensor_scalar(dt_abs[:], dt_abs[:], 1.0, None, ALU.add).then_inc(dt_step, 1)
                dve.wait_ge(dt_act, START + 4)
                dve.scalar_tensor_tensor(out=dt[:], in0=dt[:], scalar=0.0, in1=dt_abs[:], op0=ALU.max, op1=ALU.add).then_inc(dt_step, 1)
                dve.wait_ge(dt_step, START + 3)
                dve.memset(dt[:, NS:P - META], 0.0).then_inc(dt_step, 1)
                dve.wait_ge(dt_step, START + 4)
                dve.tensor_scalar(log_decay[:], dt[:], dt_par[:, 1:2], -1.0, ALU.mult, ALU.mult).then_inc(dt_step, 1)
                dve.wait_ge(dt_step, START + 5)
                dve.tensor_tensor_scan(cum[:], keep[:], log_decay[:], 0.0, ALU.mult, ALU.add).then_inc(dt_step, 1)
                dve.wait_ge(consts_loaded, START + 16 * CONSTS)

                def front(k, s, c):
                    first = is_tile(c, 0)
                    which = 0 if first else 1
                    x_dt, x_end, from_start, c_start, weights = x_dt_of[s], x_end_of[s], from_start_of[s], c_start_of[s], weights_of[s]
                    dve.wait_ge(loaded[s], START + k * 16 + 16)
                    dve.wait_ge(by_row_ready, START + c + 1)
                    dve.wait_ge(end_done, START + c + 1)
                    dve.tensor_tensor(to_end[:], small_ps[:, 2, :], by_row[:, 1, :], ALU.subtract).then_inc(end_diff, 1)
                    dve.wait_ge(start_ready, START + c + 1)
                    for hh in range(HEADS):
                        last = dve.tensor_scalar(decay[:, hh, :], rows_ps[:, hh, :], by_row[:, 1, hh:hh + 1], 0.0,
                                                 ALU.subtract, ALU.min)
                    last.then_inc(seg_ready, 1)
                    dve.wait_ge(x_done, START + c + 1)
                    dve.wait_ge(y_done, START + c - 1)
                    dve.tensor_tensor(x_dt[:], x_ps[:], by_row[:, 0, :].unsqueeze(2).broadcast_to([P, HEADS, HD]), ALU.mult).then_inc(xdt_ready, 1)
                    dve.wait_ge(scores_done, START + c + 1)
                    dve.tensor_tensor(scores[:], scores_ps[:], causal[:, which:which + 1, :].broadcast_to([P, GROUPS, P]), ALU.mult).then_inc(masked, 1)
                    for g in range(GROUPS):
                        lo = g * PER_GROUP
                        last = dve.tensor_tensor(c_start[:, lo:lo + PER_GROUP, :], from_start[:, lo:lo + PER_GROUP, :],
                                                 xbc[s][:, 6 + g:7 + g, :].broadcast_to([P, PER_GROUP, P]), ALU.mult)
                    last.then_inc(c_ready, 1)
                    dve.wait_ge(decay_ready, START + c + 1)
                    dve.wait_ge(masked, START + c + 1)
                    for g in range(GROUPS):
                        lo = g * PER_GROUP
                        last = dve.tensor_tensor(weights[:, lo:lo + PER_GROUP, :], decay[:, lo:lo + PER_GROUP, :],
                                                 scores[:, g:g + 1, :].broadcast_to([P, PER_GROUP, P]), ALU.mult)
                    last.then_inc(w_ready, 1)
                    dve.wait_ge(end_ready, START + c + 1)
                    dve.wait_ge(xdt_ready, START + c + 1)
                    dve.wait_ge(h_done, START + c - 1)
                    dve.tensor_tensor(x_end[:], x_dt[:], to_end[:].unsqueeze(2).broadcast_to([P, HEADS, HD]), ALU.mult).then_inc(xend_ready, 1)
                    if first:
                        dve.wait_ge(xend_ready, START + 1)
                        xe = x_end[:].rearrange("p h d -> p (h d)")
                        for b in range(SEQS + 1):
                            last = dve.tensor_scalar(x_block[:, b, :], xe, block_row[:, b:b + 1], None, ALU.mult)
                        last.then_inc(block_ready, 1)

                def back(k, s, c):
                    first, from_start = is_tile(c, 0), from_start_of[s]
                    dve.wait_ge(kept_ready, START + c + 1)
                    dve.wait_ge(gate_loaded[s], START + k * 16 + 16)
                    dve.wait_ge(y_ready, START + c)
                    dve.wait_ge(y_done, START + c + 1)
                    for j in range(GATE_TILES):
                        last = dve.scalar_tensor_tensor(out=y[:, j, :], in0=x_kept[s][:, j, :], scalar=ssd_par[:, 0, j:j + 1],
                                                        in1=y_ps[:, j, :], op0=ALU.mult, op1=ALU.add)
                    last.then_inc(skip_done, 1)
                    dve.wait_ge(skip_done, START + c + 1)
                    dve.tensor_tensor(y[:], y[:], gate[s][:], ALU.mult).then_inc(gated, 1)
                    if first:
                        dve.wait_ge(start_ready, START + 1)
                        for b in range(SEQS):
                            kept = from_start[:, :, b * STEPS + STEPS - 1:b * STEPS + STEPS].broadcast_to([P, HEADS, HD])
                            dve.tensor_tensor(h_kept[:].rearrange("p (h d) -> p h d", h=HEADS),
                                              h_seq[:, b, :].rearrange("p (h d) -> p h d", h=HEADS), kept, ALU.mult).then_inc(seq_step, 1)
                            dve.wait_ge(seq_step, START + b + 1)
                            dve.wait_ge(seq_done, START + b + 1)
                            if b >= 2:
                                dve.wait_ge(h_stored[b % 2], 16 * (b // 2))
                            dve.tensor_tensor(h_next[:, b % 2, :], h_kept[:], h_ps[:], ALU.add).then_inc(seq_ready, 1)
                            dve.wait_ge(seq_ready, START + b + 1)
                        dve.wait_ge(h_done, START + 1)
                        dve.tensor_copy(h[:], h_ps[:]).then_inc(h_ready, 1)
                    else:
                        dve.wait_ge(h_done, START + c + 1)
                        kept = from_start[:, :, P - 1:P].broadcast_to([P, HEADS, HD])
                        dve.tensor_tensor(h_kept[:].rearrange("p (h d) -> p h d", h=HEADS),
                                          h[:].rearrange("p (h d) -> p h d", h=HEADS), kept, ALU.mult).then_inc(h_step, 1)
                        dve.wait_ge(h_step, START + c)
                        dve.tensor_tensor(h[:], h_kept[:], h_ps[:], ALU.add).then_inc(h_ready, 1)
                        dve.wait_ge(h_ready, START + c + 1)
                    dve.wait_ge(var_done, START + c + 1)
                    dve.tensor_scalar(y_rms[:], var_ps, 1.0 / SSD_W, RMS_EPS, ALU.mult, ALU.add).then_inc(mean_ready, 1)
                    dve.wait_ge(root_ready, START + c + 1)
                    dve.reciprocal(y_rms[:], y_rms[:]).then_inc(inv_ready, 1)
                    dve.wait_ge(inv_ready, START + c + 1)
                    if not first:
                        dve.wait_ge(y_stored, c * 16)
                    for j in range(GATE_TILES):
                        last = dve.scalar_tensor_tensor(out=y_out[:, j, :], in0=y[:, j, :], scalar=ssd_par[:, 1, j:j + 1],
                                                        in1=y_rms[:], op0=ALU.mult, op1=ALU.mult)
                    last.then_inc(y_ready, 1)

                over_chunks(dve, front, back)

            @block.tensor
            def _(pe):
                pe.wait_ge(consts_loaded, START + 16 * CONSTS)
                pe.wait_ge(ones_ready, START + 1)

                def front(k, s, c):
                    first = is_tile(c, 0)
                    which = 0 if first else 1
                    pe.wait_ge(fix_ready, START + c + 1)
                    if not first:
                        pe.wait_ge(end_diff, START + c)
                    for a in range(2):
                        mm = pe.matmul(small_ps[:, a, :], dt_cum[:, a, :], eye[0:HEADS, 0:HEADS], start=True, stop=True)
                    mm.then_inc(small_done, 1)
                    if not first:
                        pe.wait_ge(seg_ready, START + c)
                        pe.wait_ge(start_ready, START + c)
                    for hh in range(HEADS):
                        mm = pe.matmul(rows_ps[:, hh, :], head_row[:, hh, :], dt_cum[:, 1, :], start=True, stop=True)
                    mm.then_inc(rows_done, 1)
                    pe.wait_ge(by_row_ready, START + c + 1)
                    pe.matmul(small_ps[:, 2, :], last_row[:, which, :], by_row[:, 1, :], start=True, stop=True).then_inc(end_done, 1)
                    pe.wait_ge(loaded[s], START + k * 16 + 16)
                    if not first:
                        pe.wait_ge(xdt_ready, START + c)
                    for j in range(4):
                        mm = pe.transpose(x_ps[:, 2 * j:2 * j + 2, :].rearrange("p h d -> p (h d)"), xbc[s][:, j, :], eye[:])
                    mm.then_inc(x_done, 1)
                    pe.wait_ge(mean_ready, START + c - 1)
                    for g in range(GROUPS):
                        mm = pe.transpose(b_ps[:, g, :], xbc[s][:, 4 + g, :], eye[:])
                    mm.then_inc(b_done, 1)
                    if not first:
                        pe.wait_ge(masked, START + c)
                    for g in range(GROUPS):
                        mm = pe.matmul(scores_ps[:, g, :], xbc[s][:, 4 + g, :], xbc[s][:, 6 + g, :], start=True, stop=True)
                    mm.then_inc(scores_done, 1)

                def back(k, s, c):
                    first = is_tile(c, 0)
                    x_dt, x_end, c_start, weights, b_rows = x_dt_of[s], x_end_of[s], c_start_of[s], weights_of[s], b_rows_of[s]
                    pe.wait_ge(xdt_ready, START + c + 1)
                    pe.wait_ge(w_ready, START + c + 1)
                    pe.wait_ge(c_ready, START + c + 1)
                    if first:
                        pe.wait_ge(seq_loaded, START + 16)
                    else:
                        pe.wait_ge(skip_done, START + c)
                        pe.wait_ge(h_ready, START + c)
                    for hh in range(HEADS):
                        mm = pe.matmul(y_rows(hh), x_dt[:, hh, :], weights[:, hh, :], start=True, stop=False,
                                       skip_group_check=True)
                        if first:
                            for b in range(SEQS):
                                t = slice(b * STEPS, b * STEPS + STEPS)
                                mm = pe.matmul(y_rows(hh)[:, t], of_head(h_seq[:, b, :], hh), c_start[:, hh, t], start=False,
                                               stop=(b == SEQS - 1), skip_group_check=True)
                        else:
                            mm = pe.matmul(y_rows(hh), of_head(h, hh), c_start[:, hh, :], start=False, stop=True, skip_group_check=True)
                    mm.then_inc(y_done, 1)
                    pe.wait_ge(b_ready, START + c + 1)
                    half = SSD_W // GROUPS
                    if first:
                        pe.wait_ge(block_ready, START + 1)
                        for b in range(SEQS + 1):
                            if b >= 1:
                                pe.wait_ge(seq_ready, START + b)
                            for g in range(GROUPS):
                                mm = pe.matmul(h_ps[:, g * half:g * half + half], b_rows[:, g, :], x_block[:, b, g * half:g * half + half],
                                               start=True, stop=True)
                            mm.then_inc(seq_done if b < SEQS else h_done, 1)
                        pe.wait_ge(squared, START + 1)
                    else:
                        pe.wait_ge(xend_ready, START + c + 1)
                        for g in range(GROUPS):
                            mm = pe.matmul(h_ps[:, g * half:g * half + half], b_rows[:, g, :],
                                           x_end[:, g * PER_GROUP:g * PER_GROUP + PER_GROUP, :].rearrange("p h d -> p (h d)"),
                                           start=True, stop=True)
                    if not first:
                        mm.then_inc(h_done, 1)
                        pe.wait_ge(squared, START + c + 1)
                    pe.wait_ge(b_ready, START + NT if is_tile(c, NT - 1) else START + c + 2)
                    for j in range(GATE_TILES):
                        mm = pe.matmul(var_ps, ones[:], y_sq[:, j, :], start=(j == 0), stop=(j == GATE_TILES - 1))
                    mm.then_inc(var_done, 1)

                over_chunks(pe, front, back)


PAIRS = HEADS // 2
R0, K0, V0 = CONV_TILES, CONV_TILES + 4, CONV_TILES + 8
LORA0 = CONV_TILES + 12
GROUP_COUNT = 1 + (NT - 1) // 2
MERGES = LEVELS - 1
COEFS = 8
C_W0, C_A0, C_KK, C_KA, C_RK, C_LNW, C_LNB = range(7)
LOG_RATE = -float(np.exp(-0.5))


class Prepared:

    def __init__(self, sb, x):
        def rows(name):
            return sb(f"{name}_{x}", [P, T])

        self.r, self.v, self.kk, self.k_mod, self.b = rows("r"), rows("v"), rows("kk"), rows("k_mod"), rows("b")
        self.before_decay, self.in_decay, self.inv_decay = rows("before_decay"), rows("in_decay"), rows("inv_decay")
        self.bonus, self.gate = rows("bonus"), rows("gate")
        self.par = sb(f"pair_par_{x}", [P, 3 * P + COEFS])
        self.to_next = sb(f"to_next_{x}", [P, NT])

    def coef(self, i):
        return self.par[:, 3 * P + i:3 * P + i + 1]


PREP_PE = ("decay0", "decay1", "decay2", "rate0", "rate1", "rate2", "gate0", "gate1", "gate2", "norm0", "norm1", "norm2",
           "bonus0", "bonus1", "bonus2")
PREP_ACT = ("decay0", "decay1", "square", "decay2", "rate0", "rate1", "rate2", "gate0", "exp_inv", "gate1", "exp_in", "gate2",
            "exp_before", "exp_next", "exp_seq", "norm0", "norm1", "norm2")
PREP_DVE = ("kk_raw", "less_ka", "log_rate", "cum", "mid", "in_log", "before_log", "next_diff", "next_log", "k_scale", "k_mod",
            "clipped", "inverse0", "inverse1", "inverse2", "kk", "b", "weighted", "bonus0", "bonus1", "bonus2")
DECAY_AT, RATE_AT, GATE_AT, NORM_AT, INVERSE_AT, BONUS_AT = 0, 3, 6, 9, 13, 19
PREP_STEPS = (LEVELS - 1) * (GROUP_COUNT - 1)


def reached(made, j, name):
    return START + j * len(made) + made.index(name) + 1


def rwkv_heads(nc, cols_d, pair_par_d, state_d, eye_d, causal_d, before_d, level_d, level0_t_d, keep_d, block_row_d, head_pair_d,
               y_d, new_state_s, new_state_p):
    with Stage(nc, "rwkv") as st:
        sb, psum, sem = st.sb, st.psum, st.sem
        eye, head_pair = sb("eye", [P, P]), sb("head_pair", [P, P])
        masks = sb("masks", [P, 2, 2, P])
        level = sb("level", [P, 2, LEVELS, P])
        level0_t = sb("level0_t", [P, P])
        keep = sb("keep", [P, T])
        block_row = sb("block_row", [P, SEQS + 1])
        lora_in, gate_in = sb("lora_in", [P, T]), sb("gate_in", [P, T])
        prepared = [Prepared(sb, x) for x in range(2)]
        one_less_ka = sb("one_less_ka", [P, 1])
        k, cum, tmp, y_all = sb("k", [P, T]), sb("cum", [P, T]), sb("tmp", [P, T]), sb("y_all", [P, T])
        mid = sb("mid", [P, NT + 1])
        seq_end = sb("seq_end", [P, SEQS])
        s_seq = sb("s_seq", [P, SEQS, P])
        s_new = sb("s_new", [P, SEQS, P])
        s = sb("s", [P, P])
        queries_of = [sb(f"queries_{x}", [P, 2, 2, P]) for x in range(2)]
        keys = sb("keys", [P, 2, 2, P])
        v_fix = sb("v_fix", [P, 2, P])
        by_row_of = [sb(f"by_row_{x}", [P, 2, 3, P]) for x in range(2)]
        from_k_of = [sb(f"from_k_{x}", [P, 4, 2, P]) for x in range(2)]
        from_b_of = [sb(f"from_b_{x}", [P, 4, 2, P]) for x in range(2)]
        joins = sb("joins", [P, MERGES, 4, P])
        inv_t_of = [sb(f"inv_t_{x}", [P, 4, P]) for x in range(2)]
        inv, neg_x = sb("inv", [P, 4, P]), sb("neg_x", [P, 4, P])
        start_rows = sb("start_rows", [P, P])
        rhs, neg_u = sb("rhs", [P, P]), sb("neg_u", [P, P])
        v_block, u_block = sb("v_block", [P, SEQS + 1, P]), sb("u_block", [P, SEQS + 1, P])
        bank = [psum(f"bank_{i}", BANK) for i in range(8)]

        def quads(i):
            return bank[i].rearrange("p (m t) -> p m t", m=4)

        def halves(i):
            return bank[i][:, 0:4 * HD].rearrange("p (m t) -> p m t", m=4)

        masks_loaded = sem("rw_masks_loaded")
        consts_loaded, lora_loaded, loaded, zeroed, lora_ready = sem("rw_consts_loaded"), sem("lora_loaded"), sem("rw_loaded"), sem("rw_zeroed"), sem("lora_ready")
        prep_pe, prep_act, prep_vec = sem("prep_pe"), sem("prep_act"), sem("prep_vec")
        qk_ready, v_ready, turned, by_row_ready = sem("qk_ready"), sem("v_ready"), sem("turned"), sem("rw_by_row_ready")
        l_done, fk_done, fb_done = sem("l_done"), sem("from_k_done"), sem("from_b_done")
        inv_step, inv_ready, fk_ready, fb_ready = sem("inv_step"), sem("inv_start_ready"), sem("from_k_ready"), sem("from_b_ready")
        joins_ready, x_done, x_ready, z_done, merged = sem("joins_ready"), sem("x_done"), sem("x_ready"), sem("z_done"), sem("merged")
        start_done, start_ready = sem("start_rows_done"), sem("start_rows_ready")
        rhs_done, rhs_ready, u_done, u_ready = sem("rhs_done"), sem("rhs_ready"), sem("u_done"), sem("u_ready")
        y_done, y_ready, s_done, s_ready = sem("y_done"), sem("y_ready"), sem("s_done"), sem("s_ready")
        blocks_ready, seq_ready = sem("blocks_ready"), sem("rw_seq_ready")
        ep_pe, ep_vec, ep_act = sem("ep_pe"), sem("ep_vec"), sem("ep_act")
        out_stored, seq_stored = sem("rw_out_stored"), sem("rw_seq_stored")
        CONSTS, MASKS = 2, 6
        LOADS = 6
        EP_VEC = 7

        class Group:

            def __init__(self, j, x, g):
                self.j, self.x, self.g, self.slot, self.pre = j, x, g, g % 2, prepared[x]
                self.n = 1 if g == 0 else 2
                self.c = 0 if g == 0 else 2 * g - 1
                self.gi, self.ci = j * GROUP_COUNT + g, j * NT + self.c
                self.ended = j * NT + (0, 1, 1, 3, 5)[g]

        def over_groups(eng, prepare, before, start, within, chain, after):
            for step in range(PREP_STEPS):
                prepare(step, 0, prepared[0])
            with eng.Fori(0, PAIRS // 2) as q:
                for x in range(2):
                    j = q * 2 + x
                    before(j, x)
                    groups = [Group(j, x, g) for g in range(GROUP_COUNT)]
                    for g, group in enumerate(groups):
                        start(group)
                        within(group, groups[g - 1] if g >= 2 else None)
                        if g == 0 or g == GROUP_COUNT - 1:
                            chain(group)
                    after(j, x)

        def prepare_next(prepare, group, l):
            if group.g >= 1:
                prepare((group.g - 1) * MERGES + l - 1, group.j + 1, prepared[1 - group.x])

        RHS_AT, U_AT, Y_AT = (1, 4), (2.5, 5.5), (3, 6)

        def group_cols(buf, c, n):
            cols = buf[:, c * P:(c + n) * P]
            return cols.rearrange("p (a t) -> p a t", a=n)

        def thirds(buf, c):
            return buf[:, c * CH:c * CH + CH]

        def half_cols(buf, l, which):
            return buf.rearrange("p m (a h w) -> p m a h w", h=2, w=1 << l)[:, :, :, which, :]

        with nc.Block() as block:
            @block.sync
            def _(sp):
                sp.dma_start(lora_in[:], cols_d[LORA0]).then_inc(lora_loaded, 16)
                sp.dma_start(gate_in[:], cols_d[LORA0 + 1]).then_inc(lora_loaded, 16)
                sp.dma_start(keep[:], keep_d).then_inc(consts_loaded, 16)
                sp.dma_start(head_pair[:], head_pair_d).then_inc(consts_loaded, 16)
                sp.wait_ge(zeroed, START + 1)

                def load(j, x):
                    pre = prepared[x]
                    for dst, first in ((k, K0), (pre.r, R0), (pre.v, V0)):
                        sp.dma_start(dst[:], cols_d[bass.ds(j + first, 1)].rearrange("a p t -> (a p) t")).then_inc(loaded, 16)
                    sp.dma_start(pre.par[:], pair_par_d[bass.ds(j, 1)].rearrange("a p t -> (a p) t")).then_inc(loaded, 16)
                    for h in range(2):
                        half = slice(h * HD, h * HD + HD)
                        sp.dma_start(s_seq[half, :, half], state_d[bass.ds(j, 1), half, :, :].rearrange("a k b v -> (a k) b v")).then_inc(loaded, 16)

                load(0, 0)
                sp.dma_start(eye[:], eye_d).then_inc(masks_loaded, 16)
                sp.dma_start(masks[:, :, 0, :], before_d.rearrange("a s t -> s a t")).then_inc(masks_loaded, 16)
                sp.dma_start(masks[:, :, 1, :], causal_d.rearrange("a s t -> s a t")).then_inc(masks_loaded, 16)
                sp.dma_start(level[:], level_d.rearrange("a l s t -> s a l t")).then_inc(masks_loaded, 16)
                sp.dma_start(level0_t[:], level0_t_d).then_inc(masks_loaded, 16)
                sp.dma_start(block_row[:], block_row_d).then_inc(masks_loaded, 16)
                with sp.Fori(0, PAIRS // 2) as q:
                    for x in range(2):
                        j = q * 2 + x
                        sp.wait_ge(ep_vec, START + j * EP_VEC)
                        sp.wait_ge(prep_vec, reached(PREP_DVE, j, "k_mod"))
                        sp.wait_ge(s_done, START + j * NT + 1)
                        load(j + 1, 1 - x)

            @block.gpsimd
            def _(pool):
                st.start(pool, out_stored, seq_stored)
                pool.memset(s_seq[:], 0.0)
                pool.memset(start_rows[:], 0.0)
                pool.memset(mid[:], 0.0).then_inc(zeroed, 1)
                pool.wait_ge(masks_loaded, START + 16 * MASKS)

                def start(group):
                    which, m, from_b = 0 if group.n == 1 else 1, 2 * group.n, from_b_of[group.slot]
                    pool.wait_ge(fb_ready, START + group.gi + 1)
                    pool.wait_ge(z_done, START + group.gi * MERGES)
                    for l in range(1, LEVELS):
                        pool.tensor_tensor(joins[:, l - 1, 0:m, :], from_b[:, 0:m, 0, :],
                                           level[:, which, l:l + 1, :].broadcast_to([P, m, P]), ALU.mult).then_inc(joins_ready, 1)

                def chain(group):
                    if group.g == 0:
                        j = group.j
                        pool.wait_ge(seq_ready, START + j + 1)
                        for h in range(2):
                            half = slice(h * HD, h * HD + HD)
                            pool.dma_start(new_state_s[bass.ds(j, 1), half, :, :].rearrange("a k b v -> (a k) b v"), s_new[half, :, half]).then_inc(seq_stored, 16)

                def after(j, x):
                    pool.wait_ge(ep_vec, START + j * EP_VEC + EP_VEC)
                    out = y_d[bass.ds(j + GATE_TILES, 1)].rearrange("a p t -> (a p) t")
                    pool.dma_start(out[:, 0:NS], y_all[:, 0:NS]).then_inc(out_stored, 16)
                    pool.dma_start(out[:, NS:KEPT], y_all[:, P:T]).then_inc(out_stored, 16)
                    for h in range(2):
                        half = slice(h * HD, h * HD + HD)
                        pool.dma_start(new_state_p[bass.ds(j, 1), half, :].rearrange("a k v -> (a k) v"), s[half, half]).then_inc(out_stored, 16)
                    pool.wait_ge(out_stored, j * 64 + 64)
                    pool.wait_ge(seq_stored, j * 32 + 32)

                nothing = lambda *_: None
                over_groups(pool, nothing, nothing, start, nothing, chain, after)

            @block.scalar
            def _(act):
                act.wait_ge(lora_loaded, START + 32)
                act.activation(lora_in[0:HD, :], lora_in[0:HD, :], ACT.Tanh)
                act.activation(gate_in[:], gate_in[:], ACT.Sigmoid).then_inc(lora_ready, 1)

                def third(j, name, c, out, func, **more):
                    act.wait_ge(prep_pe, reached(PREP_PE, j, f"{name}{c}"))
                    act.activation(thirds(out, c), bank[7][:, 0:CH], func, **more).then_inc(prep_act, 1)

                def prepare(step, j, pre):
                    if step == 0:
                        act.wait_ge(loaded, START + j * 16 * LOADS + 16 * LOADS)
                    if DECAY_AT <= step < DECAY_AT + 3:
                        third(j, "decay", step - DECAY_AT, pre.before_decay, ACT.Sigmoid, bias=pre.coef(C_W0))
                    if step == 1:
                        act.wait_ge(prep_vec, reached(PREP_DVE, j, "kk_raw"))
                        act.activation(tmp[:], pre.kk[:], ACT.Square).then_inc(prep_act, 1)
                    if RATE_AT <= step < RATE_AT + 3:
                        third(j, "rate", step - RATE_AT, pre.b, ACT.Sigmoid, bias=pre.coef(C_A0))
                    if GATE_AT <= step < GATE_AT + 3:
                        third(j, "gate", step - GATE_AT, pre.gate, ACT.Copy)
                    if step == 6:
                        act.wait_ge(prep_vec, reached(PREP_DVE, j, "in_log"))
                        act.activation(pre.inv_decay[:], pre.in_decay[:], ACT.Exp, scale=-1.0).then_inc(prep_act, 1)
                    if step == 7:
                        act.wait_ge(prep_vec, reached(PREP_DVE, j, "next_diff"))
                        act.wait_ge(prep_act, reached(PREP_ACT, j, "exp_inv"))
                        act.activation(pre.in_decay[:], pre.in_decay[:], ACT.Exp).then_inc(prep_act, 1)
                    if step == 8:
                        act.activation(pre.before_decay[:], pre.before_decay[:], ACT.Exp).then_inc(prep_act, 1)
                    if step == 9:
                        act.wait_ge(prep_vec, reached(PREP_DVE, j, "next_log"))
                        act.activation(pre.to_next[:], pre.to_next[:], ACT.Exp).then_inc(prep_act, 1)
                        act.activation(seq_end[:], cum[:, 0:NS].rearrange("p (b w) -> p b w", b=SEQS)[:, :, STEPS - 1], ACT.Exp).then_inc(prep_act, 1)
                    if NORM_AT <= step < NORM_AT + 3:
                        third(j, "norm", step - NORM_AT, tmp, ACT.Sqrt)

                def start(group):
                    gi, n, by_row = group.gi, group.n, by_row_of[group.slot]
                    act.wait_ge(turned, START + gi)
                    act.activation(v_fix[:, 0:n, :], group_cols(group.pre.v, group.c, n), ACT.Copy).then_inc(v_ready, 1)
                    act.wait_ge(s_done, START + group.ended)
                    act.wait_ge(turned, START + gi + 1)
                    for a in range(n):
                        out = act.activation(by_row[:, a, :, :], bank[a][:, 0:3 * P].rearrange("p (a t) -> p a t", a=3), ACT.Copy)
                    out.then_inc(by_row_ready, 1)
                    if n == 1:
                        act.wait_ge(start_done, START + group.j + 1)
                        act.activation(start_rows[:, 0:NS], bank[7][:, 0:NS], ACT.Copy).then_inc(start_ready, 1)

                def copy_rhs(i):
                    act.wait_ge(rhs_done, START + i + 1)
                    act.activation(rhs[:], bank[3][:, 0:P], ACT.Copy).then_inc(rhs_ready, 1)

                def copy_u(i):
                    act.wait_ge(u_done, START + i + 1)
                    act.activation(neg_u[:], bank[4][:, 0:P], ACT.Copy, scale=-1.0).then_inc(u_ready, 1)

                def copy_y(i, c):
                    act.wait_ge(y_done, START + i + 1)
                    act.activation(y_all[:, c * P:c * P + P], bank[5][:, 0:P], ACT.Copy).then_inc(y_ready, 1)

                def within(group, chained):
                    for l in range(1, LEVELS):
                        act.wait_ge(x_done, START + group.gi * MERGES + l)
                        act.activation(neg_x[:, 0:2 * group.n, :], quads(0)[:, 0:2 * group.n, :], ACT.Copy, scale=-1.0).then_inc(x_ready, 1)
                        if chained:
                            for a in range(2):
                                i = chained.ci + a
                                if l == RHS_AT[a]:
                                    copy_rhs(i)
                                if l == U_AT[a] + 0.5:
                                    copy_u(i)
                                if l == Y_AT[a]:
                                    copy_y(i, chained.c + a)
                        prepare_next(prepare, group, l)

                def chain(group):
                    for a in range(group.n):
                        i = group.ci + a
                        copy_rhs(i)
                        copy_u(i)
                        copy_y(i, group.c + a)

                def after(j, x):
                    inv_decay = prepared[x].inv_decay
                    act.wait_ge(ep_vec, START + j * EP_VEC + 1)
                    act.activation(cum[:], tmp[:], ACT.Square).then_inc(ep_act, 1)
                    act.wait_ge(ep_vec, START + j * EP_VEC + 2)
                    act.activation(inv_decay[:], inv_decay[:], ACT.Sqrt).then_inc(ep_act, 1)

                over_groups(act, prepare, lambda *_: None, start, within, chain, after)

            @block.vector
            def _(dve):
                dve.wait_ge(consts_loaded, START + 16 * CONSTS)
                dve.wait_ge(zeroed, START + 1)

                def own(j, name):
                    dve.wait_ge(prep_vec, reached(PREP_DVE, j, name))

                def from_act(j, name):
                    dve.wait_ge(prep_act, reached(PREP_ACT, j, name))

                by_tile = cum[:].rearrange("p (c t) -> p c t", c=NT)

                def prepare(step, j, pre):
                    if step == 0:
                        dve.wait_ge(loaded, START + j * 16 * LOADS + 16 * LOADS)
                        dve.tensor_scalar(pre.kk[:], k[:], pre.coef(C_KK), None, ALU.mult).then_inc(prep_vec, 1)
                        dve.tensor_scalar(one_less_ka[:], pre.coef(C_KA), -1.0, 1.0, ALU.mult, ALU.add).then_inc(prep_vec, 1)
                    if step == 3:
                        from_act(j, "decay2")
                        dve.tensor_scalar(pre.before_decay[:], pre.before_decay[:], LOG_RATE, None, ALU.mult).then_inc(prep_vec, 1)
                    if step == 4:
                        own(j, "log_rate")
                        dve.tensor_tensor_scan(cum[:], keep[:], pre.before_decay[:], 0.0, ALU.mult, ALU.add).then_inc(prep_vec, 1)
                    if step == 5:
                        own(j, "cum")
                        dve.tensor_copy(mid[:, 1:NT], by_tile[:, 1:NT, P // 2 - 1]).then_inc(prep_vec, 1)
                        own(j, "mid")
                        dve.tensor_tensor(pre.in_decay[:].rearrange("p (c t) -> p c t", c=NT), by_tile,
                                          mid[:, 0:NT].unsqueeze(2).broadcast_to([P, NT, P]), ALU.subtract).then_inc(prep_vec, 1)
                    if step == 6:
                        own(j, "in_log")
                        dve.tensor_tensor(pre.before_decay[:], pre.in_decay[:], pre.before_decay[:], ALU.subtract).then_inc(prep_vec, 1)
                        dve.tensor_tensor(pre.to_next[:], by_tile[:, :, P - 1], mid[:, 0:NT], ALU.subtract).then_inc(prep_vec, 1)
                    if step == 7:
                        own(j, "next_diff")
                        dve.tensor_tensor(pre.to_next[:], pre.to_next[:], mid[:, 1:NT + 1], ALU.add).then_inc(prep_vec, 1)
                        from_act(j, "rate2")
                        dve.tensor_scalar(pre.k_mod[:], pre.b[:], pre.coef(C_KA), one_less_ka[:], ALU.mult, ALU.add).then_inc(prep_vec, 1)
                    if step == 8:
                        own(j, "k_scale")
                        dve.tensor_tensor(pre.k_mod[:], pre.k_mod[:], k[:], ALU.mult).then_inc(prep_vec, 1)
                    if step == 12:
                        from_act(j, "norm2")
                        dve.tensor_scalar(tmp[:], tmp[:], 1e-12, None, ALU.max).then_inc(prep_vec, 1)
                    if INVERSE_AT <= step < INVERSE_AT + 3:
                        own(j, "clipped")
                        inverse = thirds(tmp, step - INVERSE_AT)
                        dve.reciprocal(inverse, inverse).then_inc(prep_vec, 1)
                    if step == 16:
                        own(j, "inverse2")
                        dve.tensor_tensor(pre.kk[:], pre.kk[:], tmp[:], ALU.mult).then_inc(prep_vec, 1)
                    if step == 17:
                        own(j, "kk")
                        dve.tensor_tensor(pre.b[:], pre.kk[:], pre.b[:], ALU.mult).then_inc(prep_vec, 1)
                    if step == 18:
                        dve.scalar_tensor_tensor(out=tmp[:], in0=pre.r[:], scalar=pre.coef(C_RK), in1=pre.k_mod[:],
                                                 op0=ALU.mult, op1=ALU.mult).then_inc(prep_vec, 1)
                    if BONUS_AT <= step < BONUS_AT + 3:
                        c = step - BONUS_AT
                        dve.wait_ge(prep_pe, reached(PREP_PE, j, f"bonus{c}"))
                        dve.tensor_tensor(thirds(pre.bonus, c), bank[7][:, 0:CH], thirds(pre.v, c), ALU.mult).then_inc(prep_vec, 1)

                def before(j, x):
                    dve.wait_ge(masks_loaded, START + 16 * MASKS)
                    own(j, "bonus2")
                    from_act(j, "norm2")

                def start(group):
                    gi, c, n, slot, pre = group.gi, group.c, group.n, group.slot, group.pre
                    which, m = 0 if n == 1 else 1, 2 * n
                    queries, from_k, from_b, inv_t = queries_of[slot], from_k_of[slot], from_b_of[slot], inv_t_of[slot]
                    dve.wait_ge(fk_done, START + gi)
                    dve.tensor_tensor(keys[:, 0:n, 0, :], group_cols(pre.k_mod, c, n), group_cols(pre.inv_decay, c, n), ALU.mult)
                    dve.tensor_tensor(keys[:, 0:n, 1, :], group_cols(pre.b, c, n), group_cols(pre.inv_decay, c, n), ALU.mult)
                    dve.wait_ge(s_done, START + group.ended)
                    dve.tensor_tensor(queries[:, 0:n, 0, :], group_cols(pre.kk, c, n), group_cols(pre.before_decay, c, n), ALU.mult)
                    dve.tensor_tensor(queries[:, 0:n, 1, :], group_cols(pre.r, c, n), group_cols(pre.in_decay, c, n), ALU.mult).then_inc(qk_ready, 1)
                    pair_masks = masks[:, which, :, :]
                    dve.wait_ge(fb_done, START + gi + 1)
                    for i in range(m):
                        last = dve.tensor_tensor(from_b[:, i, :, :], bank[5 + i % 2][:, i // 2 * 2 * P:(i // 2 + 1) * 2 * P].rearrange("p (a t) -> p a t", a=2), pair_masks, ALU.mult)
                    last.then_inc(fb_ready, 1)
                    dve.wait_ge(l_done, START + gi + 1)
                    for h in range(2):
                        last = dve.tensor_tensor(inv[:].rearrange("p (a h) t -> p a h t", h=2)[:, 0:n, h, :],
                                                 bank[(2, 7)[h]][:, 0:n * P].rearrange("p (a t) -> p a t", a=n),
                                                 level0_t[:].unsqueeze(1).broadcast_to([P, n, P]), ALU.mult)
                    last.then_inc(inv_step, 1)
                    dve.wait_ge(fb_ready, START + gi + 1)
                    dve.tensor_tensor(inv_t[:, 0:m, :], from_b[:, 0:m, 0, :], level[:, 1, 0:1, :].broadcast_to([P, m, P]), ALU.mult).then_inc(inv_step, 1)
                    dve.wait_ge(inv_step, START + gi * 2 + 2)
                    eyes = eye[:].unsqueeze(1).broadcast_to([P, m, P])
                    dve.tensor_tensor(inv[:, 0:m, :], eyes, inv[:, 0:m, :], ALU.subtract)
                    dve.tensor_tensor(inv_t[:, 0:m, :], eyes, inv_t[:, 0:m, :], ALU.subtract).then_inc(inv_ready, 1)
                    dve.wait_ge(fk_done, START + gi + 1)
                    for i in range(m):
                        last = dve.tensor_tensor(from_k[:, i, :, :], bank[3 + i % 2][:, i // 2 * 2 * P:(i // 2 + 1) * 2 * P].rearrange("p (a t) -> p a t", a=2), pair_masks, ALU.mult)
                    last.then_inc(fk_ready, 1)
                    dve.wait_ge(inv_ready, START + gi + 1)

                def next_state(i, c, to_next):
                    dve.wait_ge(s_done, START + i + 1)
                    dve.scalar_tensor_tensor(out=s[:], in0=bank[6][:, 0:P], scalar=to_next[:, c:c + 1],
                                             in1=head_pair[:], op0=ALU.mult, op1=ALU.mult).then_inc(s_ready, 1)

                def within(group, chained):
                    m, inv_t = 2 * group.n, inv_t_of[group.slot]
                    for l in range(1, LEVELS):
                        dve.wait_ge(z_done, START + group.gi * MERGES + l)
                        if l < LEVELS - 1:
                            t = half_cols(inv[:, 0:m, :], l, 0)
                            dve.tensor_tensor(t, t, half_view(1, m, l), ALU.add)
                        t = half_cols(inv_t[:, 0:m, :], l, 1)
                        dve.tensor_tensor(t, t, half_view(2, m, l), ALU.add).then_inc(merged, 1)
                        dve.wait_ge(merged, START + group.gi * MERGES + l)
                        if chained and l in Y_AT:
                            a = Y_AT.index(l)
                            next_state(chained.ci + a, chained.c + a, chained.pre.to_next)
                        prepare_next(prepare, group, l)

                def chain(group):
                    by_row = by_row_of[group.slot]
                    if group.g == 0:
                        dve.wait_ge(by_row_ready, START + group.gi + 1)
                        dve.wait_ge(u_ready, START + group.ci + 1)
                        for bb in range(SEQS + 1):
                            dve.tensor_scalar(v_block[:, bb, :], by_row[:, 0, 2, :], block_row[:, bb:bb + 1], None, ALU.mult)
                            last = dve.tensor_scalar(u_block[:, bb, :], neg_u[:], block_row[:, bb:bb + 1], None, ALU.mult)
                        last.then_inc(blocks_ready, 1)
                        dve.wait_ge(s_done, START + group.ci + 1)
                        for bb in range(SEQS):
                            last = dve.scalar_tensor_tensor(out=s_new[:, bb, :], in0=bank[bb // 3][:, bb % 3 * P:bb % 3 * P + P],
                                                            scalar=seq_end[:, bb:bb + 1], in1=head_pair[:], op0=ALU.mult, op1=ALU.mult)
                        last.then_inc(seq_ready, 1)
                        dve.scalar_tensor_tensor(out=s[:], in0=bank[2][:, 2 * P:3 * P], scalar=group.pre.to_next[:, 0:1],
                                                 in1=head_pair[:], op0=ALU.mult, op1=ALU.mult).then_inc(s_ready, 1)
                    else:
                        for a in range(group.n):
                            next_state(group.ci + a, group.c + a, group.pre.to_next)

                def half_view(i, m, l):
                    return halves(i)[:, 0:m, :].rearrange("p m (a w) -> p m a w", w=1 << l)

                def after(j, x):
                    e0, pre = j * EP_VEC, prepared[x]
                    inv_decay = pre.inv_decay
                    dve.wait_ge(ep_pe, START + j * 2 + 1)
                    for c in range(3):
                        last = dve.scalar_tensor_tensor(out=thirds(tmp, c), in0=bank[c][:, 0:CH], scalar=-1.0 / HD,
                                                        in1=thirds(y_all, c), op0=ALU.mult, op1=ALU.add)
                    last.then_inc(ep_vec, 1)
                    dve.wait_ge(ep_pe, START + j * 2 + 2)
                    for c in range(3):
                        last = dve.tensor_scalar(thirds(inv_decay, c), bank[3 + c][:, 0:CH], 1.0 / HD, GN_EPS, ALU.mult, ALU.add)
                    last.then_inc(ep_vec, 1)
                    dve.wait_ge(ep_act, START + j * 2 + 2)
                    dve.reciprocal(inv_decay[:], inv_decay[:]).then_inc(ep_vec, 1)
                    dve.wait_ge(ep_vec, START + e0 + 3)
                    dve.tensor_tensor(tmp[:], tmp[:], inv_decay[:], ALU.mult).then_inc(ep_vec, 1)
                    dve.wait_ge(ep_vec, START + e0 + 4)
                    dve.tensor_scalar(tmp[:], tmp[:], pre.coef(C_LNW), pre.coef(C_LNB), ALU.mult, ALU.add).then_inc(ep_vec, 1)
                    dve.wait_ge(ep_vec, START + e0 + 5)
                    dve.tensor_tensor(tmp[:], tmp[:], pre.bonus[:], ALU.add).then_inc(ep_vec, 1)
                    dve.wait_ge(ep_vec, START + e0 + 6)
                    dve.tensor_tensor(y_all[:], tmp[:], pre.gate[:], ALU.mult).then_inc(ep_vec, 1)

                over_groups(dve, prepare, before, start, within, chain, after)

            @block.tensor
            def _(pe):
                pe.wait_ge(consts_loaded, START + 16 * CONSTS)
                pe.wait_ge(lora_ready, START + 1)
                pe.wait_ge(zeroed, START + 1)

                def head_sums(src, first_bank, done):
                    for c in range(3):
                        mm = pe.matmul(bank[first_bank + c][:, 0:CH], head_pair[:], thirds(src, c), start=True, stop=True)
                    mm.then_inc(done, 1)

                def third(j, name, c, weights, src):
                    place = PREP_PE.index(f"{name}{c}")
                    if place > 0:
                        last = PREP_PE[place - 1]
                        if last in PREP_ACT:
                            pe.wait_ge(prep_act, reached(PREP_ACT, j, last))
                        else:
                            pe.wait_ge(prep_vec, reached(PREP_DVE, j, last))
                    pe.matmul(bank[7][:, 0:CH], weights, thirds(src, c), start=True, stop=True).then_inc(prep_pe, 1)

                def prepare(step, j, pre):
                    if step == 0:
                        pe.wait_ge(loaded, START + j * 16 * LOADS + 16 * LOADS)
                    if DECAY_AT <= step < DECAY_AT + 3:
                        third(j, "decay", step - DECAY_AT, pre.par[:, 0:P], lora_in)
                    if RATE_AT <= step < RATE_AT + 3:
                        third(j, "rate", step - RATE_AT, pre.par[:, P:2 * P], lora_in)
                    if GATE_AT <= step < GATE_AT + 3:
                        third(j, "gate", step - GATE_AT, pre.par[:, 2 * P:3 * P], gate_in)
                    if NORM_AT <= step < NORM_AT + 3:
                        pe.wait_ge(prep_act, reached(PREP_ACT, j, "square"))
                        third(j, "norm", step - NORM_AT, head_pair[:], tmp)
                    if BONUS_AT <= step < BONUS_AT + 3:
                        pe.wait_ge(prep_vec, reached(PREP_DVE, j, "weighted"))
                        third(j, "bonus", step - BONUS_AT, head_pair[:], tmp)

                def start(group):
                    gi, n, slot = group.gi, group.n, group.slot
                    m, queries = 2 * n, queries_of[slot]
                    pe.wait_ge(qk_ready, START + gi + 1)
                    pe.wait_ge(v_ready, START + gi + 1)
                    pe.wait_ge(merged, START + gi * MERGES)
                    pe.wait_ge(s_ready, START + group.ended)
                    pe.wait_ge(y_ready, START + group.ended)
                    if group.g == 0:
                        pe.wait_ge(prep_vec, reached(PREP_DVE, group.j, "bonus2"))
                    if group.g == 2:
                        pe.wait_ge(prep_act, reached(PREP_ACT, group.j + 1, "rate2"))
                    if group.g == 3:
                        pe.wait_ge(prep_act, reached(PREP_ACT, group.j + 1, "norm2"))
                    for a in range(n):
                        for i, src in enumerate((keys[:, a, 0, :], keys[:, a, 1, :], v_fix[:, a, :])):
                            mm = pe.transpose(bank[a][:, i * P:i * P + P], src, eye[:])
                    mm.then_inc(turned, 1)

                    def head(buf, i):
                        lo = i % 2 * HD
                        return buf[lo:lo + HD, i // 2]

                    for which, first_bank, done in ((1, 5, fb_done), (0, 3, fk_done)):
                        for i in range(m):
                            mm = pe.matmul(bank[first_bank + i % 2][:, i // 2 * 2 * P:(i // 2 + 1) * 2 * P], head(keys, i)[:, which, :],
                                           head(queries, i).rearrange("p a t -> p (a t)"), start=True, stop=True)
                        mm.then_inc(done, 1)
                        if which == 1:
                            for i in range(m):
                                mm = pe.matmul(bank[(2, 7)[i % 2]][:, i // 2 * P:i // 2 * P + P], head(queries, i)[:, 0, :], head(keys, i)[:, 1, :], start=True, stop=True)
                            mm.then_inc(l_done, 1)
                    if n == 1:
                        pe.wait_ge(inv_ready, START + gi + 1)
                        for bb in range(SEQS):
                            t = slice(bb * STEPS, bb * STEPS + STEPS)
                            mm = pe.matmul(bank[7][:, t], s_seq[:, bb, :], queries[:, 0, 0, t], start=True, stop=True)
                        mm.then_inc(start_done, 1)
                    pe.wait_ge(by_row_ready, START + gi + 1)

                def within(group, chained):
                    m, inv_t = 2 * group.n, inv_t_of[group.slot]

                    def chain_steps(point):
                        for a in range(2 if chained else 0):
                            for times, step in ((RHS_AT, make_rhs), (U_AT, make_u), (Y_AT, make_y)):
                                if times[a] == point:
                                    step(chained, a)

                    for l in range(1, LEVELS):
                        k0 = group.gi * MERGES + l
                        pe.wait_ge(joins_ready, START + k0)
                        if l == 1:
                            pe.wait_ge(inv_ready, START + group.gi + 1)
                        else:
                            pe.wait_ge(merged, START + k0 - 1)
                        for i in range(m):
                            mm = pe.matmul(quads(0)[:, i, :], joins[:, l - 1, i, :], inv[:, i, :], start=True, stop=True)
                        mm.then_inc(x_done, 1)
                        chain_steps(l - 0.5)
                        pe.wait_ge(x_ready, START + k0)
                        if l < LEVELS - 1:
                            for i in range(m):
                                pe.matmul(halves(1)[:, i, :], inv_t[:, i, :], half_cols(neg_x[:, i:i + 1, :], l, 0)[:, 0], start=True, stop=True)
                        for i in range(m):
                            mm = pe.matmul(halves(2)[:, i, :], neg_x[:, i, :], half_cols(inv_t[:, i:i + 1, :], l, 1)[:, 0], start=True, stop=True)
                        mm.then_inc(z_done, 1)
                        if l == 1:
                            pe.wait_ge(fk_ready, START + group.gi + 1)
                        chain_steps(l)
                        prepare_next(prepare, group, l)

                heads = (0, 1)

                def cols(h):
                    return slice(h * HD, h * HD + HD)

                def make_rhs(group, a):
                    i, slot = group.ci + a, group.slot
                    pe.wait_ge(s_ready, START + i)
                    if group.g == 0:
                        pe.wait_ge(start_ready, START + group.j + 1)
                        pe.matmul(bank[3][:, 0:P], start_rows[:], eye[:], start=True, stop=False, skip_group_check=True)
                    else:
                        pe.matmul(bank[3][:, 0:P], queries_of[slot][:, a, 0, :], s[:], start=True, stop=False, skip_group_check=True)
                    for h in heads:
                        mm = pe.matmul(bank[3][:, cols(h)], from_k_of[slot][:, 2 * a + h, 0, :], by_row_of[slot][:, a, 2, cols(h)], start=False, stop=True,
                                       skip_group_check=True)
                    mm.then_inc(rhs_done, 1)

                def make_u(group, a):
                    i = group.ci + a
                    pe.wait_ge(rhs_ready, START + i + 1)
                    for h in heads:
                        mm = pe.matmul(bank[4][:, cols(h)], inv_t_of[group.slot][:, 2 * a + h, :], rhs[:, cols(h)], start=True, stop=True)
                    mm.then_inc(u_done, 1)

                def make_y(group, a):
                    i, slot = group.ci + a, group.slot
                    queries, by_row, from_k, from_b = queries_of[slot], by_row_of[slot], from_k_of[slot], from_b_of[slot]
                    pe.wait_ge(u_ready, START + i + 1)
                    pe.wait_ge(y_ready, START + i)
                    for h in heads:
                        pe.matmul(bank[5][cols(h), 0:P], by_row[:, a, 2, cols(h)], from_k[:, 2 * a + h, 1, :], start=True, stop=False,
                                  skip_group_check=True)
                        pe.matmul(bank[5][cols(h), 0:P], neg_u[:, cols(h)], from_b[:, 2 * a + h, 1, :], start=False, stop=False,
                                  skip_group_check=True)
                    if group.g == 0:
                        for bb in range(SEQS):
                            t = slice(bb * STEPS, bb * STEPS + STEPS)
                            mm = pe.matmul(bank[5][:, t], s_seq[:, bb, :], queries[:, 0, 1, t], start=False, stop=(bb == SEQS - 1),
                                           skip_group_check=True)
                    else:
                        mm = pe.matmul(bank[5][:, 0:P], s[:], queries[:, a, 1, :], start=False, stop=True, skip_group_check=True)
                    mm.then_inc(y_done, 1)
                    if group.g == 0:
                        pe.wait_ge(blocks_ready, START + group.j + 1)
                        for g in range(3):
                            out = bank[g][:, 0:3 * P]
                            flat = slice(3 * g, 3 * g + 3)
                            pe.matmul(out, by_row[:, 0, 0, :], v_block[:, flat, :].rearrange("p a v -> p (a v)"), start=True, stop=False,
                                      skip_group_check=True)
                            pe.matmul(out, by_row[:, 0, 1, :], u_block[:, flat, :].rearrange("p a v -> p (a v)"), start=False, stop=False,
                                      skip_group_check=True)
                            had = min(3, SEQS - 3 * g)
                            mm = pe.matmul(bank[g][:, 0:had * P], eye[:], s_seq[:, 3 * g:3 * g + had, :].rearrange("p a v -> p (a v)"),
                                           start=False, stop=True, skip_group_check=True)
                    else:
                        pe.matmul(bank[6][:, 0:P], by_row[:, a, 0, :], by_row[:, a, 2, :], start=True, stop=False, skip_group_check=True)
                        pe.matmul(bank[6][:, 0:P], by_row[:, a, 1, :], neg_u[:], start=False, stop=False, skip_group_check=True)
                        mm = pe.matmul(bank[6][:, 0:P], eye[:], s[:], start=False, stop=True, skip_group_check=True)
                    mm.then_inc(s_done, 1)

                def chain(group):
                    pe.wait_ge(merged, START + group.gi * MERGES + MERGES)
                    for a in range(group.n):
                        make_rhs(group, a)
                        make_u(group, a)
                        make_y(group, a)

                def after(j, x):
                    pe.wait_ge(s_ready, START + j * NT + NT)
                    pe.wait_ge(y_ready, START + j * NT + NT)
                    head_sums(y_all, 0, ep_pe)
                    pe.wait_ge(ep_act, START + j * 2 + 1)
                    head_sums(cum, 3, ep_pe)

                def before(j, x):
                    pe.wait_ge(masks_loaded, START + 16 * MASKS)

                over_groups(pe, prepare, before, start, within, chain, after)


KEPT_CHUNKS = ((0, CH), (CH, CH), (2 * CH, KEPT - 2 * CH))
ROW_TILES = [(lo, min(P, KEPT - lo)) for lo in range(0, KEPT, P)]
RT = len(ROW_TILES)
PEER_HEADS = 8
TOPK = 16
N_KEYS = 128
LOWEST = -3.0e38


def inverse_rms_steps(dve, act_sqrt_done, src_banks, dst, chunks, width, step, start):
    for c, (lo, n) in enumerate(chunks):
        last = dve.tensor_scalar(dst[:, lo:lo + n], src_banks[c][:, 0:n], 1.0 / width, RMS_EPS, ALU.mult, ALU.add)
    last.then_inc(step, 1)
    dve.wait_ge(act_sqrt_done, start + 1)
    dve.reciprocal(dst[:], dst[:]).then_inc(step, 1)
    dve.wait_ge(step, start + 2)


def output_projection(nc, h, u, x_kept_d, y_d, w_out_d, norm_g_d):
    with Stage(nc, "outp") as st:
        sb, psum, sem = st.sb, st.psum, st.sem
        y_hi, y_lo = sb("y_hi", [P, KD, KEPT], F32R), sb("y_lo", [P, KD, KEPT], F32R)
        w = [sb(f"w_out_{s}", [P, WCOLS]) for s in range(2)]
        w_hi = [sb(f"w_out_hi_{s}", [P, WCOLS], F32R) for s in range(2)]
        w_lo = [sb(f"w_out_lo_{s}", [P, WCOLS], F32R) for s in range(2)]
        inv_rms = sb("inv_rms", [P, KEPT])
        norm_g, ones = sb("norm_ffn_g", [P, KD]), sb("ones", [P, P])
        out = [[psum(f"out_{s}{c}", BANK) for c in range(3)] for s in range(2)]
        x_loaded, g_loaded, ones_ready = sem("xk_loaded"), sem("g_loaded"), sem("ones_ready")
        y_loaded = [sem(f"y_loaded_{k}") for k in range(KD)]
        w_loaded = [sem(f"w_out_loaded_{s}") for s in range(2)]
        y_rounded, y_split, w_rounded, w_split = sem("y_rounded"), sem("y_split"), sem("w_rounded"), sem("w_split")
        out_done, h_ready, squared, sum_done, rms_step, rooted, u_ready = (
            sem("out_done"), sem("h_ready"), sem("squared"), sem("sum_done"), sem("rms_step"), sem("rooted"), sem("u_ready"))

        def over_tiles(eng, body):
            for s in range(2):
                body(0, s, s)
            with eng.Fori(1, KD // 2 - 1) as q:
                for s in range(2):
                    body(q, s, q * 2 + s)
            for s in range(2):
                body(KD // 2 - 1, s, KD - 2 + s)

        with nc.Block() as block:
            @block.sync
            def _(sp):
                for k in range(KD):
                    sp.dma_start(u[:, k, :], y_d[k]).then_inc(y_loaded[k], 16)
                sp.dma_start(norm_g[:], norm_g_d).then_inc(g_loaded, 16)
                sp.dma_start(h[:], x_kept_d.rearrange("k p t -> p k t")).then_inc(x_loaded, 16)

            @block.gpsimd
            def _(pool):
                st.start(pool, *w_loaded)
                pool.memset(ones[:], 1.0).then_inc(ones_ready, 1)

                def load(q, s, m):
                    pool.wait_ge(w_split, START + m - 1)
                    pool.dma_start(w[s][:], at(w_out_d, m)).then_inc(w_loaded[s], 16)

                pool.wait_ge(ones_ready, START + 1)
                over_tiles(pool, load)

            @block.tensor
            def _(pe):
                def project(q, s, m):
                    pe.wait_ge(w_split, START + m + 1)
                    pe.wait_ge(h_ready, START + q * 6)
                    for c, (lo, n) in enumerate(KEPT_CHUNKS):
                        for k in range(KD):
                            if isinstance(m, int) and m == 0 and c == 0:
                                pe.wait_ge(y_split, START + k + 1)
                            cut = slice(k * P, k * P + P)
                            mm = product(pe, out[s][c][:, 0:n], w_hi[s][:, cut], w_lo[s][:, cut],
                                         y_hi[:, k, lo:lo + n], y_lo[:, k, lo:lo + n], k == 0, k == KD - 1)
                        mm.then_inc(out_done, 1)

                over_tiles(pe, project)
                pe.wait_ge(ones_ready, START + 1)
                pe.wait_ge(h_ready, START + 3 * KD)
                for k in range(KD):
                    pe.wait_ge(squared, START + k + 1)
                    for c, (lo, n) in enumerate(KEPT_CHUNKS):
                        mm = pe.matmul(out[0][c][:, 0:n], ones[:], u[:, k, lo:lo + n], start=(k == 0), stop=(k == KD - 1))
                    mm.then_inc(sum_done, 1)

            @block.scalar
            def _(act):
                def round_w(q, s, m):
                    act.wait_ge(w_loaded[s], q * 16 + 16)
                    act.wait_ge(out_done, START + q * 6)
                    act.activation(w_hi[s][:], w[s][:], ACT.Copy).then_inc(w_rounded, 1)
                    if isinstance(m, int) and m == 1:
                        for k in range(KD):
                            act.wait_ge(y_loaded[k], START + 16)
                            act.activation(y_hi[:, k, :], u[:, k, :], ACT.Copy).then_inc(y_rounded, 1)

                over_tiles(act, round_w)
                for k in range(KD):
                    act.wait_ge(h_ready, START + 3 * (k + 1))
                    act.activation(u[:, k, :], h[:, k, :], ACT.Square).then_inc(squared, 1)
                act.wait_ge(rms_step, START + 1)
                act.activation(inv_rms[:], inv_rms[:], ACT.Sqrt).then_inc(rooted, 1)

            @block.vector
            def _(dve):
                def split_w(s, m):
                    dve.wait_ge(w_rounded, START + m + 1)
                    dve.tensor_tensor(w_lo[s][:], w[s][:], w_hi[s][:], ALU.subtract).then_inc(w_split, 1)

                split_w(0, 0)
                for k in range(KD):
                    dve.wait_ge(y_rounded, START + k + 1)
                    dve.tensor_tensor(y_lo[:, k, :], u[:, k, :], y_hi[:, k, :], ALU.subtract).then_inc(y_split, 1)
                dve.wait_ge(x_loaded, START + 16)
                dve.wait_ge(g_loaded, START + 16)

                def add(q, s, m):
                    if not (isinstance(m, int) and m == KD - 1):
                        split_w(1 - s, m + 1)
                    row = h[:, bass.ds(m, 1), :].rearrange("p a t -> p (a t)")
                    for c, (lo, n) in enumerate(KEPT_CHUNKS):
                        dve.wait_ge(out_done, START + q * 6 + (3 * s + c + 1))
                        dve.tensor_tensor(row[:, lo:lo + n], row[:, lo:lo + n], out[s][c][:, 0:n], ALU.add).then_inc(h_ready, 1)

                over_tiles(dve, add)
                dve.wait_ge(sum_done, START + KD)
                inverse_rms_steps(dve, rooted, out[0], inv_rms, KEPT_CHUNKS, D, rms_step, START)
                for k in range(KD):
                    dve.scalar_tensor_tensor(out=u[:, k, :], in0=h[:, k, :], scalar=norm_g[:, k:k + 1], in1=inv_rms[:],
                                             op0=ALU.mult, op1=ALU.mult).then_inc(u_ready, 1)


def pick_experts(nc, u, u_d, picks, w_query_d, keys_d, iota_d):
    with Stage(nc, "pick") as st:
        sb, psum, sem = st.sb, st.psum, st.sem
        w = [sb(f"w_query_{s}", [P, WCOLS]) for s in range(2)]
        keys = sb("sub_keys", [P, 2, N_KEYS])
        q_cols = [sb(f"q_{s}", [P, KEPT]) for s in range(2)]
        scores = [sb(f"scores_{s}", [P, RT, 2, N_KEYS]) for s in range(2)]
        rest = sb("rest", [P, 4, 2, N_KEYS])
        top = sb("top", [P, RT, 2, TOPK])
        top_at = sb("top_at", [P, RT, 2, TOPK], U32)
        top_key = sb("top_key", [P, RT, 2, TOPK], BF16)
        sums = sb("sums", [P, 4, 2, TOPK, TOPK])
        best = sb("best", [P, RT, TOPK])
        expo = sb("expo", [P, RT, TOPK])
        best_at = sb("best_at", [P, RT, TOPK], U32)
        half_at = sb("half_at", [P, 2, RT, TOPK], U32)
        half_f = sb("half_f", [P, 2, RT, TOPK], BF16)
        hit = sb("hit", [P, RT, TOPK, TOPK], BF16)
        places = sb("places", [P, TOPK], BF16)
        total = sb("total", [P, RT])
        iota = sb("iota", [P, P])
        q_ps = [psum(f"q_ps_{c}", BANK) for c in range(3)]
        s_ps = [psum(f"s_ps_{i}", BANK) for i in range(4)]
        iota_loaded, keys_loaded, u_stored = sem("iota_loaded"), sem("keys_loaded"), sem("u_stored")
        w_loaded = [sem(f"w_query_loaded_{s}") for s in range(2)]
        q_done, q_ready, s_done, s_ready = sem("q_done"), sem("q_ready"), sem("s_done"), sem("s_ready")
        vec, topped, shifted, exped = sem("pick_vec"), sem("topped"), sem("shifted"), sem("exped")
        SCORE_BANKS = -(-RT // 2)
        SCORES_AFTER = [[b for b in range(SCORE_BANKS) if lo < min(2 * b * P + 2 * P, KEPT) <= lo + n] for lo, n in KEPT_CHUNKS]

        with nc.Block() as block:
            @block.sync
            def _(sp):
                sp.dma_start(iota[:], iota_d).then_inc(iota_loaded, 16)
                with sp.Fori(0, PEER_HEADS) as i:
                    for s in range(2):
                        sp.wait_ge(q_done, START + i * 6)
                        sp.dma_start(w[s][:], w_query_d[bass.ds(i * 2 + s, 1)].rearrange("a p c -> (a p) c")).then_inc(w_loaded[s], 16)
                    sp.wait_ge(s_done, START + i * SCORE_BANKS)
                    sp.dma_start(keys[:], keys_d[bass.ds(i, 1)].rearrange("a p h k -> (a p) h k")).then_inc(keys_loaded, 16)
                sp.dma_start(u_d.rearrange("k p t -> p k t"), u[:]).then_inc(u_stored, 16)
                sp.wait_ge(u_stored, START + 16)

            @block.tensor
            def _(pe):
                with pe.Fori(0, PEER_HEADS) as i:
                    pe.wait_ge(keys_loaded, START + i * 16 + 16)
                    for c, (lo, n) in enumerate(KEPT_CHUNKS):
                        for s in range(2):
                            if c == 0:
                                pe.wait_ge(w_loaded[s], START + i * 16 + 16)
                            at_q = 2 * c + s
                            pe.wait_ge(q_ready, START + i * 6 + max(at_q - 2, 0))
                            for k in range(KD):
                                mm = pe.matmul(q_ps[at_q % 3][:, 0:n], w[s][:, k * P:k * P + P], u[:, k, lo:lo + n], start=(k == 0), stop=(k == KD - 1))
                            mm.then_inc(q_done, 1)
                        pe.wait_ge(q_ready, START + i * 6 + (2 * c + 2))
                        for b in SCORES_AFTER[c]:
                            if b >= 4:
                                pe.wait_ge(s_ready, START + i * SCORE_BANKS + (b - 3))
                            else:
                                pe.wait_ge(s_ready, START + i * SCORE_BANKS)
                            for a in range(2 * b, min(2 * b + 2, RT)):
                                first_row, rows = ROW_TILES[a]
                                for s in range(2):
                                    col = (a % 2 * 2 + s) * N_KEYS
                                    mm = pe.matmul(s_ps[b % 4][0:rows, col:col + N_KEYS], q_cols[s][:, first_row:first_row + rows], keys[:, s, :],
                                                   start=True, stop=True)
                            mm.then_inc(s_done, 1)

            @block.scalar
            def _(act):
                st.start(act, vec)

                def head(i, slot, even):
                    act.wait_ge(s_done, START + i * SCORE_BANKS)
                    for c, (lo, n) in enumerate(KEPT_CHUNKS):
                        for s in range(2):
                            at_q = 2 * c + s
                            act.wait_ge(q_done, START + i * 6 + (at_q + 1))
                            act.activation(q_cols[s][:, lo:lo + n], q_ps[at_q % 3][:, 0:n], ACT.Copy).then_inc(q_ready, 1)
                        if c == 0:
                            act.wait_ge(topped, START + even)
                        for b in SCORES_AFTER[c]:
                            act.wait_ge(s_done, START + i * SCORE_BANKS + (b + 1))
                            tiles = ROW_TILES[2 * b:2 * b + 2]
                            n = tiles[0][1]
                            act.activation(scores[slot][0:n, 2 * b:2 * b + len(tiles), :, :],
                                           s_ps[b % 4][0:n, 0:len(tiles) * 2 * N_KEYS].rearrange("p (a h k) -> p a h k", a=len(tiles), h=2),
                                           ACT.Copy).then_inc(s_ready, 1)

                def softmax(i):
                    act.wait_ge(shifted, START + i + 1)
                    act.activation(expo[:], expo[:], ACT.Exp).then_inc(exped, 1)

                head(0, 0, 0)
                head(1, 1, 0)
                softmax(0)
                with act.Fori(1, PEER_HEADS // 2) as q:
                    head(q * 2, 0, q * 2 - 1)
                    softmax(q * 2 - 1)
                    head(q * 2 + 1, 1, q * 2)
                    softmax(q * 2)
                softmax(PEER_HEADS - 1)

            @block.vector
            def _(dve):
                dve.memset(best[:], 0.0)
                dve.memset(total[:], 0.0)
                dve.memset(best_at[:], 0)
                dve.memset(top_at[:], 0)
                dve.wait_ge(iota_loaded, START + 16)
                dve.tensor_copy(places[:], iota[:, 0:TOPK]).then_inc(vec, 1)
                dve.wait_ge(vec, 1)

                def head(i, slot):
                    dve.sem_clear(vec)
                    steps = [0]

                    def step(last):
                        steps[0] += 1
                        last.then_inc(vec, 1)
                        dve.wait_ge(vec, steps[0])

                    dve.wait_ge(s_ready, START + i * SCORE_BANKS + len(SCORES_AFTER[0]))
                    step(dve.tensor_copy(best[:, 0, 0:1], total[:, 0:1]))
                    for banks in SCORES_AFTER:
                        first_tile = 2 * banks[0]
                        tiles = [(a, a - first_tile, ROW_TILES[a][1]) for a in range(first_tile, min(2 * banks[-1] + 2, RT))]
                        halves = [(a, t, n, s) for a, t, n in tiles for s in range(2)]
                        for a, t, n, s in halves:
                            last = dve.max(top[0:n, a, s, 0:8], scores[slot][0:n, a, s, :])
                        step(last)
                        for a, t, n, s in halves:
                            dve.max_index(top_at[0:n, a, s, 0:8], top[0:n, a, s, 0:8], scores[slot][0:n, a, s, :])
                            last = dve.match_replace(rest[0:n, t, s, :], top[0:n, a, s, 0:8], scores[slot][0:n, a, s, :], LOWEST)
                        step(last)
                        for a, t, n, s in halves:
                            last = dve.max(top[0:n, a, s, 8:16], rest[0:n, t, s, :])
                        step(last)
                        for a, t, n, s in halves:
                            last = dve.max_index(top_at[0:n, a, s, 8:16], top[0:n, a, s, 8:16], rest[0:n, t, s, :])
                        if banks is not SCORES_AFTER[-1]:
                            following = SCORES_AFTER[SCORES_AFTER.index(banks) + 1]
                            dve.wait_ge(s_ready, START + i * SCORE_BANKS + (following[-1] + 1))
                        for a, t, n in tiles:
                            last = dve.tensor_tensor(sums[0:n, t, 0, :, :], top[0:n, a, 0, :].unsqueeze(2).broadcast_to([n, TOPK, TOPK]),
                                                     top[0:n, a, 1, :].unsqueeze(1).broadcast_to([n, TOPK, TOPK]), ALU.add)
                        step(last)
                        every = sums[:].rearrange("p t s i j -> p t s (i j)")
                        for a, t, n in tiles:
                            last = dve.max(best[0:n, a, 0:8], every[0:n, t, 0, :])
                        step(last)
                        for a, t, n in tiles:
                            dve.max_index(best_at[0:n, a, 0:8], best[0:n, a, 0:8], every[0:n, t, 0, :])
                            last = dve.match_replace(every[0:n, t, 1, :], best[0:n, a, 0:8], every[0:n, t, 0, :], LOWEST)
                        step(last)
                        for a, t, n in tiles:
                            last = dve.max(best[0:n, a, 8:16], every[0:n, t, 1, :])
                        step(last)
                        for a, t, n in tiles:
                            last = dve.max_index(best_at[0:n, a, 8:16], best[0:n, a, 8:16], every[0:n, t, 1, :])
                    last.then_inc(topped, 1)
                    dve.wait_ge(topped, START + i + 1)
                    dve.tensor_tensor(expo[:], best[:], best[:, :, 0:1].broadcast_to([P, RT, TOPK]), ALU.subtract).then_inc(shifted, 1)
                    dve.tensor_copy(top_key[:], top_at[:])
                    dve.tensor_scalar(half_at[:, 0, :, :], best_at[:], 4, None, ALU.logical_shift_right)
                    step(dve.tensor_scalar(half_at[:, 1, :, :], best_at[:], 15, None, ALU.bitwise_and))
                    step(dve.tensor_copy(half_f[:], half_at[:]))
                    for s in range(2):
                        cube = [P, RT, TOPK, TOPK]
                        step(dve.tensor_tensor(hit[:], places[:].unsqueeze(1).unsqueeze(1).broadcast_to(cube),
                                               half_f[:, s, :, :].unsqueeze(3).broadcast_to(cube), ALU.is_equal))
                        step(dve.tensor_tensor(hit[:], hit[:], top_key[:, :, s, :].unsqueeze(2).broadcast_to(cube), ALU.mult))
                        step(dve.tensor_reduce(picks[:, s, :, bass.ds(i * TOPK, TOPK)], hit[:], AX_X, ALU.add))
                    dve.wait_ge(exped, START + i + 1)
                    step(dve.tensor_reduce(total[:], expo[:], AX_X, ALU.add))
                    step(dve.reciprocal(total[:], total[:]))
                    step(dve.tensor_tensor(picks[:, 2, :, bass.ds(i * TOPK, TOPK)], expo[:], total[:].unsqueeze(2).broadcast_to([P, RT, TOPK]), ALU.mult))

                with dve.Fori(0, PEER_HEADS // 2) as q:
                    head(q * 2, 0)
                    head(q * 2 + 1, 1)


GROUP_ROWS = 64
ROW_GROUPS = KEPT // GROUP_ROWS
BATCH = 8
GATE_PARTS = 3


def spread_gates(nc, picks, gates_d, eye_d, iota_d):
    with Stage(nc, "spread") as st:
        sb, psum, sem = st.sb, st.psum, st.sem
        eye, iota = sb("eye", [P, P]), sb("iota", [P, P])
        keys_of = sb("keys_of", [P, 2, KEPT], BF16)
        gate_of = sb("gate_of", [P, KEPT])
        parts = sb("gate_parts", [P, GATE_PARTS, KEPT], BF16)
        every_key = sb("every_key", [P, N_KEYS, BATCH], BF16)
        hot_i = [sb(f"hot_i_{s}", [P, N_KEYS, BATCH], BF16) for s in range(2)]
        hot_j = [sb(f"hot_j_{s}", [P, N_KEYS, BATCH], BF16) for s in range(2)]
        weighted_j = [[sb(f"weighted_{s}_{p}", [P, N_KEYS, BATCH], BF16) for p in range(GATE_PARTS)] for s in range(2)]
        spread = [sb(f"spread_{s}", [P, N_KEYS, GROUP_ROWS]) for s in range(2)]
        g_ps = [psum(f"g_ps_{s}", BATCH, P) for s in range(2)]
        t_ps = [psum(f"t_ps_{s}", BANK) for s in range(2)]
        consts_loaded, turned, turned_out = sem("consts_loaded"), sem("turned"), sem("turned_out")
        hot_j_ready, dve_ready, pool_ready = sem("hot_j_ready"), sem("dve_ready"), sem("pool_ready")
        prep = sem("gate_parts_step")
        g_done, g_out = sem("g_done"), sem("g_out")
        stored = [sem(f"g_stored_{s}") for s in range(2)]
        PER_GROUP = GROUP_ROWS // BATCH

        def over_groups(eng, before, batch, after):
            def group(q, s, g):
                before(q, s, g)
                with eng.Fori(0, PER_GROUP // 2) as b:
                    for a in range(2):
                        batch(s, a, g * PER_GROUP + b * 2 + a, b * 2 + a)
                after(q, s, g)

            with eng.Fori(0, ROW_GROUPS // 2) as q:
                for s in range(2):
                    group(q, s, q * 2 + s)
            group(ROW_GROUPS // 2, 0, ROW_GROUPS - 1)

        cube = [P, N_KEYS, BATCH]
        PREP = 2 * GATE_PARTS

        def of_rows(buf, i):
            return buf[:, bass.ds(i * BATCH, BATCH)].unsqueeze(1).broadcast_to(cube)

        nothing = lambda *_: None
        with nc.Block() as block:
            @block.sync
            def _(sp):
                sp.dma_start(eye[:], eye_d).then_inc(consts_loaded, 16)
                sp.dma_start(iota[:], iota_d).then_inc(consts_loaded, 16)

                def store(q, s, g):
                    sp.wait_ge(g_out, START + g * PER_GROUP + PER_GROUP)
                    sp.dma_start(at(gates_d, g), spread[s][:].rearrange("p j t -> p (j t)")).then_inc(stored[s], 16)

                over_groups(sp, nothing, lambda *_: None, store)
                for s in range(2):
                    sp.wait_ge(stored[s], START + 16 * ((ROW_GROUPS + 1 - s) // 2))

            @block.tensor
            def _(pe):
                pe.wait_ge(consts_loaded, START + 32)
                for a, (lo, n) in enumerate(ROW_TILES):
                    if a >= 2:
                        pe.wait_ge(turned_out, START + a - 1)
                    for s in range(3):
                        mm = pe.transpose(t_ps[a % 2][:, s * P:s * P + n], picks[0:n, s, a, :], eye[0:n, 0:n])
                    mm.then_inc(turned, 1)

                def batch(s, a, i, b):
                    pe.wait_ge(dve_ready, START + i + 1)
                    pe.wait_ge(pool_ready, START + i + 1)
                    pe.wait_ge(g_out, START + i - 1)
                    for t in range(BATCH):
                        for p in range(GATE_PARTS):
                            mm = pe.matmul(g_ps[a][:, t, :], hot_i[a][:, :, t], weighted_j[a][p][:, :, t], start=(p == 0), stop=(p == GATE_PARTS - 1))
                    mm.then_inc(g_done, 1)

                over_groups(pe, nothing, batch, nothing)

            @block.scalar
            def _(act):
                for a, (lo, n) in enumerate(ROW_TILES):
                    act.wait_ge(turned, START + a + 1)
                    by_slice = t_ps[a % 2][:, 0:3 * P].rearrange("p (s t) -> p s t", s=3)[:, :, 0:n]
                    act.activation(keys_of[:, :, lo:lo + n], by_slice[:, 0:2, :], ACT.Copy)
                    act.activation(gate_of[:, lo:lo + n], by_slice[:, 2, :], ACT.Copy).then_inc(turned_out, 1)

                def before(q, s, g):
                    act.wait_ge(stored[s], START + q * 16)

                def batch(s, a, i, b):
                    act.wait_ge(g_done, START + i + 1)
                    act.activation(spread[s][:, :, bass.ds(b * BATCH, BATCH)], g_ps[a].rearrange("p t j -> p j t"), ACT.Copy).then_inc(g_out, 1)

                over_groups(act, before, batch, nothing)

            @block.vector
            def _(dve):
                dve.wait_ge(consts_loaded, START + 32)
                dve.tensor_copy(every_key[:], iota[:].unsqueeze(2).broadcast_to(cube)).then_inc(prep, 1)
                dve.wait_ge(turned_out, START + RT)
                for p in range(GATE_PARTS):
                    dve.tensor_copy(parts[:, p, :], gate_of[:]).then_inc(prep, 1)
                    dve.wait_ge(prep, START + 2 + 2 * p)
                    if p < GATE_PARTS - 1:
                        dve.tensor_tensor(gate_of[:], gate_of[:], parts[:, p, :], ALU.subtract).then_inc(prep, 1)
                        dve.wait_ge(prep, START + 3 + 2 * p)

                def batch(s, a, i, b):
                    dve.wait_ge(g_done, START + i - 1)
                    dve.tensor_tensor(hot_j[a][:], every_key[:], of_rows(keys_of[:, 1], i), ALU.is_equal).then_inc(hot_j_ready, 1)
                    dve.tensor_tensor(hot_i[a][:], every_key[:], of_rows(keys_of[:, 0], i), ALU.is_equal)
                    dve.wait_ge(hot_j_ready, START + i + 1)
                    for p in range(GATE_PARTS - 1):
                        last = dve.tensor_tensor(weighted_j[a][p][:], hot_j[a][:], of_rows(parts[:, p], i), ALU.mult)
                    last.then_inc(dve_ready, 1)

                over_groups(dve, nothing, batch, nothing)

            @block.gpsimd
            def _(pool):
                st.start(pool)

                def batch(s, a, i, b):
                    pool.wait_ge(hot_j_ready, START + i + 1)
                    pool.tensor_tensor(weighted_j[a][GATE_PARTS - 1][:], hot_j[a][:], of_rows(parts[:, GATE_PARTS - 1], i), ALU.mult).then_inc(pool_ready, 1)

                pool.wait_ge(prep, START + PREP)
                over_groups(pool, nothing, batch, nothing)


SET = 2
SETS = N_KEYS // SET


def run_experts(nc, h, u_d, gates_d, up_d, down_d, norm_g_d, out_d):
    with Stage(nc, "experts") as st:
        sb, psum, sem = st.sb, st.psum, st.sem
        u_hi, u_lo = sb("u_hi", [P, KD, KEPT], F32R), sb("u_lo", [P, KD, KEPT], F32R)
        up = [sb(f"up_{e}", [P, WCOLS]) for e in range(SET)]
        up_hi = [sb(f"up_hi_{e}", [P, WCOLS], F32R) for e in range(SET)]
        up_lo = [sb(f"up_lo_{e}", [P, WCOLS], F32R) for e in range(SET)]
        down = sb("down", [P, D])
        down_hi, down_lo = sb("down_hi", [P, SET, D], F32R), sb("down_lo", [P, SET, D], F32R)
        gates = [sb(f"gates_{s}", [P, ROW_GROUPS, SET, GROUP_ROWS]) for s in range(2)]
        act_v = [sb(f"act_v_{e}", [P, KEPT]) for e in range(SET)]
        act_hi = [sb(f"act_hi_{s}", [P, SET, KEPT], F32R) for s in range(2)]
        act_lo = [sb(f"act_lo_{s}", [P, SET, KEPT], F32R) for s in range(2)]
        norm_g, ones = sb("norm_final_g", [P, KD]), sb("ones", [P, P])
        halves = [g[:].rearrange("p g j t -> p (g j t)")[:, n * KEPT:n * KEPT + KEPT] for n in range(2) for g in gates]
        inv_rms = halves[0]
        up_ps = [[psum(f"up_ps_{e}{c}", BANK) for c in range(3)] for e in range(SET)]
        down_ps = [up_ps[0][0], up_ps[0][1], psum("down_ps_0", BANK), psum("down_ps_1", BANK), up_ps[0][2]]
        DOWN_BANKS = len(down_ps)
        squares = [act_v[0][:], act_v[1][:], *halves[1:]]
        u_loaded = [sem(f"u_loaded_{k}") for k in range(KD)]
        up_loaded = [sem(f"up_loaded_{e}") for e in range(SET)]
        down_loaded = sem("down_loaded")
        gates_loaded = [sem(f"gates_loaded_{s}") for s in range(2)]
        ones_ready, g_loaded = sem("ones_ready"), sem("g_loaded")
        u_rounded, u_split = sem("u_rounded"), sem("u_split")
        squared, sum_done, rms_step, rooted, out_ready, out_stored = (
            sem("squared"), sem("sum_done"), sem("rms_step"), sem("rooted"), sem("out_ready"), sem("out_stored"))
        FROM = 3
        up_rounded, up_split, up_done, gelu_ready = sem("up_rounded"), sem("up_split"), sem("up_done"), sem("gelu_ready")
        gated, act_rounded, act_split = sem("gated"), sem("act_rounded"), sem("act_split")
        down_rounded, down_split, down_done, added = sem("down_rounded"), sem("down_split"), sem("down_done"), sem("added")
        UNITS = KD * 3

        def over_sets(eng, first, second):
            first(0, 0)
            with eng.Fori(0, SETS // 2 - 1) as q:
                first(q * 2 + 1, 1)
                second(q * 2, 0)
                first(q * 2 + 2, 0)
                second(q * 2 + 1, 1)
            first(SETS - 1, 1)
            second(SETS - 2, 0)
            second(SETS - 1, 1)

        def is_set(g, n):
            return isinstance(g, int) and g == n

        nothing = lambda *_: None
        with nc.Block() as block:
            @block.sync
            def _(sp):
                for e in range(SET):
                    sp.dma_start(up[e][:], up_d[e]).then_inc(up_loaded[e], 16)
                for k in range(KD):
                    if k >= 4:
                        sp.wait_ge(u_split, k - 3)
                    sp.dma_start(halves[k % 4], u_d[k]).then_inc(u_loaded[k], 16)

                def first(g, slot):
                    i0 = g * SET
                    for e in range(0 if is_set(g, 0) else SET):
                        sp.wait_ge(up_split, FROM + i0 + (e - 1))
                        sp.dma_start(up[e][:], at(up_d, i0 + e)).then_inc(up_loaded[e], 16)
                    if is_set(g, 0):
                        sp.wait_ge(u_split, KD)
                    else:
                        sp.wait_ge(gated, FROM + i0 - SET)
                    src = gates_d[:, :, g * SET:g * SET + SET, :] if isinstance(g, int) else gates_d[:, :, bass.ds(g * SET, SET), :]
                    sp.dma_start(gates[slot][:], src.rearrange("g p j t -> p g j t")).then_inc(gates_loaded[slot], 16)

                over_sets(sp, first, nothing)
                for k in range(KD):
                    sp.wait_ge(out_ready, k + 1)
                    sp.dma_start(out_d[k], h[:, k, :]).then_inc(out_stored, 16)
                sp.wait_ge(out_stored, 16 * KD)

            @block.gpsimd
            def _(pool):
                pool.memset(ones[:], 1.0).then_inc(ones_ready, 1)
                pool.dma_start(norm_g[:], norm_g_d).then_inc(g_loaded, 16)
                pool.dma_start(down[:], down_d[0]).then_inc(down_loaded, 16)
                with pool.Fori(1, N_KEYS) as i:
                    pool.wait_ge(down_split, FROM + i)
                    pool.dma_start(down[:], at(down_d, i)).then_inc(down_loaded, 16)

            @block.tensor
            def _(pe):
                pe.sem_inc(up_done, FROM)
                pe.sem_inc(down_done, FROM)

                def first(g, slot):
                    i0 = g * SET
                    for e in range(SET):
                        pe.wait_ge(up_split, FROM + i0 + (e + 1))
                        for c, (lo, n) in enumerate(KEPT_CHUNKS):
                            if not is_set(g, 0):
                                pe.wait_ge(gelu_ready, FROM + i0 * 3 + (3 * e - 5 + c))
                            if e == 0 and not is_set(g, 0):
                                pe.wait_ge(added, FROM + g * UNITS - (UNITS + 2))
                            for k in range(KD):
                                if is_set(g, 0) and e == 0 and c == 0:
                                    pe.wait_ge(u_split, k + 1)
                                cut = slice(k * P, k * P + P)
                                mm = product(pe, up_ps[e][c][:, 0:n], up_hi[e][:, cut], up_lo[e][:, cut],
                                             u_hi[:, k, lo:lo + n], u_lo[:, k, lo:lo + n], k == 0, k == KD - 1)
                            mm.then_inc(up_done, 1)

                def second(g, slot):
                    pe.wait_ge(down_split, FROM + g * SET + SET)
                    pe.wait_ge(act_split, FROM + g * SET + SET)
                    pe.wait_ge(added, FROM + g * UNITS)
                    pe.wait_ge(gelu_ready, FROM + SETS * SET * 3 if is_set(g, SETS - 1) else FROM + g * (SET * 3) + (SET * 3 + 3))
                    for m in range(KD):
                        for c, (lo, n) in enumerate(KEPT_CHUNKS):
                            i = 3 * m + c
                            if i >= DOWN_BANKS:
                                pe.wait_ge(added, FROM + g * UNITS + (i - DOWN_BANKS + 1))
                            for e in range(SET):
                                cut = slice(m * P, m * P + P)
                                mm = product(pe, down_ps[i % DOWN_BANKS][:, 0:n], down_hi[:, e, cut], down_lo[:, e, cut],
                                             act_hi[slot][:, e, lo:lo + n], act_lo[slot][:, e, lo:lo + n], e == 0, e == SET - 1)
                            mm.then_inc(down_done, 1)

                over_sets(pe, first, second)
                pe.wait_ge(ones_ready, 1)
                for k in range(KD):
                    pe.wait_ge(squared, k + 1)
                    for c, (lo, n) in enumerate(KEPT_CHUNKS):
                        mm = pe.matmul(up_ps[1][c][:, 0:n], ones[:], squares[k % len(squares)][:, lo:lo + n], start=(k == 0), stop=(k == KD - 1))
                    mm.then_inc(sum_done, 1)

            @block.scalar
            def _(act):
                for s in (up_rounded, gelu_ready, act_rounded, down_rounded):
                    act.sem_inc(s, FROM)
                act.wait_ge(up_loaded[0], 16)
                act.activation(up_hi[0][:], up[0][:], ACT.Copy).then_inc(up_rounded, 1)
                for k in range(KD):
                    act.wait_ge(u_loaded[k], 16)
                    act.activation(u_hi[:, k, :], halves[k % 4], ACT.Copy).then_inc(u_rounded, 1)

                def round_up(i, e, loads):
                    act.wait_ge(up_loaded[e], loads * 16)
                    act.wait_ge(up_done, FROM + (i - 1) * 3)
                    act.activation(up_hi[e][:], up[e][:], ACT.Copy).then_inc(up_rounded, 1)

                def round_down(g, e):
                    act.wait_ge(down_loaded, (g * SET + (e + 1)) * 16)
                    if not is_set(g, 0):
                        act.wait_ge(down_done, FROM + g * UNITS)
                    act.activation(down_hi[:, e, :], down[:], ACT.Copy).then_inc(down_rounded, 1)

                def first(g, slot):
                    i0 = g * SET
                    for e in range(SET):
                        if e == 0:
                            round_up(i0 + 1, 1, g + 1)
                        elif not is_set(g, SETS - 1):
                            round_up(i0 + 2, 0, g + 2)
                        if not is_set(g, 0):
                            round_down(g - 1, e)
                            act.wait_ge(act_split, FROM + i0 + (e - 1))
                        for c, (lo, n) in enumerate(KEPT_CHUNKS):
                            act.wait_ge(up_done, FROM + i0 * 3 + (3 * e + c + 1))
                            act.activation(act_v[e][:, lo:lo + n], up_ps[e][c][:, 0:n], ACT.Gelu).then_inc(gelu_ready, 1)
                        act.wait_ge(gated, FROM + i0 + (e + 1))
                        act.activation(act_hi[slot][:, e, :], act_v[e][:], ACT.Copy).then_inc(act_rounded, 1)

                over_sets(act, first, nothing)
                for e in range(SET):
                    round_down(SETS - 1, e)
                for k in range(KD):
                    act.wait_ge(added, FROM + (SETS - 1) * UNITS + 3 * (k + 1))
                    if k >= len(squares):
                        act.wait_ge(sum_done, k - len(squares) + 1)
                    act.activation(squares[k % len(squares)], h[:, k, :], ACT.Square).then_inc(squared, 1)
                act.wait_ge(rms_step, 1)
                act.activation(inv_rms, inv_rms, ACT.Sqrt).then_inc(rooted, 1)

            @block.vector
            def _(dve):
                for s in (up_split, gated, act_split, down_split, added):
                    dve.sem_inc(s, FROM)

                def rest(out, x, x_hi):
                    return dve.tensor_tensor(out, x, x_hi, ALU.subtract)

                def split_up(i, e):
                    dve.wait_ge(up_rounded, FROM + i + 1)
                    rest(up_lo[e][:], up[e][:], up_hi[e][:]).then_inc(up_split, 1)

                def split_down(g, e):
                    dve.wait_ge(down_rounded, FROM + g * SET + (e + 1))
                    rest(down_lo[:, e, :], down[:], down_hi[:, e, :]).then_inc(down_split, 1)

                def gate(g, slot, e):
                    if e == 0:
                        dve.wait_ge(gates_loaded[slot], g * 8 + (16 - 8 * slot))
                    dve.wait_ge(gelu_ready, FROM + g * (3 * SET) + (3 * e + 3))
                    a = act_v[e][:].rearrange("p (g t) -> p g t", g=ROW_GROUPS)
                    dve.tensor_tensor(a, a, gates[slot][:, :, e, :], ALU.mult).then_inc(gated, 1)

                def split_act(g, slot, e):
                    dve.wait_ge(act_rounded, FROM + g * SET + (e + 1))
                    rest(act_lo[slot][:, e, :], act_v[e][:], act_hi[slot][:, e, :]).then_inc(act_split, 1)

                def first(g, slot):
                    for e in range(SET):
                        if not (e == 1 and is_set(g, SETS - 1)):
                            split_up(g * SET + (e + 1), 1 - e)
                        if not is_set(g, 0):
                            split_down(g - 1, e)
                        if e == 0 or is_set(g, 0):
                            gate(g, slot, e)
                            split_act(g, slot, e)

                def second(g, slot):
                    if is_set(g, SETS - 1):
                        for e in range(SET):
                            split_down(g, e)
                    for m in range(KD):
                        for c, (lo, n) in enumerate(KEPT_CHUNKS):
                            i = 3 * m + c
                            dve.wait_ge(down_done, FROM + g * UNITS + (i + 1))
                            dve.tensor_tensor(h[:, m, lo:lo + n], h[:, m, lo:lo + n], down_ps[i % DOWN_BANKS][:, 0:n], ALU.add).then_inc(added, 1)
                            if i == 3 and not is_set(g, SETS - 1):
                                gate(g + 1, 1 - slot, 1)
                            if i == 7 and not is_set(g, SETS - 1):
                                split_act(g + 1, 1 - slot, 1)

                split_up(0, 0)
                for k in range(KD):
                    dve.wait_ge(u_rounded, k + 1)
                    rest(u_lo[:, k, :], halves[k % 4], u_hi[:, k, :]).then_inc(u_split, 1)
                over_sets(dve, first, second)
                dve.wait_ge(sum_done, KD)
                dve.wait_ge(g_loaded, 16)
                inverse_rms_steps(dve, rooted, up_ps[1], inv_rms, KEPT_CHUNKS, D, rms_step, 0)
                for k in range(KD):
                    dve.scalar_tensor_tensor(out=h[:, k, :], in0=h[:, k, :], scalar=norm_g[:, k:k + 1], in1=inv_rms,
                                             op0=ALU.mult, op1=ALU.mult).then_inc(out_ready, 1)


def pack_w_in(inputs):
    w_in = np.asarray(inputs["w_in"])[0]
    gate, conv, dt, shift = np.split(w_in, [512, 1536, 1544], axis=1)
    coefs = np.zeros((IN_TILES, P, COEFS_IN), w_in.dtype)
    w_cols = np.zeros((D, IN_TILES * P), w_in.dtype)
    w_cols[:, :1024] = conv
    w_cols[:, 1024:2816] = shift
    w_cols[:, 2816:3328] = gate
    w_cols[:, 3328:3336] = dt
    coefs[:8, :, 0:4] = np.asarray(inputs["conv_w"])[0].T.reshape(8, P, 4)
    coefs[:8, :, 4] = np.asarray(inputs["conv_b"])[0].reshape(8, P)
    coefs[8:22, :, 0] = np.asarray(inputs["shift_mu"])[0].reshape(14, P)
    return tile_weights(w_cols), coefs.transpose(1, 0, 2).reshape(P, IN_TILES * COEFS_IN)


def pack_hist(inputs):
    conv = np.asarray(inputs["state_conv"])[0]
    shift = np.asarray(inputs["state_shift"])[0]
    out = np.zeros((CONV_TILES + SHIFT_TILES + 1, P, SEQS, HIST), conv.dtype)
    out[:8] = conv.transpose(2, 0, 1).reshape(8, P, SEQS, HIST)
    out[8:22, :, :, HIST - 1] = shift.T.reshape(14, P, SEQS)
    return out


def pack_ssd_par(inputs):
    a = np.asarray
    by_head = np.stack([a(inputs["dt_bias"])[0], a(inputs["a_log"])[0]], axis=1)
    d = np.repeat(a(inputs["d_skip"])[0], HD).reshape(4, P).T
    g = a(inputs["ssm_norm"])[0].reshape(4, P).T
    return by_head, np.stack([d, g], axis=1)


def pack_ssd_state(inputs):
    return np.asarray(inputs["state_ssd"])[0].transpose(3, 0, 1, 2).reshape(STATE, SEQS, SSD_W)


def pack_pair_par(inputs):
    a = lambda name: np.asarray(inputs[name])[0]
    out = np.zeros((PAIRS + 1, P, 3 * P + COEFS), a("decay_w2").dtype)
    cut = lambda w: w.reshape(w.shape[0], PAIRS, P).transpose(1, 0, 2)
    out[:PAIRS, 0:HD, 0:P] = cut(a("decay_w2"))
    out[:PAIRS, HD:P, P:2 * P] = cut(a("iclr_a2"))
    out[:PAIRS, :, 2 * P:3 * P] = cut(a("gate_g2"))
    for i, name in enumerate(("decay_w0", "iclr_a0", "k_k", "k_a", "r_k", "lnx_w", "lnx_b")):
        out[:PAIRS, :, 3 * P + i] = a(name).reshape(PAIRS, P)
    return out


def pack_wkv(inputs):
    w = np.asarray(inputs["state_wkv"])[0]
    out = np.zeros((PAIRS + 1, P, SEQS, HD), w.dtype)
    out[:PAIRS] = w.reshape(SEQS, PAIRS, 2, HD, HD).transpose(1, 2, 4, 0, 3).reshape(PAIRS, P, SEQS, HD)
    return out


def tile_weights(w):
    return np.ascontiguousarray(w.reshape(KD, P, -1, P).transpose(2, 1, 0, 3).reshape(-1, P, WCOLS))


def pack_keys(inputs):
    return np.ascontiguousarray(np.asarray(inputs["sub_keys"])[0].transpose(1, 3, 0, 2))


def pack_up(inputs):
    w = np.asarray(inputs["expert_u"])[0].reshape(N_KEYS, N_KEYS, KD, P)
    return np.ascontiguousarray(w.transpose(1, 3, 2, 0).reshape(N_KEYS, P, WCOLS))


def pack_down(inputs):
    return np.ascontiguousarray(np.asarray(inputs["expert_v"])[0].reshape(N_KEYS, N_KEYS, D).transpose(1, 0, 2))


def decoder_step(nc, i, o):
    def scratch(name, *shape):
        return nc.dram_tensor(name, shape, F32, kind="Internal").ap()

    cols = scratch("cols", IN_TILES, P, T)
    y = scratch("mixed", KD, P, KEPT)
    u_d = scratch("u_ffn", KD, P, KEPT)
    gates = scratch("gates", ROW_GROUPS, P, N_KEYS * GROUP_ROWS)
    input_projection(nc, i["x_t"], i["norm_mix"], i["w_in"], i["coefs_in"], i["hist"], cols, o["conv_s"], o["conv_p"], o["shift_s"], o["shift_p"])
    ssd_heads(nc, cols, i["dt_par"], i["ssd_par"], i["state_ssd"], i["eye"], i["causal"], i["last_row"], i["keep"],
              i["block_row"], i["head_row"], y, o["ssd_s"], o["ssd_p"])
    rwkv_heads(nc, cols, i["pair_par"], i["state_wkv"], i["eye"], i["causal"], i["before"], i["level"], i["level0_t"], i["keep"],
               i["block_row"], i["head_pair"], y, o["wkv_s"], o["wkv_p"])
    with Stage(nc, "stream") as st:
        h = st.sb("h", [P, KD, KEPT])
        with Stage(nc, "picking") as kept:
            u = kept.sb("u", [P, KD, KEPT])
            picks = kept.sb("picks", [P, 3, RT, P])
            output_projection(nc, h, u, i["x_kept"], y, i["w_out"], i["norm_ffn"])
            pick_experts(nc, u, u_d, picks, i["w_query"], i["keys"], i["iota"])
            spread_gates(nc, picks, gates, i["eye"], i["iota"])
        run_experts(nc, h, u_d, gates.rearrange("g p (j t) -> g p j t", j=N_KEYS), i["up"], i["down"], i["norm_final"], o["y"])


OUTS = {
    "y": (KD, P, KEPT),
    "conv_s": (CONV_TILES, P, SEQS, HIST), "conv_p": (CONV_TILES, P, HIST),
    "shift_s": (SHIFT_TILES, P, SEQS, HIST), "shift_p": (SHIFT_TILES, P, HIST),
    "ssd_s": (SEQS, STATE, SSD_W), "ssd_p": (STATE, SSD_W),
    "wkv_s": (PAIRS, P, SEQS, HD), "wkv_p": (PAIRS, P, HD),
}


def by_channel(g):
    return g.reshape(-1, P).T


def lay_out(inputs):
    a = {name: np.asarray(value) for name, value in inputs.items()}
    samples, prompt = a["x_sample"].reshape(NS, D), a["x_prompt"].reshape(PROMPT, D)
    padding = np.zeros((P - NS - META, D), prompt.dtype)
    rows = np.concatenate([samples, padding, a["meta_tokens"], prompt])
    dt_par, ssd_par = pack_ssd_par(a)
    w_in, coefs_in = pack_w_in(a)
    arrays = {
        "x_t": rows.T.reshape(KD, P, T), "x_kept": np.concatenate([samples, prompt]).T.reshape(KD, P, KEPT),
        "norm_mix": by_channel(a["norm_mix"][0]), "norm_ffn": by_channel(a["norm_ffn"][0]), "norm_final": by_channel(a["norm_final"]),
        "w_in": w_in, "coefs_in": coefs_in, "hist": pack_hist(a), "dt_par": dt_par, "ssd_par": ssd_par, "state_ssd": pack_ssd_state(a),
        "pair_par": pack_pair_par(a), "state_wkv": pack_wkv(a), "w_out": tile_weights(a["w_out"][0]),
        "w_query": tile_weights(a["w_query"][0]), "keys": pack_keys(a), "up": pack_up(a), "down": pack_down(a),
        **constants(),
    }
    return {name: np.ascontiguousarray(value) for name, value in arrays.items()}


def kernel(**inputs):
    import concourse.bacc as bacc
    from concourse.bass_utils import run_bass_kernel_spmd

    nc = bacc.Bacc("TRN2", target_bir_lowering=False, num_devices=1)
    arrays = lay_out(inputs)
    ins = {name: nc.dram_tensor("in_" + name, value.shape, mybir.dt.from_np(value.dtype), kind="ExternalInput").ap()
           for name, value in arrays.items()}
    outs = {name: nc.dram_tensor("out_" + name, shape, F32, kind="ExternalOutput").ap() for name, shape in OUTS.items()}
    decoder_step(nc, ins, outs)
    ran = run_bass_kernel_spmd(nc, [{"in_" + name: value for name, value in arrays.items()}], core_ids=[0])
    r = {name: np.asarray(ran.results[0]["out_" + name]) for name in OUTS}

    y = r["y"].reshape(D, KEPT).T
    conv_dim, rwkv_in = CONV_TILES * P, SHIFT_TILES * P
    return (
        y[NS:].reshape(1, PROMPT, D), y[:NS].reshape(SEQS, STEPS, D),
        r["conv_p"].reshape(conv_dim, HIST).T[None, None],
        r["ssd_p"].T.reshape(1, 1, HEADS, HD, STATE),
        r["shift_p"][:, :, HIST - 1].reshape(1, 1, rwkv_in),
        r["wkv_p"].reshape(HEADS, HD, HD).transpose(0, 2, 1)[None, None],
        r["conv_s"].reshape(conv_dim, SEQS, HIST).transpose(1, 2, 0)[None],
        r["ssd_s"].transpose(0, 2, 1).reshape(1, SEQS, HEADS, HD, STATE),
        r["shift_s"][:, :, :, HIST - 1].reshape(rwkv_in, SEQS).T[None],
        r["wkv_s"].reshape(HEADS, HD, SEQS, HD).transpose(2, 0, 3, 1)[None],
    )
```
